# Optimizing a Trainium2 kernel written in Bass

```python
import math
import jax, jax.numpy as jnp
from jax import lax
import numpy as np

D_MODEL = 1024
BATCH = 1
SEQ = 512
DEPTH = 2
DEC_BATCH = 8
DEC_SEQ = 8
PAST_LEN = 2048
PAGE_SIZE = 128

N_HEADS = 16
KV_HEADS = 4
GROUP = N_HEADS // KV_HEADS
HEAD_DIM = 64
Q_DIM = N_HEADS * HEAD_DIM
KV_DIM = KV_HEADS * HEAD_DIM
QKV_DIM = Q_DIM + 2 * KV_DIM
WINDOW = 128
BLOCK = 128
ROPE_THETA = 10000.0
SSM_GROUP_CH = 16
SSM_GROUPS = D_MODEL // SSM_GROUP_CH
SSM_STATE = 64
N_EXPERT_GROUPS = 4
EXPERTS_PER_GROUP = 8
N_EXPERTS = N_EXPERT_GROUPS * EXPERTS_PER_GROUP
TOP_K = 2
EXPERT_FF = 128
N_ATTN_LAYERS = (DEPTH + 1) // 2
N_SSM_LAYERS = DEPTH // 2
NORM_EPS = 1e-5
F32 = jnp.float32

kernel_name = 'hybrid_swa_sink_s5_hmoe_step'

def rmsnorm(x, g):
    xf = x.astype(F32)
    y = xf * lax.rsqrt(jnp.mean(xf * xf, axis=-1, keepdims=True) + NORM_EPS)
    return (y * g.astype(F32)).astype(x.dtype)

def rotary(x, pos):
    half = HEAD_DIM // 2
    inv = 1.0 / (ROPE_THETA ** (jnp.arange(half, dtype=F32) * (2.0 / HEAD_DIM)))
    ang = pos.astype(F32)[:, None] * inv[None, :]
    cos = jnp.cos(ang)[:, None, :]
    sin = jnp.sin(ang)[:, None, :]
    xf = x.astype(F32)
    x1, x2 = xf[..., :half], xf[..., half:]
    return jnp.concatenate([x1 * cos - x2 * sin, x2 * cos + x1 * sin], axis=-1).astype(x.dtype)

def qkv_proj(xn, w_qkv, b_qkv, pos):
    lead = xn.shape[:-1]
    qkv = xn @ w_qkv + b_qkv
    q = qkv[..., :Q_DIM].reshape(*lead, N_HEADS, HEAD_DIM)
    k = qkv[..., Q_DIM:Q_DIM + KV_DIM].reshape(*lead, KV_HEADS, HEAD_DIM)
    v = qkv[..., Q_DIM + KV_DIM:].reshape(*lead, KV_HEADS, HEAD_DIM)
    return rotary(q, pos), rotary(k, pos), v

def attend(q, k, v, mask, sinks):
    s = jnp.einsum('...qhgd,...khd->...hgqk', q, k).astype(F32) * (HEAD_DIM ** -0.5)
    s = jnp.where(mask, s, -jnp.inf)
    sink = sinks.astype(F32).reshape(KV_HEADS, GROUP, 1, 1)
    m = jnp.maximum(jnp.max(s, axis=-1, keepdims=True), sink)
    p = jnp.exp(s - m)
    denom = jnp.sum(p, axis=-1, keepdims=True) + jnp.exp(sink - m)
    w = (p / denom).astype(v.dtype)
    return jnp.einsum('...hgqk,...khd->...qhgd', w, v)

def swa_prompt(xn, w_qkv, b_qkv, w_o, b_o, sinks):
    bsz, seq, _ = xn.shape
    nb = seq // BLOCK
    q, k, v = qkv_proj(xn, w_qkv, b_qkv, jnp.arange(seq, dtype=jnp.int32))
    qb = q.reshape(bsz, nb, BLOCK, KV_HEADS, GROUP, HEAD_DIM)
    kb = k.reshape(bsz, nb, BLOCK, KV_HEADS, HEAD_DIM)
    vb = v.reshape(bsz, nb, BLOCK, KV_HEADS, HEAD_DIM)

    def with_prev(t):
        prev = jnp.concatenate([jnp.zeros_like(t[:, :1]), t[:, :-1]], axis=1)
        return jnp.concatenate([prev, t], axis=2)

    blk = jnp.arange(nb, dtype=jnp.int32)[:, None, None] * BLOCK
    qpos = blk + jnp.arange(BLOCK, dtype=jnp.int32)[None, :, None]
    kpos = blk - BLOCK + jnp.arange(2 * BLOCK, dtype=jnp.int32)[None, None, :]
    mask = (kpos >= 0) & (kpos <= qpos) & (qpos - kpos <= WINDOW)
    o = attend(qb, with_prev(kb), with_prev(vb), mask[:, None, None], sinks)
    y = o.reshape(bsz, seq, Q_DIM) @ w_o + b_o
    return y, k[:, seq - WINDOW:], v[:, seq - WINDOW:]

def swa_sample(xn, ck, cv, w_qkv, b_qkv, w_o, b_o, sinks):
    bsz, n_new, _ = xn.shape
    rows = ck.shape[1]
    qpos = PAST_LEN + jnp.arange(n_new, dtype=jnp.int32)
    q, k, v = qkv_proj(xn, w_qkv, b_qkv, qpos)
    kk = jnp.concatenate([ck.astype(k.dtype), k], axis=1)
    vv = jnp.concatenate([cv.astype(v.dtype), v], axis=1)
    kpos = jnp.concatenate([PAST_LEN - rows + jnp.arange(rows, dtype=jnp.int32), qpos])
    mask = (kpos[None, :] <= qpos[:, None]) & (qpos[:, None] - kpos[None, :] <= WINDOW)
    o = attend(q.reshape(bsz, n_new, KV_HEADS, GROUP, HEAD_DIM), kk, vv, mask, sinks)
    y = o.reshape(bsz, n_new, Q_DIM) @ w_o + b_o
    return y, kk[:, -rows:], vv[:, -rows:]

def complex_affine_combine(e1, e2):
    a1r, a1i, b1r, b1i = e1
    a2r, a2i, b2r, b2i = e2
    ar = a1r * a2r - a1i * a2i
    ai = a1r * a2i + a1i * a2r
    br = a2r * b1r - a2i * b1i + b2r
    bi = a2r * b1i + a2i * b1r + b2i
    return (ar, ai, br, bi)

def s5_mix(xn, h0_re, h0_im, a_re, a_im, log_dt, b_re, b_im, c_re, c_im, d, w_a, w_b):
    bt, seq, _ = xn.shape
    u = xn.astype(F32)
    ug = u.reshape(bt, seq, SSM_GROUPS, SSM_GROUP_CH)
    delta = jnp.exp(log_dt.astype(F32))[:, None]
    lr, li = a_re.astype(F32), a_im.astype(F32)
    mag = jnp.exp(delta * lr)
    abar_r = mag * jnp.cos(delta * li)
    abar_i = mag * jnp.sin(delta * li)
    nr, ni = abar_r - 1.0, abar_i
    den = lr * lr + li * li
    coef_r = ((nr * lr + ni * li) / den)[..., None]
    coef_i = ((ni * lr - nr * li) / den)[..., None]
    br, bi = b_re.astype(F32), b_im.astype(F32)
    bbar_r = coef_r * br - coef_i * bi
    bbar_i = coef_r * bi + coef_i * br
    bu_r = jnp.einsum('blgc,gpc->lbgp', ug, bbar_r)
    bu_i = jnp.einsum('blgc,gpc->lbgp', ug, bbar_i)
    a_r = jnp.broadcast_to(abar_r, (seq, 1, SSM_GROUPS, SSM_STATE))
    a_i = jnp.broadcast_to(abar_i, (seq, 1, SSM_GROUPS, SSM_STATE))
    cum_r, cum_i, h_r, h_i = lax.associative_scan(complex_affine_combine, (a_r, a_i, bu_r, bu_i), axis=0)
    g0r, g0i = h0_re.astype(F32), h0_im.astype(F32)
    h_r = h_r + cum_r * g0r - cum_i * g0i
    h_i = h_i + cum_r * g0i + cum_i * g0r
    y = (jnp.einsum('lbgp,gcp->blgc', h_r, c_re.astype(F32))
         - jnp.einsum('lbgp,gcp->blgc', h_i, c_im.astype(F32)))
    y = y.reshape(bt, seq, D_MODEL) + d.astype(F32) * u
    z = jax.nn.gelu(y)
    out = (z @ w_a.astype(F32)) * jax.nn.sigmoid(z @ w_b.astype(F32))
    return out.astype(xn.dtype), h_r[-1], h_i[-1]

def hier_moe(xn, w_rg, b_rg, w_re, b_re, w_gate, w_up, w_down):
    lead = xn.shape[:-1]
    t = xn.reshape(-1, D_MODEL)
    g_prob = jax.nn.softmax((t @ w_rg).astype(F32) + b_rg.astype(F32), axis=-1)
    g_val, g_idx = lax.top_k(g_prob, 1)
    e_logit = ((t @ w_re).astype(F32) + b_re.astype(F32)).reshape(-1, N_EXPERT_GROUPS, EXPERTS_PER_GROUP)
    sel = jnp.take_along_axis(e_logit, g_idx[:, :, None], axis=1)[:, 0]
    e_val, e_idx = lax.top_k(sel, TOP_K)
    e_w = jax.nn.softmax(e_val, axis=-1)
    within = jnp.sum(jax.nn.one_hot(e_idx, EXPERTS_PER_GROUP, dtype=F32) * e_w[..., None], axis=1)
    combine = (jax.nn.one_hot(g_idx[:, 0], N_EXPERT_GROUPS, dtype=F32)[:, :, None]
               * (g_val * within)[:, None, :]).reshape(-1, N_EXPERTS)
    g = jnp.einsum('td,edf->tef', t, w_gate)
    u = jnp.einsum('td,edf->tef', t, w_up)
    hid = jax.nn.silu(g) * u * combine[..., None].astype(g.dtype)
    out = jnp.einsum('tef,efd->td', hid, w_down)
    return out.reshape(*lead, D_MODEL).astype(xn.dtype)

def setup_inputs(seed: int = 0) -> dict:
    key = jax.random.key(seed)
    ks = iter(jax.random.split(key, 40))

    def nrm(shape, scale):
        return jax.random.normal(next(ks), shape, F32) * scale

    rows = min(WINDOW, PAST_LEN)
    na, ns = N_ATTN_LAYERS, N_SSM_LAYERS
    n_idx = jnp.arange(SSM_STATE, dtype=F32)
    return {
        'x_prompt': nrm((BATCH, SEQ, D_MODEL), 1.0),
        'x_sample': nrm((DEC_BATCH, DEC_SEQ, D_MODEL), 1.0),
        'cache_k': nrm((na, DEC_BATCH, rows, KV_HEADS, HEAD_DIM), 1.0),
        'cache_v': nrm((na, DEC_BATCH, rows, KV_HEADS, HEAD_DIM), 1.0),
        'state_ssm_re': nrm((ns, DEC_BATCH, SSM_GROUPS, SSM_STATE), 0.5),
        'state_ssm_im': nrm((ns, DEC_BATCH, SSM_GROUPS, SSM_STATE), 0.5),
        'norm_mix': 1.0 + nrm((DEPTH, D_MODEL), 0.05),
        'norm_ffn': 1.0 + nrm((DEPTH, D_MODEL), 0.05),
        'norm_final': 1.0 + nrm((D_MODEL,), 0.05),
        'attn_w_qkv': nrm((na, D_MODEL, QKV_DIM), D_MODEL ** -0.5),
        'attn_b_qkv': nrm((na, QKV_DIM), 0.01),
        'attn_w_o': nrm((na, Q_DIM, D_MODEL), Q_DIM ** -0.5),
        'attn_b_o': nrm((na, D_MODEL), 0.01),
        'attn_sinks': nrm((na, N_HEADS), 0.5),
        'ssm_a_re': -0.5 + nrm((ns, SSM_GROUPS, SSM_STATE), 0.01),
        'ssm_a_im': math.pi * n_idx + nrm((ns, SSM_GROUPS, SSM_STATE), 0.01),
        'ssm_log_dt': jax.random.uniform(next(ks), (ns, SSM_GROUPS), F32, math.log(1e-3), math.log(1e-1)),
        'ssm_b_re': nrm((ns, SSM_GROUPS, SSM_STATE, SSM_GROUP_CH), (2 * SSM_GROUP_CH) ** -0.5),
        'ssm_b_im': nrm((ns, SSM_GROUPS, SSM_STATE, SSM_GROUP_CH), (2 * SSM_GROUP_CH) ** -0.5),
        'ssm_c_re': nrm((ns, SSM_GROUPS, SSM_GROUP_CH, SSM_STATE), SSM_STATE ** -0.5),
        'ssm_c_im': nrm((ns, SSM_GROUPS, SSM_GROUP_CH, SSM_STATE), SSM_STATE ** -0.5),
        'ssm_d': nrm((ns, D_MODEL), 0.5),
        'ssm_w_glu_a': nrm((ns, D_MODEL, D_MODEL), D_MODEL ** -0.5),
        'ssm_w_glu_b': nrm((ns, D_MODEL, D_MODEL), D_MODEL ** -0.5),
        'moe_w_router_group': nrm((DEPTH, D_MODEL, N_EXPERT_GROUPS), D_MODEL ** -0.5),
        'moe_b_router_group': nrm((DEPTH, N_EXPERT_GROUPS), 0.01),
        'moe_w_router_expert': nrm((DEPTH, D_MODEL, N_EXPERTS), D_MODEL ** -0.5),
        'moe_b_router_expert': nrm((DEPTH, N_EXPERTS), 0.01),
        'moe_w_gate': nrm((DEPTH, N_EXPERTS, D_MODEL, EXPERT_FF), D_MODEL ** -0.5),
        'moe_w_up': nrm((DEPTH, N_EXPERTS, D_MODEL, EXPERT_FF), D_MODEL ** -0.5),
        'moe_w_down': nrm((DEPTH, N_EXPERTS, EXPERT_FF, D_MODEL), EXPERT_FF ** -0.5),
    }

def reference(x_prompt, x_sample, cache_k, cache_v, state_ssm_re, state_ssm_im,
              norm_mix, norm_ffn, norm_final,
              attn_w_qkv, attn_b_qkv, attn_w_o, attn_b_o, attn_sinks,
              ssm_a_re, ssm_a_im, ssm_log_dt, ssm_b_re, ssm_b_im, ssm_c_re, ssm_c_im,
              ssm_d, ssm_w_glu_a, ssm_w_glu_b,
              moe_w_router_group, moe_b_router_group, moe_w_router_expert, moe_b_router_expert,
              moe_w_gate, moe_w_up, moe_w_down):
    xp, xs = x_prompt, x_sample
    k_p, k_s, v_p, v_s = [], [], [], []
    hr_p, hr_s, hi_p, hi_s = [], [], [], []
    for layer in range(DEPTH):
        np_ = rmsnorm(xp, norm_mix[layer])
        ns_ = rmsnorm(xs, norm_mix[layer])
        if layer % 2 == 0:
            a = layer // 2
            attn = (attn_w_qkv[a], attn_b_qkv[a], attn_w_o[a], attn_b_o[a], attn_sinks[a])
            mp, kp_new, vp_new = swa_prompt(np_, *attn)
            ms, ks_new, vs_new = swa_sample(ns_, cache_k[a], cache_v[a], *attn)
            k_p.append(kp_new)
            v_p.append(vp_new)
            k_s.append(ks_new)
            v_s.append(vs_new)
        else:
            s = layer // 2
            ssm = (ssm_a_re[s], ssm_a_im[s], ssm_log_dt[s], ssm_b_re[s], ssm_b_im[s],
                   ssm_c_re[s], ssm_c_im[s], ssm_d[s], ssm_w_glu_a[s], ssm_w_glu_b[s])
            h0 = jnp.zeros((xp.shape[0], SSM_GROUPS, SSM_STATE), F32)
            mp, rp_new, ip_new = s5_mix(np_, h0, h0, *ssm)
            ms, rs_new, is_new = s5_mix(ns_, state_ssm_re[s], state_ssm_im[s], *ssm)
            hr_p.append(rp_new)
            hi_p.append(ip_new)
            hr_s.append(rs_new)
            hi_s.append(is_new)
        xp = xp + mp
        xs = xs + ms
        moe_w = (moe_w_router_group[layer], moe_b_router_group[layer], moe_w_router_expert[layer],
                 moe_b_router_expert[layer], moe_w_gate[layer], moe_w_up[layer], moe_w_down[layer])
        xp = xp + hier_moe(rmsnorm(xp, norm_ffn[layer]), *moe_w)
        xs = xs + hier_moe(rmsnorm(xs, norm_ffn[layer]), *moe_w)
    y_prompt = rmsnorm(xp, norm_final)
    y_sample = rmsnorm(xs, norm_final)
    return (y_prompt, y_sample,
            jnp.stack(k_p), jnp.stack(k_s), jnp.stack(v_p), jnp.stack(v_s),
            jnp.stack(hr_p), jnp.stack(hr_s), jnp.stack(hi_p), jnp.stack(hi_s))


_drawn_inputs = setup_inputs


def setup_inputs(seed=0):
    import zlib

    import numpy as np

    out = dict(_drawn_inputs(seed))
    spreads = {}
    factors = {}
    for name, (base, spread) in spreads.items():
        noise = np.random.default_rng([zlib.crc32(name.encode()), seed]).standard_normal(out[name].shape)
        drawn = base * np.exp(spread * noise) if base else spread * noise
        out[name] = __import__('jax').numpy.asarray(drawn.astype(out[name].dtype))
    for name, factor in factors.items():
        out[name] = (out[name] * factor).astype(out[name].dtype)
    return out
```

```python
import math
from contextlib import ExitStack

import numpy as np

import concourse.bass as bass
from concourse import mybir

FP = mybir.dt.float32
I32 = mybir.dt.int32
U32 = mybir.dt.uint32
ALU = mybir.AluOpType
ACT = mybir.ActivationFunctionType
AX = mybir.AxisListType

P = 128
D = 1024
SEQ = 512
NSEQ, DSEQ = 8, 8
NTOK = SEQ + NSEQ * DSEQ
NT = 5
ROWS = [P, P, P, P, NSEQ * DSEQ]
PAST = 2048
NH, KVH, HD = 16, 4, 64
GRP = NH // KVH
QD, KVD = NH * HD, KVH * HD
QKV = QD + 2 * KVD
NBLK = SEQ // P
SCALE = HD ** -0.5
BIG = 1.0e30
EPS = 1e-5
KC = D // P
NG, EPG = 4, 8
NE = NG * EPG
FF = 128
CAP = 64
PAIRS = NE // 2
ROUNDS = PAIRS // 2
OVT = (2 * NTOK - 1) // CAP
OVP = (OVT + 1) // 2
NPAIR = PAIRS + OVP
SLOTS = NPAIR * P
NGR, CH, ST = 64, 16, 64
GP = NGR // 2
L = 8
NCH = NTOK // L
PCH = SEQ // L
BP = 4
NB = GP // BP
RS = 4
RW = 3072


def bc(ap, shape):
    return ap.to_broadcast(shape)


def build(nc, x_prompt, x_sample, cache_k, cache_v, st_re, st_im, norm_mix, norm_ffn, norm_final,
          w_qkv, b_qkv, w_o, b_o, sinks, a_re, a_im, log_dt, b_re, b_im, c_re, c_im, ssm_d,
          w_ga, w_gb, w_rg, b_rg, w_re, b_re_r, w_gate, w_up, w_down, cs_tab,
          y_p, y_s, nk_p, nk_s, nv_p, nv_s, hr_p, hr_s, hi_p, hi_s):
    ctx = ExitStack()
    with ctx:
        def sem(name):
            return ctx.enter_context(nc.semaphore(name))

        def sb(name, shape, dt=FP):
            return ctx.enter_context(nc.sbuf_tensor(name, shape, dt))

        X = sb("X", [P, NT, D])
        XN = sb("XN", [P, NT, D])
        XT = sb("XT", [P, KC, NTOK])
        RING = sb("RING", [P, RS, RW])
        IDENT = sb("IDENT", [P, P])
        UPPER = sb("UPPER", [P, P])
        ONES = sb("ONES", [P, P])
        GAM = sb("GAM", [P, D])
        SS = sb("SS", [P, 5, NT])
        RSTD = sb("RSTD", [P, 5, NT])
        IOTA = sb("IOTA", [P, P])
        TOKID = sb("TOKID", [P, NT])
        PIDX = sb("PIDX", [P, 1], I32)
        PMOD = sb("PMOD", [P, 2])
        PMI = sb("PMI", [P, 2], I32)
        EPSC = sb("EPSC", [P, 1])
        OVR = sb("OVR", [P, 2, 1 + 2 * OVP], I32)
        IOI = sb("IOI", [P, P], I32)
        PH_F = 24200
        PH = sb("PH", [P, PH_F])

        class Area:

            def __init__(self, base=0):
                self.at = base

            def take(self, n, parts=P):
                v = PH[0:parts, self.at:self.at + n]
                self.at += n
                assert self.at <= PH_F, self.at
                return v

        PSUM = ctx.enter_context(nc.psum_tensor("PSUM", [P, 8, 512], FP))

        def bank(i, n=1):
            return PSUM[:, i:i + n, :]

        xn_d = [nc.dram_tensor("xn_scratch", (NTOK, D), FP).ap()] * 2
        y_d = [nc.dram_tensor("y_scratch", (SLOTS, D), FP).ap()] * 2
        ZER = PH[:, PH_F - D:PH_F]

        a = Area()
        QT = a.take(KC * SEQ).rearrange("p (c t) -> p c t", c=KC)
        QTS = a.take(NH * 64, 64).rearrange("p (s n) -> p s n", s=NSEQ)
        OT = PH[:, 0:KC * NTOK].rearrange("p (c t) -> p c t", c=KC)
        KT = a.take(KVH * SEQ).rearrange("p (h t) -> p h t", h=KVH)
        KTS = a.take(KVH * 64, 64).rearrange("p (h t) -> p h t", h=KVH)
        V = a.take(NT * KVD).rearrange("p (t n) -> p t n", t=NT)
        VC = a.take(NSEQ * KVD).rearrange("p (s n) -> p s n", s=NSEQ)
        BQKV = a.take(QKV)
        MPCUR = a.take(2 * P)
        MPREV, MCUR = MPCUR[:, 0:P], MPCUR[:, P:2 * P]
        MSC = a.take(P)
        MSN = a.take(120)
        SINK = a.take(NH)
        SINKS = a.take(1)
        SM = a.take(64)
        CS = a.take(NT * 64).rearrange("p (t n) -> p t n", t=NT)
        BO = a.take(D)
        at0 = a.at
        QR = a.take(QD + KVD)
        TA = a.take(QD + KVD)
        TB = a.take(QD + KVD)
        QO = a.take(2 * QD).rearrange("p (b n) -> p b n", b=2)
        KD = a.take(2 * 512).rearrange("p (b n) -> p b n", b=2)
        a.at = at0
        CK = a.take(NSEQ * KVD).rearrange("p (s n) -> p s n", s=NSEQ)
        SB_ = a.take(2 * 1024).rearrange("p (b n) -> p b n", b=2)
        PT = a.take(2 * 1024).rearrange("p (b n) -> p b n", b=2)
        OD = CK[:, 0:4, 0:P]
        KCT = XT[0:64, :, :].rearrange("p c t -> p (c t)")[:, 0:NSEQ * KVH * P].rearrange(
            "p (s h k) -> p s h k", s=NSEQ, h=KVH)
        O = XN

        a = Area()
        WR = a.take(KC * 36).rearrange("p (c n) -> p c n", c=KC)
        BR = a.take(36)
        LG = a.take(NT * 36).rearrange("p (t n) -> p t n", t=NT)
        GL8 = a.take(NT * 8).rearrange("p (t n) -> p t n", t=NT)
        GM8 = a.take(NT * 8).rearrange("p (t n) -> p t n", t=NT)
        GI8 = a.take(NT * 8).bitcast(U32).rearrange("p (t n) -> p t n", t=NT)
        GIF = a.take(NT)
        GOH = a.take(NT * 4).rearrange("p (t n) -> p t n", t=NT)
        GE = a.take(NT * 4).rearrange("p (t n) -> p t n", t=NT)
        GV = a.take(NT)
        EM = a.take(NT * 32).rearrange("p (t n) -> p t n", t=NT)
        EV8 = a.take(NT * 8).rearrange("p (t n) -> p t n", t=NT)
        EI8 = a.take(NT * 8).bitcast(U32).rearrange("p (t n) -> p t n", t=NT)
        EIF = a.take(NT * 2).rearrange("p (t n) -> p t n", t=NT)
        EX = a.take(NT)
        CW = a.take(NT * 2).rearrange("p (t n) -> p t n", t=NT)
        EOH = a.take(NT * 2 * 32).rearrange("p (t k n) -> p t k n", t=NT, k=2)
        ET = a.take(NT * 2 * 32).rearrange("p (t k n) -> p t k n", t=NT, k=2)
        MM = a.take(NT * 32).rearrange("p (t n) -> p t n", t=NT)
        RK = a.take(6 * 32).rearrange("p (t n) -> p t n", t=6)
        OVN = a.take(32)
        OVI = a.take(32)
        OVE = a.take(32)
        OVM = a.take(32)
        RR = a.take(NT * 2).rearrange("p (t n) -> p t n", t=NT)
        OB = a.take(NT * 2).rearrange("p (t n) -> p t n", t=NT)
        SL = a.take(NT * 2).rearrange("p (t n) -> p t n", t=NT)
        SLI = a.take(NT * 2).bitcast(I32).rearrange("p (t n) -> p t n", t=NT)
        SMOD = a.take(NT * 2).rearrange("p (t n) -> p t n", t=NT)
        SDIV = a.take(NT * 2).rearrange("p (t n) -> p t n", t=NT)
        SMI = a.take(NT * 2).bitcast(I32).rearrange("p (t n) -> p t n", t=NT)
        SDI = a.take(NT * 2).bitcast(I32).rearrange("p (t n) -> p t n", t=NT)
        OVNI = a.take(32).bitcast(I32)
        R1 = a.take(NT * 2 * P).rearrange("p (t k n) -> p t k n", t=NT, k=2)
        P1 = a.take(NT * 2 * NPAIR).rearrange("p (t k n) -> p t k n", t=NT, k=2)
        IDX = a.take(NPAIR).bitcast(I32)
        IDXB = a.take(2).bitcast(I32)
        EIDT = a.take(2 * OVP * 32).rearrange("p (j n) -> p j n", n=32)
        EIDF = a.take(2 * OVP)
        NPF = a.take(2)
        XG = a.take(2 * D).rearrange("p (b n) -> p b n", b=2)
        XGT = a.take(2 * D).rearrange("p (b c t) -> p b c t", b=2, c=KC)
        SG = a.take(2 * FF).rearrange("p (b f) -> p b f", b=2)
        HTM = a.take(2 * FF).rearrange("p (b f) -> p b f", b=2)
        HID = a.take(2 * P).rearrange("p (b m t) -> p b m t", b=2, m=2)
        YB = a.take(2 * D).rearrange("p (b n) -> p b n", b=2)
        YG = a.take(4 * D).rearrange("p (b n) -> p b n", b=4)

        a = Area()
        AL = a.take(L * D, NCH).rearrange("p (s d) -> p s d", s=L)
        Z = AL
        H = a.take(2 * GP * (NCH + 1)).rearrange("p (r g c) -> p r g c", r=2, g=GP)
        U = XN.rearrange("p t d -> p (t d)")[:, 0:NGR * NCH].rearrange("p (g c) -> p g c", g=NGR)
        G = XT.rearrange("p c t -> p (c t)")[:, 0:2 * GP * NCH].rearrange("p (r g c) -> p r g c", r=2, g=GP)
        BB = a.take(2 * GP * CH).rearrange("p (r g c) -> p r g c", r=2, g=GP)
        CT = a.take(2 * GP * CH).rearrange("p (r g c) -> p r g c", r=2, g=GP)
        PW = a.take(2 * 9 * GP).rearrange("p (r k g) -> p r k g", r=2, k=9)
        PWR = a.take(2 * 8 * GP).rearrange("p (r k g) -> p r k g", r=2, k=8)
        CC = a.take(4 * GP).rearrange("p (a x g) -> p a x g", a=2, x=2)
        CF = a.take(2 * GP).rearrange("p (r g) -> p r g", r=2)
        HO = a.take(2 * GP * NSEQ).rearrange("p (r g s) -> p r g s", r=2, g=GP)
        HF = a.take(2 * GP).rearrange("p (r g) -> p r g", r=2)
        PR = a.take(4 * GP).rearrange("p (a x g) -> p a x g", a=2, x=2)
        QQ = a.take(2 * GP).rearrange("p (r g) -> p r g", r=2)
        DCOL = a.take(2 * GP, CH).rearrange("p (w g) -> p w g", w=2)
        EYE = a.take(CH, CH)
        DD2 = a.take(2 * GP * CH, 32 + CH).rearrange("p (w g c) -> p w g c", w=2, g=GP)
        DD = [DD2[32 * b:32 * b + CH] for b in range(2)]
        at1 = a.at
        WSB = a.take(2 * BP * P).rearrange("p (r g n) -> p r g n", r=2, g=BP)
        WT = a.take(2 * BP * P).rearrange("p (r g n) -> p r g n", r=2, g=BP)
        TMPW = a.take(BP * 144)
        TMPX = a.take(BP * 144)
        a.at = at1
        VV = a.take(3 * 2 * BP * 144).rearrange("p (b w g n) -> p b w g n", b=3, w=2, g=BP)
        TT = a.take(2 * 2 * BP * P).rearrange("p (b w g n) -> p b w g n", b=2, w=2, g=BP)
        A1S = a.take(2 * 9 * GP).rearrange("p (w k g) -> p w k g", w=2, k=9)
        A2S = PW
        B1S = GAM[:, 0:2 * GP * CH].rearrange("p (w g c) -> p w g c", w=2, g=GP)
        B2S = CT
        BSWAP = XN.rearrange("p t d -> p (t d)")[64:P, NGR * NCH:NGR * NCH + GP * CH].rearrange(
            "p (g c) -> p g c", g=GP)
        XTF = XT.rearrange("p c t -> p (c t)")
        KP = [XTF[32 * b:32 * b + CH, 0:2 * BP * 240].rearrange("p (w g n) -> p w g n", w=2, g=BP) for b in range(2)]
        HSWAP = XTF[64:P, 0:GP * NCH].rearrange("p (g c) -> p g c", g=GP)
        TMPV = XTF[:, GP * NCH:GP * NCH + 2 * BP * 144]
        a.at = at1 + 2 * 2 * BP * P + 2 * BP * 144
        UA = a.take(2 * 8 * L * CH, NCH).rearrange("p (b g s c) -> p b g s c", b=2, g=8, s=L)
        a.at = at1
        NAT = a.take(24 * P, 32).rearrange("p (k n) -> p k n", k=24)
        DT2 = a.take(2, 32)
        a.at = at1
        CL = Area(0).take(16 * P).rearrange("p (k n) -> p k n", k=16)
        SIN_ = Area(16 * P).take(2 * NSEQ * P, 32).rearrange("p (r s n) -> p r s n", r=2, s=NSEQ)
        SOUT = WSB.rearrange("p r g n -> p (r g n)")[0:32, :]
        GL_SG = PH[:, 0:2 * 512].rearrange("p (b n) -> p b n", b=2)
        GL_T = PH[:, 1024:1024 + 512]

        s = {}

        def S(name):
            if name not in s:
                s[name] = sem(name)
            return s[name]

        phase = S("phase_done")
        NENG = 4

        def end_phase(eng, n):
            eng.drain().then_inc(phase, 1)
            eng.wait_ge(phase, NENG * n)

        class Chain:

            def __init__(self, eng, name):
                self.eng, self.sem, self.n = eng, S(name), 0

            def __call__(self, ins):
                self.n += 1
                ins.then_inc(self.sem, 1)
                self.eng.wait_ge(self.sem, self.n)

        LOADS = [1] * 4 + [1] * 3 + [3] * NE + [2] * 6 + [3] * NE
        Q_QKV, Q_WO, Q_M0, Q_GLU, Q_M1 = 0, 4, 7, 7 + NE, 13 + NE

        def full(q):
            return 16 * sum(LOADS[j] for j in range(q % RS, q + 1, RS))

        Q_M = [Q_M0, Q_M1]

        def toeplitz(eng, k, half):
            eng.wait_ge(S("taps_ready"), k + 1)
            if k >= 2:
                eng.wait_ge(S("y_ssm"), k - 1)
            for sh in range(half * L // 2, (half + 1) * L // 2):
                eng.dma_start(TT[CH * sh:CH * sh + CH, k % 2].rearrange("p w g n -> p (w g) n"),
                              KP[k % 2][:, :, :, 112 - CH * sh:240 - CH * sh].rearrange("p w g n -> p (w g) n")
                              ).then_inc(S(f"toeplitz{k % 2}"), 16)

        block = ctx.enter_context(nc.Block())

        @block.sync
        def _(sp):
            for t in range(4):
                sp.dma_start(X[:, t, :], x_prompt[0, t * P:(t + 1) * P, :]).then_inc(S(f"x_in{t}"), 16)
            sp.dma_start(X[0:64, 4, :], x_sample.rearrange("b t d -> (b t) d")).then_inc(S("x_in4"), 16)

            def ring_load(q, pieces):
                if q >= RS:
                    sp.wait_ge(S("ring_free"), q - RS + 1)
                assert len(pieces) == LOADS[q]
                for dst, src in pieces:
                    sp.dma_start(dst, src).then_inc(S(f"ring_full{q % RS}"), 16)

            for j in range(4):
                ring_load(Q_QKV + j, [(RING[:, j, :].rearrange("p (k n) -> p k n", k=2),
                                       w_qkv[0, 2 * j * P:(2 * j + 2) * P, :].rearrange("(k p) n -> p k n", p=P))])
            for j, k in enumerate([3, 3, 2]):
                q = Q_WO + j
                ring_load(q, [(RING[:, q % RS, 0:k * D].rearrange("p (k n) -> p k n", k=k),
                               w_o[0, 3 * j * P:(3 * j + k) * P, :].rearrange("(k p) n -> p k n", p=P))])

            def experts(layer):
                q0 = Q_M[layer]
                with sp.Fori(0, NE // RS) as it:
                    for j in range(RS):
                        slot = (q0 + j) % RS
                        sp.wait_ge(S("ring_free"), it * RS + (q0 + j - RS + 1))
                        for i, src in enumerate((w_gate, w_up)):
                            sp.dma_start(RING[:, slot, i * D:(i + 1) * D].rearrange("p (c f) -> p c f", c=KC),
                                         src[layer, bass.ds(it * RS + j, 1), :, :].rearrange("o (c p) f -> p (o c) f", p=P)
                                         ).then_inc(S(f"ring_full{slot}"), 16)
                        sp.dma_start(RING[:, slot, 2 * D:3 * D],
                                     w_down[layer, bass.ds(it * RS + j, 1), :, :].rearrange("o f d -> f (o d)")
                                     ).then_inc(S(f"ring_full{slot}"), 16)

            def overflow(layer):
                sp.wait_ge(S("routed"), layer + 1)
                sp.wait_ge(S(f"xn_stored{layer}"), 16 * NT)
                n = sp.value_load(OVR[0:1, layer, 0:1], min_val=0, max_val=OVP)
                before = sp.value_load(OVR[0:1, 0, 0:1], min_val=0, max_val=OVP) if layer else 0
                with sp.Fori(0, OVP) as j:
                    with sp.If(j < n):
                        sp.wait_ge(S("ov_wfree"), before + j + (layer + 1))
                        for m, area in enumerate((XN.rearrange("p t d -> p (t d)"), XT.rearrange("p c t -> p (c t)"))):
                            e = sp.value_load(OVR[0:1, layer, bass.ds(2 * j + m + 1, 1)], min_val=0, max_val=NE - 1)
                            for i, src in enumerate((w_gate, w_up)):
                                sp.dma_start(area[:, i * D:(i + 1) * D].rearrange("p (c f) -> p c f", c=KC),
                                             src[layer, bass.ds(e, 1), :, :].rearrange("o (c p) f -> p (o c) f", p=P)
                                             ).then_inc(S("ov_w"), 16)
                            sp.dma_start(area[:, 2 * D:3 * D],
                                         w_down[layer, bass.ds(e, 1), :, :].rearrange("o f d -> f (o d)")
                                         ).then_inc(S("ov_w"), 16)

            experts(0)
            overflow(0)
            for n in range(2):
                for j, k in enumerate([3, 3, 2]):
                    q = Q_GLU + 3 * n + j
                    if q == Q_GLU + RS:
                        for k_ in range(NB):
                            toeplitz(sp, k_, 0)
                    view = RING[:, q % RS, 0:k * D].rearrange("p (k w n) -> p k w n", k=k, w=2)
                    ring_load(q, [(view[:, :, w, :],
                                   src[0, 3 * j * P:(3 * j + k) * P, n * 512:(n + 1) * 512].rearrange(
                                       "(k p) n -> p k n", p=P)) for w, src in enumerate((w_ga, w_gb))])
            experts(1)
            overflow(1)
            for t in range(NT):
                sp.wait_ge(S("xn_done"), 4 * NT + t + 1)
                dst = y_p[0, t * P:(t + 1) * P, :] if t < 4 else y_s.rearrange("b t d -> (b t) d")
                sp.dma_start(dst, XN[0:ROWS[t], t, :]).then_inc(S("y_out"), 16)
            sp.wait_ge(S("y_out"), 16 * NT)

        @block.gpsimd
        def _(pool):
            ch = Chain(pool, "pool_chain")
            pool.memset(EPSC[:, :], EPS).then_inc(S("eps_ready"), 1)
            pool.memset(IDENT[:, :], 0.0)
            pool.memset(UPPER[:, :], 1.0)
            pool.memset(MPREV, 0.0)
            pool.memset(MCUR, 0.0)
            ch(pool.memset(ONES[:, :], 1.0))
            pool.affine_select(out=IDENT[:, :], in_=IDENT[:, :], compare_op=ALU.not_equal, fill=1.0, base=0,
                               pattern=[[-1, P]], channel_multiplier=1).then_inc(S("ident_ready"), 1)
            pool.affine_select(out=UPPER[:, :], in_=UPPER[:, :], compare_op=ALU.is_ge, fill=0.0, base=-1,
                               pattern=[[1, P]], channel_multiplier=-1)
            pool.affine_select(out=MPREV, in_=MPREV, compare_op=ALU.is_ge, fill=-BIG, base=0,
                               pattern=[[1, P]], channel_multiplier=-1)
            pool.affine_select(out=MCUR, in_=MCUR, compare_op=ALU.is_ge, fill=-BIG, base=0,
                               pattern=[[-1, P]], channel_multiplier=1)
            ch(pool.iota(IOI[:, :], pattern=[[1, P]], base=0, channel_multiplier=0))
            ch(pool.tensor_copy(IOTA[:, :], IOI[:, :]))
            ch(pool.iota(PIDX[:, :], pattern=[[0, 1]], base=0, channel_multiplier=1))
            ch(pool.iota(IOI[:, 0:NT], pattern=[[P, NT]], base=0, channel_multiplier=1))
            ch(pool.tensor_copy(TOKID[:, :], IOI[:, 0:NT]))
            ch(pool.memset(TOKID[64:P, 4:5], 0.0))
            pool.sem_inc(S("consts_ready"), 1)
            ch(pool.memset(ZER, 0.0))
            for i in range(OVP):
                pool.dma_start(y_d[0][(PAIRS + i) * P:(PAIRS + i + 1) * P, :], ZER).then_inc(S("zeros_out"), 16)
            pool.wait_ge(S("zeros_out"), 16 * OVP)
            end_phase(pool, 1)
            end_phase(pool, 2)
            end_phase(pool, 3)

            def moe(layer, ph):
                pool.wait_ge(S("routed"), layer + 1)
                pool.wait_ge(S(f"xn_stored{layer}"), 16 * NT)
                with pool.Fori(0, ROUNDS) as it:
                    for b in range(2):
                        pool.wait_ge(S(f"xg_transposed{b}"), it + (ROUNDS * layer + 1))
                        pool.tensor_copy(IDXB[:, b:b + 1], IDX[:, bass.ds(2 * it + b, 1)]).then_inc(S(f"idx_ready{b}"), 1)
                        pool.wait_ge(S(f"idx_ready{b}"), it + (ROUNDS * layer + 1))
                        pool.sem_inc(S("gathers"), 1)
                        pool.indirect_dma_start(
                            out=XG[:, b, :], out_offset=None, in_=xn_d[layer],
                            in_offset=bass.IndirectOffsetOnAxis(ap=IDXB[:, b:b + 1], axis=0),
                        ).then_inc(S(f"xg_full{b}"), 16)
                n = pool.value_load(OVR[0:1, layer, 0:1], min_val=0, max_val=OVP)
                before = pool.value_load(OVR[0:1, 0, 0:1], min_val=0, max_val=OVP) if layer else 0
                with pool.Fori(0, OVP) as j:
                    with pool.If(j < n):
                        pool.wait_ge(S("ov_wfree"), before + j + (layer + 1))
                        pool.tensor_copy(IDXB[:, 0:1], IDX[:, bass.ds(j + PAIRS, 1)]).then_inc(S("ov_idx"), 1)
                        pool.wait_ge(S("ov_idx"), before + (j + 1))
                        pool.sem_inc(S("gathers"), 1)
                        pool.indirect_dma_start(
                            out=XG[:, 0, :], out_offset=None, in_=xn_d[layer],
                            in_offset=bass.IndirectOffsetOnAxis(ap=IDXB[:, 0:1], axis=0),
                        ).then_inc(S("ov_x"), 16)
                pool.wait_ge(S("all_stored"), layer + 1)
                for t in range(NT):
                    for k in range(2):
                        n = 2 * t + k
                        b = n % 4
                        if n >= 4:
                            pool.wait_ge(S("yg_used"), layer * 10 + n - 3)
                        pool.indirect_dma_start(
                            out=YG[0:ROWS[t], b, :], out_offset=None, in_=y_d[layer],
                            in_offset=bass.IndirectOffsetOnAxis(ap=SLI[0:ROWS[t], t, k:k + 1], axis=0),
                        ).then_inc(S(f"yg_full{b}"), 16)
                end_phase(pool, ph)

            moe(0, 4)
            end_phase(pool, 5)
            pool.wait_ge(S("al_in"), 16 * NT)
            for k in range(NB):
                if k >= 2:
                    pool.wait_ge(S("u_transposed"), k - 1)
                pool.tensor_copy(UA[:, k % 2], AL[:, :, 8 * CH * k:8 * CH * (k + 1)].rearrange(
                    "p s (g c) -> p g s c", g=8)).then_inc(S("u_gathered"), 1)
            end_phase(pool, 6)
            end_phase(pool, 7)
            end_phase(pool, 8)
            moe(1, 9)

        def norm_act(act, n):
            for t in range(NT):
                if n == 0:
                    act.wait_ge(S(f"x_in{t}"), 16)
                else:
                    act.wait_ge(S("x_updated"), NT * (n - 1) + t + 1)
                r = ROWS[t]
                nc.scalar.activation(XN[0:r, t, :], X[0:r, t, :], ACT.Square,
                                     accum_out=SS[0:r, n, t:t + 1]).then_inc(S("squares"), 1)
                act.wait_ge(S("squares"), NT * n + t + 1)
                nc.scalar.activation(RSTD[0:r, n, t:t + 1], SS[0:r, n, t:t + 1], ACT.Sqrt, bias=EPSC[0:r, :],
                                     scale=1.0 / D).then_inc(S("roots"), 1)

        TBASE = {0: 0, 1: 5, 3: 10}

        def xt_act(act, n):
            for t in range(NT):
                act.wait_ge(S("x_transposed"), TBASE[n] + t + 1)
                r = ROWS[t]
                nc.scalar.activation(XT[:, :, t * P:t * P + r], bank(2 * (t % 2), 2).rearrange(
                    "p b (c t) -> p (b c) t", c=4)[:, :, 0:r], ACT.Copy).then_inc(S("xt_ready"), 1)

        def norm_dve(dve, ch, n):
            for t in range(NT):
                dve.wait_ge(S("roots"), NT * n + t + 1)
                r = ROWS[t]
                ch(nc.vector.reciprocal(RSTD[0:r, n, t:t + 1], RSTD[0:r, n, t:t + 1]))
                if t == 0:
                    dve.wait_ge(S("gamma_in"), 16 * (n + 1))
                nc.vector.scalar_tensor_tensor(out=XN[0:r, t, :], in0=X[0:r, t, :], scalar=RSTD[0:r, n, t:t + 1],
                                               in1=GAM[0:r, :], op0=ALU.mult, op1=ALU.mult).then_inc(S("xn_done"), 1)

        def xt_pe(pe, n):
            for t in range(NT):
                pe.wait_ge(S("xn_done"), NT * n + t + 1)
                if n == 0 and t == 0:
                    pe.wait_ge(S("ident_ready"), 1)
                if t >= 2:
                    pe.wait_ge(S("xt_ready"), TBASE[n] + t - 1)
                r = ROWS[t]
                for c in range(KC):
                    last = nc.tensor.transpose(PSUM[:, 2 * (t % 2) + c // 4, (c % 4) * P:(c % 4) * P + r],
                                               XN[0:r, t, c * P:(c + 1) * P], IDENT[0:r, 0:r])
                last.then_inc(S("x_transposed"), 1)

        def gamma_load(act, n):
            src = [norm_mix[0:1, :], norm_ffn[0:1, :], norm_mix[1:2, :], norm_ffn[1:2, :],
                   norm_final.rearrange("(o d) -> o d", o=1)][n]
            if n:
                act.wait_ge(S("xn_done"), NT * n)
            act.dma_start(GAM[:, :], src.to_broadcast([P, D])).then_inc(S("gamma_in"), 16)

        UNITS = [("p", b, h) for b in range(NBLK) for h in range(KVH)] + [("s", 0, 0), ("s", 1, 0)]
        NU = len(UNITS)

        def width(u):
            kind, b, _ = u
            return 192 if kind == "s" else (P if b == 0 else 2 * P)

        def scores_ps(i, w):
            return bank(2 * (i % 2), 2).rearrange("p b (g k) -> p (b g) k", g=2)[:, :, 0:w]

        def scores_sb(i, w):
            return SB_[:, i % 2, :].rearrange("p (g k) -> p g k", g=4)[:, :, 0:w]

        @block.scalar
        def _(act):
            ch = Chain(act, "act_chain")
            for b in range(2):
                act.sem_inc(S(f"xgt_ready{b}"), 1)
                act.sem_inc(S(f"yb_act{b}"), 1)
                act.sem_inc(S(f"y_stored{b}"), 16)
            gamma_load(act, 0)
            act.dma_start(BQKV, b_qkv[0:1, :].to_broadcast([P, QKV])).then_inc(S("att_in"), 16)
            act.dma_start(CS[:, 0:4, :], cs_tab[0:SEQ, :].rearrange("(t p) n -> p t n", p=P)).then_inc(S("att_in"), 16)
            act.dma_start(CS[0:64, 4, :], cs_tab[SEQ:NTOK, :]).then_inc(S("att_in"), 16)
            act.dma_start(SINK, sinks[0:1, :].to_broadcast([P, NH])).then_inc(S("att_in"), 16)
            act.dma_start(SINKS, sinks.rearrange("o (h u) -> (o h) u", u=1).unsqueeze(1).to_broadcast([NH, 8, 1])
                          ).then_inc(S("att_in"), 16)
            act.dma_start(BO, b_o[0:1, :].to_broadcast([P, D])).then_inc(S("att_in"), 16)
            act.dma_start(VC, cache_v[0].rearrange("s r h d -> r s (h d)")).then_inc(S("vc_in"), 16)
            act.dma_start(nk_s[0, :, 0:P - DSEQ, :, :].rearrange("s r h d -> s r (h d)"),
                          cache_k[0, :, DSEQ:P, :, :].rearrange("s r h d -> s r (h d)")).then_inc(S("win_out"), 16)
            act.dma_start(nv_s[0, :, 0:P - DSEQ, :, :].rearrange("s r h d -> s r (h d)"),
                          cache_v[0, :, DSEQ:P, :, :].rearrange("s r h d -> s r (h d)")).then_inc(S("win_out"), 16)
            act.wait_ge(S("eps_ready"), 1)
            norm_act(act, 0)
            xt_act(act, 0)
            gamma_load(act, 1)
            for t in range(NT):
                act.wait_ge(S("qk_transposed"), t + 1)
                if t < 4:
                    nc.scalar.activation(QT[:, 0:4, t * P:(t + 1) * P], PSUM[:, 6, :].rearrange("p (c t) -> p c t", c=4),
                                         ACT.Copy)
                    nc.scalar.activation(QT[:, 4:8, t * P:(t + 1) * P], PSUM[:, 7, :].rearrange("p (c t) -> p c t", c=4),
                                         ACT.Copy).then_inc(S("qt_ready"), 1)
                    act.wait_ge(S("k_transposed"), t + 1)
                    nc.scalar.activation(KT[:, :, t * P:(t + 1) * P], PSUM[:, 6, :].rearrange("p (c t) -> p c t", c=4),
                                         ACT.Copy).then_inc(S("kt_ready"), 1)
                else:
                    nc.scalar.activation(QTS.rearrange("p s (h t) -> p h s t", h=NH),
                                         PSUM[0:64, 6:8, :].rearrange("p b (c s t) -> p (b c) s t", s=NSEQ, t=DSEQ),
                                         ACT.Copy).then_inc(S("qt_ready"), 1)
                    act.wait_ge(S("k_transposed"), t + 1)
                    nc.scalar.activation(KTS, PSUM[0:64, 6, 0:256].rearrange("p (c t) -> p c t", t=64),
                                         ACT.Copy).then_inc(S("kt_ready"), 1)
                if t == 3:
                    act.wait_ge(S("rotated"), 4)
                    act.dma_start(nk_p[0, 0].rearrange("r h d -> r h d"),
                                  KD[:, 1, :].rearrange("p (h w d) -> p h w d", h=KVH, w=2)[:, :, 0, :]
                                  ).then_inc(S("win_out"), 16)
                    act.dma_start(nv_p[0, 0].rearrange("r h d -> r (h d)"), V[:, 3, :]).then_inc(S("win_out"), 16)
            act.wait_ge(S("rotated"), 5)
            for i in range(NSEQ):
                act.dma_start(nk_s[0, i, P - DSEQ:P, :, :],
                              KD[8 * i:8 * i + 8, 0, :].rearrange("p (h w d) -> p h w d", h=KVH, w=2)[:, :, 0, :]
                              ).then_inc(S("win_out"), 16)
                act.dma_start(nv_s[0, i, P - DSEQ:P, :, :].rearrange("r h d -> r (h d)"),
                              V[8 * i:8 * i + 8, 4, :]).then_inc(S("win_out"), 16)
            act.wait_ge(S("win_out"), 16 * (4 + 2 * NSEQ))
            end_phase(act, 1)
            act.dma_start(CK, cache_k[0].rearrange("s r h d -> r s (h d)")).then_inc(S("ck_in"), 16)
            for i in range(NSEQ):
                act.wait_ge(S("ck_transposed"), i + 1)
                nc.scalar.activation(KCT[:, i, :, :], PSUM[0:64, 4 + i % 2, :].rearrange("p (h k) -> p h k", h=KVH),
                                     ACT.Copy).then_inc(S("kct_ready"), 1)

            def exps(i):
                act.wait_ge(S("scores_shifted"), i + 1)
                w = width(UNITS[i])
                sc = scores_sb(i, w)
                nc.scalar.activation(SM[:, 48:52], SM[:, 8 + 4 * (i % 2):12 + 4 * (i % 2)], ACT.Exp).then_inc(S("sink_exp"), 1)
                nc.scalar.activation(sc, sc, ACT.Exp).then_inc(S("probs"), 1)

            def pt_evac(i):
                act.wait_ge(S("p_transposed"), i + 1)
                if i >= 2:
                    act.wait_ge(S("pv_done"), i - 1)
                if UNITS[i][0] == "p" and UNITS[i][1] == 0:
                    nc.scalar.activation(PT[:, i % 2, 512:1024].rearrange("p (g h q) -> p g h q", g=2, h=2)[:, :, 0, :],
                                         PSUM[:, 5, :].rearrange("p (g h q) -> p g h q", g=2, h=2)[:, :, 0, :],
                                         ACT.Copy).then_inc(S("pt_ready_act"), 1)
                elif UNITS[i][0] == "p":
                    nc.scalar.activation(PT[:, i % 2, 512:1024], PSUM[:, 5, :], ACT.Copy).then_inc(S("pt_ready_act"), 1)
                else:
                    v = PT[:, i % 2, 512:1024].rearrange("p (g h q) -> p g h q", g=2, h=2)
                    ps = PSUM[:, 5, :].rearrange("p (g h q) -> p g h q", g=2, h=2)
                    nc.scalar.activation(v[:, :, 0, :], ps[:, :, 0, :], ACT.Copy)
                    nc.scalar.activation(v[0:64, :, 1, :], ps[0:64, :, 1, :], ACT.Copy).then_inc(S("pt_ready_act"), 1)

            exps(0)
            for i in range(NU):
                if i + 1 < NU:
                    exps(i + 1)
                pt_evac(i)
            end_phase(act, 2)
            for t in range(4):
                act.wait_ge(S("o_transposed"), t + 1)
                nc.scalar.activation(OT[:, :, t * P:(t + 1) * P], bank(2 * (t % 2), 2).rearrange(
                    "p b (c t) -> p (b c) t", c=4), ACT.Copy).then_inc(S("ot_ready"), 1)
            end_phase(act, 3)

            def moe(layer, ph):
                act.dma_start(WR[:, :, 0:4], w_rg[layer].rearrange("(c p) n -> p c n", p=P)).then_inc(S("router_in"), 16)
                act.dma_start(WR[:, :, 4:36], w_re[layer].rearrange("(c p) n -> p c n", p=P)).then_inc(S("router_in"), 16)
                act.dma_start(BR[:, 0:4], b_rg[layer:layer + 1, :].to_broadcast([P, 4])).then_inc(S("router_in"), 16)
                act.dma_start(BR[:, 4:36], b_re_r[layer:layer + 1, :].to_broadcast([P, 32])).then_inc(S("router_in"), 16)
                n = 1 + 2 * layer
                norm_act(act, n)
                xt_act(act, n)
                gamma_load(act, n + 1)
                for t in range(NT):
                    act.dma_start(xn_d[layer][t * P:t * P + ROWS[t], :], XN[0:ROWS[t], t, :]
                                  ).then_inc(S(f"xn_stored{layer}"), 16)
                act.wait_ge(S("group_shifted"), layer + 1)
                nc.scalar.activation(GE, GE, ACT.Exp).then_inc(S("group_exp"), 1)
                act.wait_ge(S("expert_shifted"), layer + 1)
                nc.scalar.activation(EX, EX, ACT.Exp).then_inc(S("expert_exp"), 1)
                act.wait_ge(S("routed"), layer + 1)
                with act.Fori(0, ROUNDS) as it:
                    for b in range(2):
                        done = it + ROUNDS * layer
                        act.wait_ge(S(f"xg_transposed{b}"), done + 2)
                        act.wait_ge(S(f"gate_up{b}"), done + 1)
                        nc.scalar.activation(XGT[:, b, :, :], bank(0, 2).rearrange("p b (c t) -> p (b c) t", c=4),
                                             ACT.Copy).then_inc(S(f"xgt_ready{b}"), 1)
                        act.wait_ge(S(f"gate_up{b}"), done + 2)
                        nc.scalar.activation(SG[:, b, :], PSUM[:, 2 + b, 0:FF], ACT.Silu).then_inc(S(f"silu_ready{b}"), 1)
                        act.wait_ge(S(f"expert_out{b}"), done + 1)
                        act.wait_ge(S(f"y_stored{b}"), it * 16 + 16 * (ROUNDS * layer + 1))
                        nc.scalar.activation(YB[:, b, 512:1024], PSUM[:, 4 + 2 * b + 1, :], ACT.Copy
                                             ).then_inc(S(f"yb_act{b}"), 1)
                        act.wait_ge(S(f"yb_act{b}"), done + 2)
                        act.wait_ge(S(f"yb_dve{b}"), done + 2)
                        act.dma_start(y_d[layer][bass.ds(it * (2 * P) + b * P, P), :], YB[:, b, :]
                                      ).then_inc(S(f"y_stored{b}"), 16)
                for b in range(2):
                    act.wait_ge(S(f"y_stored{b}"), 16 * (ROUNDS * (layer + 1) + 1))
                n = act.value_load(OVR[0:1, layer, 0:1], min_val=0, max_val=OVP)
                before = act.value_load(OVR[0:1, 0, 0:1], min_val=0, max_val=OVP) if layer else 0
                with act.Fori(0, OVP) as j:
                    with act.If(j < n):
                        act.wait_ge(S("ov_xt"), before + (j + 1))
                        nc.scalar.activation(XGT[:, 0, :, :], bank(0, 2).rearrange("p b (c t) -> p (b c) t", c=4),
                                             ACT.Copy).then_inc(S("ov_xgt"), 1)
                        act.wait_ge(S("ov_gu"), before + (j + 1))
                        nc.scalar.activation(SG[:, 0, :], PSUM[:, 2, 0:FF], ACT.Silu).then_inc(S("ov_silu"), 1)
                        act.wait_ge(S("ov_dn"), before + (j + 1))
                        nc.scalar.activation(YB[:, 0, :], bank(4, 2).rearrange("p b n -> p (b n)"), ACT.Copy
                                             ).then_inc(S("ov_yb"), 1)
                        act.wait_ge(S("ov_yb"), before + (j + 1))
                        act.dma_start(y_d[layer][bass.ds((j + PAIRS) * P, P), :], YB[:, 0, :]
                                      ).then_inc(S("ov_y"), 16)
                        act.wait_ge(S("ov_y"), (before + j) * 16 + 16)
                        act.sem_inc(S("ov_wfree"), 1)
                act.sem_inc(S("all_stored"), 1)
                end_phase(act, ph)

            moe(0, 4)
            norm_act(act, 2)
            for k, src in enumerate((a_re, a_im)):
                act.dma_start(NAT[:, k, :], src[0].rearrange("(g w) p -> g (w p)", w=2)).then_inc(S("ssm_in"), 16)
            act.dma_start(DT2, log_dt[0].rearrange("(g w) -> g w", w=2)).then_inc(S("ssm_in"), 16)
            for r, src in enumerate((b_re, b_im)):
                for w in range(2):
                    act.dma_start(BB[64 * w:64 * w + 64, r, :, :],
                                  src[0].rearrange("(g w) p c -> w p g c", w=2)[w]).then_inc(S("ssm_in"), 16)
            for r, src in enumerate((c_re, c_im)):
                for w in range(2):
                    act.dma_start(CL[:, 8 * r:8 * r + 8, 64 * w:64 * w + 64],
                                  src[0].rearrange("(k g) c p -> (g c) k p", g=8)).then_inc(S("ssm_in"), 16)
            for r, src in enumerate((st_re, st_im)):
                act.dma_start(SIN_[:, r, :, :], src[0].rearrange("s (g w) p -> g s (w p)", w=2)).then_inc(S("ssm_in"), 16)
            act.dma_start(NAT[:, 23, 0:32], ssm_d[0].rearrange("(g q) -> g q", q=32)).then_inc(S("ssm_in"), 16)
            act.wait_ge(S("ssm_in"), 16 * 14)
            nc.scalar.activation(DT2, DT2, ACT.Exp).then_inc(S("delta"), 1)
            act.wait_ge(S("angles"), 1)
            nc.scalar.activation(NAT[:, 4, :], NAT[:, 4, :], ACT.Exp)
            nc.scalar.activation(NAT[:, 7, :], NAT[:, 6, :], ACT.Sin)
            nc.scalar.activation(NAT[:, 9, :], NAT[:, 8, :], ACT.Sin).then_inc(S("trig"), 1)
            act.wait_ge(S("par_transposed"), 1)
            nc.scalar.activation(DCOL, PSUM[0:CH, 7, 0:64].rearrange("p (w g) -> p w g", w=2), ACT.Copy)
            nc.scalar.activation(PW[:, :, 1, :], PSUM[:, 0, 0:64].rearrange("p (r g) -> p r g", r=2), ACT.Copy)
            nc.scalar.activation(CF, PSUM[:, 0, 64:128].rearrange("p (r g) -> p r g", r=2), ACT.Copy).then_inc(S("par_ready"), 1)
            for r in range(2):
                act.wait_ge(S("st_transposed"), r + 1)
                nc.scalar.activation(H[:, r, :, PCH:NCH].rearrange("p g s -> p s g"),
                                     PSUM[:, 1 + r, 0:256].rearrange("p (s g) -> p s g", s=NSEQ), ACT.Copy
                                     ).then_inc(S("state_ready"), 1)
            for r in range(2):
                act.wait_ge(S("c_transposed"), r + 1)
                for w in range(2):
                    nc.scalar.activation(CT[64 * w:64 * w + 64, r, :, :],
                                         bank(3 + 2 * r, 2).rearrange("p b (g w c) -> p (b g) w c", w=2, c=CH)[
                                             64 * w:64 * w + 64, :, w, :], ACT.Copy).then_inc(S("c_ready"), 1)
            end_phase(act, 5)
            for t in range(NT):
                act.wait_ge(S("xn_done"), 2 * NT + t + 1)
                n = ROWS[t] // L
                act.dma_start(AL[t * 16:t * 16 + n, :, :].rearrange("c s d -> c s d"),
                              XN[0:ROWS[t], t, :]).then_inc(S("al_in"), 16)
            lo, hi = slice(0, 64), slice(64, P)
            for w, src in enumerate((lo, hi)):
                for half in (lo, hi):
                    nc.scalar.activation(A1S[half, w], PW[src, 0], ACT.Copy)
                nc.scalar.activation(B1S[lo, w], CT[src, 0], ACT.Copy)
                ins = nc.scalar.activation(B1S[hi, w], CT[src, 1], ACT.Copy)
            ch(ins)
            nc.scalar.activation(A2S[lo, 0], PW[lo, 1], ACT.Copy)
            nc.scalar.activation(A2S[hi, 0], PW[lo, 1], ACT.Copy)
            for w in range(2):
                nc.scalar.activation(B2S[lo, w], B1S[hi, w], ACT.Copy)
                ins = nc.scalar.activation(B2S[hi, w], B1S[lo, w], ACT.Copy, scale=-1.0)
            ch(ins)
            ch(nc.scalar.activation(A2S[lo, 1], PW[hi, 1], ACT.Copy))
            for k in range(NB):
                act.wait_ge(S("u_transposed"), k + 1)
                nc.scalar.activation(U[:, 8 * k:8 * k + 8, :].rearrange("p (b g) c -> p b g c", b=2),
                                     PSUM[:, 0:2, 0:4 * NCH].rearrange("p b (g c) -> p b g c", g=4), ACT.Copy
                                     ).then_inc(S("u_ready"), 1)
                act.wait_ge(S("w_transposed"), k + 1)
                nc.scalar.activation(WT.rearrange("p r g n -> p r (g n)"), bank(2, 2), ACT.Copy).then_inc(S("wt_ready"), 1)
                act.wait_ge(S("g_done"), k + 1)
                nc.scalar.activation(G[:, :, BP * k:BP * k + BP, :],
                                     PSUM[:, 4:6, 0:BP * NCH].rearrange("p r (g c) -> p r g c", g=BP), ACT.Copy
                                     ).then_inc(S("g_ready"), 1)
            act.wait_ge(S("w_ready"), NB)
            ch(nc.scalar.activation(BSWAP, BB[lo, 1], ACT.Copy))
            ch(nc.scalar.activation(BB[lo, 1], BB[hi, 0], ACT.Copy))
            nc.scalar.activation(BB[hi, 0], BSWAP, ACT.Copy).then_inc(S("stacked"), 1)
            act.wait_ge(S("hf_transposed"), 1)
            nc.scalar.activation(SOUT[:, 0:2 * P], PSUM[0:32, 0, 0:2 * P], ACT.Copy).then_inc(S("hf_copied"), 1)
            act.wait_ge(S("hf_copied"), 1)
            act.dma_start(hr_p[0, 0].rearrange("(g w) p -> g (w p)", w=2), SOUT[:, 0:P]).then_inc(S("h_out"), 16)
            act.dma_start(hi_p[0, 0].rearrange("(g w) p -> g (w p)", w=2), SOUT[:, P:2 * P]).then_inc(S("h_out"), 16)
            act.wait_ge(S("h_out"), 32)
            for r, dst in enumerate((hr_s, hi_s)):
                act.wait_ge(S("ho_transposed"), r + 1)
                nc.scalar.activation(SOUT[:, 0:NSEQ * P].rearrange("p (b n) -> p b n", b=2),
                                     PSUM[0:32, 2 + 2 * r:4 + 2 * r, :], ACT.Copy).then_inc(S("ho_copied"), 1)
                act.wait_ge(S("ho_copied"), r + 1)
                act.dma_start(dst[0].rearrange("s (g w) p -> g s (w p)", w=2),
                              SOUT[:, 0:NSEQ * P].rearrange("p (s n) -> p s n", s=NSEQ)).then_inc(S("h_out"), 16)
                act.wait_ge(S("h_out"), 48 + 16 * r)
            end_phase(act, 6)
            ch(nc.scalar.activation(HSWAP, H[lo, 1, :, 0:NCH], ACT.Copy))
            ch(nc.scalar.activation(H[lo, 1, :, 0:NCH], H[hi, 0, :, 0:NCH], ACT.Copy))
            nc.scalar.activation(H[hi, 0, :, 0:NCH], HSWAP, ACT.Copy).then_inc(S("stacked"), 1)
            toeplitz(act, 0, 1)
            for k in range(NB):
                if k + 1 < NB:
                    toeplitz(act, k + 1, 1)
                act.wait_ge(S("y_ssm"), k + 1)
                for w in range(2):
                    zv = Z.rearrange("p t (g w c) -> p g w t c", w=2, c=CH)[:, BP * k:BP * k + BP, w, :, :]
                    ins = nc.scalar.activation(zv, PSUM[0:NCH, 4 * (k % 2) + w, :].rearrange(
                        "p (g t c) -> p g t c", g=BP, c=CH), ACT.Gelu_apprx_tanh)
                ins.then_inc(S("z_ready"), 1)
            for t in range(L):
                act.wait_ge(S("z_transposed"), t + 1)
                nc.scalar.activation(
                    XT.rearrange("p c (n t) -> p c n t", t=L)[:, :, :, t],
                    PSUM[:, 2 + 2 * (t % 2):4 + 2 * (t % 2), :].rearrange("p b (c n) -> p (b c) n", c=4)[:, :, 0:NCH],
                    ACT.Copy).then_inc(S("zt_ready"), 1)
            end_phase(act, 7)
            gamma_load(act, 3)
            for n in range(2):
                for t in range(NT):
                    i = n * NT + t
                    act.wait_ge(S("glu_done"), i + 1)
                    if i >= 2:
                        act.wait_ge(S("glu_added"), i - 1)
                    nc.scalar.activation(GL_SG[0:ROWS[t], i % 2, :], PSUM[0:ROWS[t], 2 * (i % 2) + 1, :], ACT.Sigmoid
                                         ).then_inc(S("glu_gate"), 1)
            end_phase(act, 8)
            moe(1, 9)
            norm_act(act, 4)

        @block.vector
        def _(dve):
            ch = Chain(dve, "dve_chain")
            ve = nc.vector
            for b in range(2):
                dve.sem_inc(S(f"yb_dve{b}"), 1)
            norm_dve(dve, ch, 0)
            dve.wait_ge(S("consts_ready"), 1)
            ve.tensor_scalar(PMI[:, 0:1], PIDX[:, :], DSEQ - 1, None, ALU.bitwise_and)
            ch(ve.tensor_scalar(PMI[:, 1:2], PIDX[:, :], CH - 1, None, ALU.bitwise_and))
            ch(ve.tensor_copy(PMOD[:, :], PMI[:, :]))
            ch(ve.tensor_scalar(MSC, IOTA[:, :], PMOD[:, 0:1], -BIG, ALU.is_lt, ALU.mult))
            ch(ve.tensor_scalar(SM[:, 61:62], PMOD[:, 0:1], 56.0, None, ALU.add))
            ch(ve.tensor_scalar(MSN, IOTA[:, 0:120], SM[:, 61:62], -BIG, ALU.is_gt, ALU.mult))
            ch(ve.tensor_scalar(QR[:, 0:120], IOTA[:, 0:120], 56.0, -BIG, ALU.is_lt, ALU.mult))
            ch(ve.tensor_tensor(MSN, MSN, QR[:, 0:120], ALU.add))
            dve.wait_ge(S("att_in"), 16 * 6)
            for t in range(NT):
                r = ROWS[t]
                b0 = 3 * (t % 2)
                dve.wait_ge(S("qkv_done"), t + 1)
                ve.tensor_tensor(QR[0:r, 0:1024], bank(b0, 2).rearrange("p b n -> p (b n)")[0:r, :], BQKV[0:r, 0:1024], ALU.add)
                ve.tensor_tensor(QR[0:r, 1024:1280], PSUM[0:r, b0 + 2, 0:256], BQKV[0:r, 1024:1280], ALU.add)
                ch(ve.tensor_tensor(V[0:r, t, :], PSUM[0:r, b0 + 2, 256:512], BQKV[0:r, 1280:1536], ALU.add))
                q4 = QR[0:r, :].rearrange("p (h w d) -> p h w d", w=2, d=32)
                cos = CS[0:r, t, 0:32].unsqueeze(1).unsqueeze(1)
                sin = CS[0:r, t, 32:64].unsqueeze(1)
                ta = TA[0:r, :].rearrange("p (h w d) -> p h w d", w=2, d=32)
                tb = TB[0:r, :].rearrange("p (h w d) -> p h w d", w=2, d=32)
                ve.tensor_tensor(ta, q4, bc(cos, [r, 20, 2, 32]), ALU.mult).then_inc(S("qkv_read"), 1)
                ve.tensor_tensor(tb[:, :, 0, :], q4[:, :, 1, :], bc(sin, [r, 20, 32]), ALU.mult)
                ch(ve.tensor_tensor(tb[:, :, 1, :], q4[:, :, 0, :], bc(sin, [r, 20, 32]), ALU.mult))
                if t >= 2:
                    dve.wait_ge(S("k_transposed"), t - 1)
                qo = QO[0:r, t % 2, :].rearrange("p (h w d) -> p h w d", w=2, d=32)
                kd = KD[0:r, t % 2, :].rearrange("p (h e w d) -> p h e w d", e=2, w=2, d=32)
                ve.tensor_tensor(qo[:, :, 0, :], ta[:, 0:16, 0, :], tb[:, 0:16, 0, :], ALU.subtract)
                ve.tensor_tensor(qo[:, :, 1, :], ta[:, 0:16, 1, :], tb[:, 0:16, 1, :], ALU.add)
                for e in range(2):
                    ve.tensor_tensor(kd[:, :, e, 0, :], ta[:, 16:20, 0, :], tb[:, 16:20, 0, :], ALU.subtract)
                    last = ve.tensor_tensor(kd[:, :, e, 1, :], ta[:, 16:20, 1, :], tb[:, 16:20, 1, :], ALU.add)
                last.then_inc(S("rotated"), 1)
            end_phase(dve, 1)

            sc_view = lambda ap: ap.rearrange("p (b g k) -> p (b g) k", b=2, g=2)

            def sink_of(i):
                kind, b, h = UNITS[i]
                if kind == "s":
                    return bc(SINKS, [P, 4])
                return SINK[:, 4 * h:4 * h + 4].rearrange("p (g w) -> p w g", w=2)

            def scale_mask(i):
                kind, b, h = UNITS[i]
                w = width(UNITS[i])
                dve.wait_ge(S("scores"), i + 1)
                ps, sc = scores_ps(i, w), scores_sb(i, w)
                if kind == "p" and b == 0:
                    ch(ve.scalar_tensor_tensor(out=sc, in0=ps, scalar=SCALE, in1=bc(MCUR.unsqueeze(1), [P, 4, P]),
                                               op0=ALU.mult, op1=ALU.add))
                elif kind == "p":
                    m = MPCUR.unsqueeze(1)
                    ch(ve.scalar_tensor_tensor(out=sc, in0=ps, scalar=SCALE, in1=bc(m, [P, 4, 2 * P]),
                                               op0=ALU.mult, op1=ALU.add))
                else:
                    ve.scalar_tensor_tensor(out=sc[:, :, 0:P], in0=ps[:, :, 0:P], scalar=SCALE,
                                            in1=bc(MSC.unsqueeze(1), [P, 4, P]), op0=ALU.mult, op1=ALU.add)
                    for j in range(4):
                        off = 56 - 8 * (4 * b + j)
                        ins = ve.scalar_tensor_tensor(out=sc[:, j, P:192], in0=ps[:, j, P:192], scalar=SCALE,
                                                      in1=MSN[:, off:off + 64], op0=ALU.mult, op1=ALU.add)
                    ch(ins)
                ch(ve.tensor_reduce(SM[:, 0:4], sc, AX.X, ALU.max))
                ch(ve.tensor_tensor(SM[:, 4:8], SM[:, 0:4], sink_of(i), ALU.max))
                ve.tensor_tensor(SM[:, 8 + 4 * (i % 2):12 + 4 * (i % 2)], sink_of(i), SM[:, 4:8], ALU.subtract)
                ve.tensor_tensor(sc, sc, bc(SM[:, 4:8].unsqueeze(2), [P, 4, w]), ALU.subtract).then_inc(S("scores_shifted"), 1)

            def denominators(i):
                w = width(UNITS[i])
                dve.wait_ge(S("probs"), i + 1)
                ch(ve.tensor_reduce(SM[:, 16:20], scores_sb(i, w), AX.X, ALU.add))
                ch(ve.tensor_tensor(SM[:, 20:24], SM[:, 16:20], SM[:, 48:52], ALU.add))
                ve.reciprocal(SM[:, 24 + 4 * (i % 2):28 + 4 * (i % 2)], SM[:, 20:24]).then_inc(S("denominator"), 1)

            def pt_evac(i):
                dve.wait_ge(S("p_transposed"), i + 1)
                v = PT[:, i % 2, 0:512].rearrange("p (g h q) -> p g h q", g=2, h=2)
                ps = PSUM[:, 4, :].rearrange("p (g h q) -> p g h q", g=2, h=2)
                if UNITS[i][0] == "p" and UNITS[i][1] == 0:
                    ve.tensor_copy(v[:, :, 0, :], ps[:, :, 0, :]).then_inc(S("pt_ready_dve"), 1)
                elif UNITS[i][0] == "p":
                    ve.tensor_copy(PT[:, i % 2, 0:512], PSUM[:, 4, :]).then_inc(S("pt_ready_dve"), 1)
                else:
                    ve.tensor_copy(v[:, :, 0, :], ps[:, :, 0, :])
                    ve.tensor_copy(v[0:64, :, 1, :], ps[0:64, :, 1, :]).then_inc(S("pt_ready_dve"), 1)

            def out_scale(i):
                kind, b, h = UNITS[i]
                dve.wait_ge(S("pv_done"), i + 1)
                dve.wait_ge(S("denominator"), i + 1)
                rd = SM[:, 24 + 4 * (i % 2):28 + 4 * (i % 2)].unsqueeze(2)
                ps = PSUM[:, 6, 0:256].rearrange("p (g d) -> p g d", g=4)
                if kind == "p":
                    o = O[:, b, h * 256:(h + 1) * 256].rearrange("p (g w d) -> p w g d", g=2, w=2)
                    ve.tensor_tensor(o, ps.rearrange("p (w g) d -> p w g d", w=2),
                                     bc(rd, [P, 4, HD]).rearrange("p (w g) d -> p w g d", w=2), ALU.mult).then_inc(S("o_scaled"), 1)
                else:
                    if b:
                        dve.wait_ge(S("od_transposed"), 1)
                    for e in range(2):
                        ins = ve.tensor_tensor(OD[:, :, e * 64:(e + 1) * 64], ps, bc(rd, [P, 4, HD]), ALU.mult)
                    ins.then_inc(S("o_scaled"), 1)

            def od_evac(b):
                dve.wait_ge(S("od_transposed"), b + 1)
                ps = PSUM[:, 7 if b == 0 else 0, :].rearrange("p (s h t) -> p s h t", s=4, h=NH)
                for w in range(2):
                    for j in range(4):
                        col = SEQ + (4 * b + j) * 8
                        ins = ve.tensor_copy(OT[64 * w:64 * w + 64, :, col:col + 8],
                                             ps[64 * w:64 * w + 64, j, :, :].rearrange("p (c w) t -> p c w t", w=2)[:, :, w, :])
                ins.then_inc(S("ots_ready"), 1)

            scale_mask(0)
            denominators(0)
            for i in range(NU):
                if i + 1 < NU:
                    scale_mask(i + 1)
                pt_evac(i)
                if i + 1 < NU:
                    denominators(i + 1)
                out_scale(i)
            end_phase(dve, 2)
            od_evac(0)
            od_evac(1)
            for t in range(NT):
                r = ROWS[t]
                dve.wait_ge(S("wo_done"), t + 1)
                b0 = 4 + 2 * (t % 2)
                ch(ve.tensor_tensor(X[0:r, t, :], X[0:r, t, :], BO[0:r, :], ALU.add))
                ve.tensor_tensor(X[0:r, t, :], X[0:r, t, :], bank(b0, 2).rearrange("p b n -> p (b n)")[0:r, :],
                                 ALU.add).then_inc(S("x_updated"), 1)
            end_phase(dve, 3)

            def moe(layer, ph):
                norm_dve(dve, ch, 1 + 2 * layer)
                dve.wait_ge(S("router_in"), 64 * (layer + 1))
                ch(ve.memset(LG, 0.0))
                ch(ve.memset(GL8, -BIG))
                dve.wait_ge(S("logits"), layer + 1)
                ps = PSUM[:, 4, 0:NT * 36].rearrange("p (t n) -> p t n", t=NT)
                ve.tensor_tensor(LG[:, 0:4, :], ps[:, 0:4, :], bc(BR.unsqueeze(1), [P, 4, 36]), ALU.add)
                ch(ve.tensor_tensor(LG[0:64, 4, :], ps[0:64, 4, :], BR[0:64, :], ALU.add))
                ch(ve.tensor_copy(GL8[:, :, 0:4], LG[:, :, 0:4]))
                for t in range(NT):
                    ch(ve.max(GM8[:, t, :], GL8[:, t, :]))
                    ch(ve.max_index(GI8[:, t, :], GM8[:, t, :], GL8[:, t, :]))
                ve.tensor_tensor(GE, LG[:, :, 0:4], bc(GM8[:, :, 0:1], [P, NT, 4]), ALU.subtract).then_inc(S("group_shifted"), 1)
                ch(ve.tensor_copy(GIF, GI8[:, :, 0]))
                ch(ve.tensor_tensor(GOH, bc(IOTA[:, 0:4].unsqueeze(1), [P, NT, 4]), bc(GIF.unsqueeze(2), [P, NT, 4]), ALU.is_equal))
                em4 = EM.rearrange("p t (g e) -> p t g e", g=NG)
                lge = LG[:, :, 4:36].rearrange("p t (g e) -> p t g e", g=NG)
                ch(ve.tensor_tensor(em4, lge, bc(GOH.unsqueeze(3), [P, NT, NG, EPG]), ALU.mult))
                ch(ve.tensor_scalar(GOH, GOH, BIG, -BIG, ALU.mult, ALU.add))
                ch(ve.tensor_tensor(em4, em4, bc(GOH.unsqueeze(3), [P, NT, NG, EPG]), ALU.add))
                for t in range(NT):
                    ch(ve.max(EV8[:, t, :], EM[:, t, :]))
                    ch(ve.max_index(EI8[:, t, :], EV8[:, t, :], EM[:, t, :]))
                ve.tensor_tensor(EX, EV8[:, :, 1], EV8[:, :, 0], ALU.subtract).then_inc(S("expert_shifted"), 1)
                ch(ve.tensor_copy(EIF, EI8[:, :, 0:2]))
                ch(ve.tensor_tensor(EOH, bc(IOTA[:, 0:32].unsqueeze(1).unsqueeze(1), [P, NT, 2, 32]),
                                    bc(EIF.unsqueeze(3), [P, NT, 2, 32]), ALU.is_equal))
                ch(ve.memset(EOH[64:P, 4, :, :], 0.0))
                ve.tensor_tensor(MM, EOH[:, :, 0, :], EOH[:, :, 1, :], ALU.add).then_inc(S("chosen"), 1)
                dve.wait_ge(S("group_exp"), layer + 1)
                ch(ve.tensor_reduce(GV, GE, AX.X, ALU.add))
                dve.wait_ge(S("expert_exp"), layer + 1)
                ch(ve.tensor_scalar(CW[:, :, 1], EX, 1.0, None, ALU.add))
                ch(ve.tensor_tensor(CW[:, :, 1], CW[:, :, 1], GV, ALU.mult))
                ch(ve.reciprocal(CW[:, :, 0], CW[:, :, 1]))
                ch(ve.tensor_tensor(CW[:, :, 1], CW[:, :, 0], EX, ALU.mult))
                dve.wait_ge(S("ranks"), layer + 1)
                ch(ve.tensor_copy(RK, PSUM[:, 5, 0:192].rearrange("p (t n) -> p t n", t=6)))
                ch(ve.tensor_scalar(OVN, RK[:, 5, :], float(CAP - 1), None, ALU.add))
                ch(ve.tensor_copy(OVNI, OVN))
                ch(ve.tensor_scalar(OVNI, OVNI, CAP.bit_length() - 1, None, ALU.logical_shift_right))
                ch(ve.tensor_copy(OVN, OVNI))
                ch(ve.tensor_scalar(OVN, OVN, -1.0, None, ALU.add))
                ch(ve.tensor_scalar(OVN, OVN, 0.0, None, ALU.max))
                ch(ve.memset(OVM, 1.0))
                ch(ve.tensor_tensor_scan(OVI, OVM, OVN, 0.0, ALU.mult, ALU.add))
                ch(ve.tensor_tensor(OVE, OVI, OVN, ALU.subtract))
                rk4 = bc(RK[:, 0:NT, :].unsqueeze(2), [P, NT, 2, 32])
                ch(ve.tensor_tensor(ET, EOH, rk4, ALU.mult))
                ch(ve.tensor_reduce(RR, ET, AX.X, ALU.add))
                ch(ve.tensor_tensor(ET, EOH, bc(OVE.unsqueeze(1).unsqueeze(1), [P, NT, 2, 32]), ALU.mult))
                ch(ve.tensor_reduce(OB, ET, AX.X, ALU.add))
                ch(ve.tensor_scalar(SL, EIF, float(CAP), None, ALU.mult))
                ch(ve.tensor_scalar(OB, OB, float(CAP), float(NE * CAP - CAP), ALU.mult, ALU.add))
                ch(ve.tensor_tensor(OB, OB, SL, ALU.subtract))
                ch(ve.tensor_scalar(SMOD, RR, float(CAP), None, ALU.is_ge))
                ch(ve.tensor_tensor(OB, OB, SMOD, ALU.mult))
                ch(ve.tensor_tensor(SL, SL, RR, ALU.add))
                ch(ve.tensor_tensor(SL, SL, OB, ALU.add))
                ch(ve.tensor_copy(SLI, SL))
                ve.tensor_scalar(SMI, SLI, P - 1, None, ALU.bitwise_and)
                ch(ve.tensor_scalar(SDI, SLI, P.bit_length() - 1, None, ALU.logical_shift_right))
                ve.tensor_copy(SMOD, SMI)
                ch(ve.tensor_copy(SDIV, SDI))
                ve.tensor_tensor(R1, bc(IOTA[:, 0:P].unsqueeze(1).unsqueeze(1), [P, NT, 2, P]),
                                 bc(SMOD.unsqueeze(3), [P, NT, 2, P]), ALU.is_equal)
                ch(ve.tensor_tensor(P1, bc(IOTA[:, 0:NPAIR].unsqueeze(1).unsqueeze(1), [P, NT, 2, NPAIR]),
                                    bc(SDIV.unsqueeze(3), [P, NT, 2, NPAIR]), ALU.is_equal))
                ve.tensor_tensor(P1, P1, bc(TOKID[:, :].unsqueeze(2).unsqueeze(2), [P, NT, 2, NPAIR]), ALU.mult
                                 ).then_inc(S("onehots"), 1)
                ch(ve.tensor_tensor(EIDT[0:1], bc(OVI[0:1, :].unsqueeze(1), [1, 2 * OVP, 32]),
                                    bc(IOTA[0:1, 0:2 * OVP].unsqueeze(2), [1, 2 * OVP, 32]), ALU.is_le))
                ch(ve.tensor_reduce(EIDF[0:1, :], EIDT[0:1], AX.X, ALU.add))
                ch(ve.tensor_scalar(EIDF[0:1, :], EIDF[0:1, :], float(NE - 1), None, ALU.min))
                ch(ve.tensor_copy(OVR[0:1, layer, 1:1 + 2 * OVP], EIDF[0:1, :]))
                ch(ve.tensor_scalar(NPF[0:1, 0:1], OVI[0:1, 31:32], 1.0, None, ALU.add))
                ch(ve.tensor_copy(OVR[0:1, layer, 0:1], NPF[0:1, 0:1]))
                ch(ve.tensor_scalar(OVR[0:1, layer, 0:1], OVR[0:1, layer, 0:1], 1, None, ALU.logical_shift_right))
                dve.wait_ge(S("token_lists"), layer + 1)
                ch(ve.tensor_copy(IDX, PSUM[:, 6, 0:NPAIR]))
                dve.sem_inc(S("routed"), 1)
                with dve.Fori(0, ROUNDS) as it:
                    for b in range(2):
                        done = it + ROUNDS * layer
                        dve.wait_ge(S(f"silu_ready{b}"), done + 1)
                        ve.tensor_tensor(HTM[:, b, :], SG[:, b, :], PSUM[:, 2 + b, FF:2 * FF], ALU.mult
                                         ).then_inc(S(f"hidden_ready{b}"), 1)
                        dve.wait_ge(S(f"hidden_transposed{b}"), done + 1)
                        ve.tensor_copy(HID[:, b, :, :].rearrange("p m t -> p (m t)"), PSUM[:, 2 + b, 256:256 + P]
                                       ).then_inc(S(f"hid_ready{b}"), 1)
                        dve.wait_ge(S(f"expert_out{b}"), done + 1)
                        dve.wait_ge(S(f"y_stored{b}"), it * 16 + 16 * (ROUNDS * layer + 1))
                        ve.tensor_copy(YB[:, b, 0:512], PSUM[:, 4 + 2 * b, :]).then_inc(S(f"yb_dve{b}"), 1)
                n = dve.value_load(OVR[0:1, layer, 0:1], min_val=0, max_val=OVP)
                before = dve.value_load(OVR[0:1, 0, 0:1], min_val=0, max_val=OVP) if layer else 0
                with dve.Fori(0, OVP) as j:
                    with dve.If(j < n):
                        dve.wait_ge(S("ov_silu"), before + (j + 1))
                        ve.tensor_tensor(HTM[:, 0, :], SG[:, 0, :], PSUM[:, 2, FF:2 * FF], ALU.mult
                                         ).then_inc(S("ov_htm"), 1)
                        dve.wait_ge(S("ov_ht"), before + (j + 1))
                        ve.tensor_copy(HID[:, 0, :, :].rearrange("p m t -> p (m t)"), PSUM[:, 2, 256:256 + P]
                                       ).then_inc(S("ov_hid"), 1)
                for t in range(NT):
                    r = ROWS[t]
                    for k in range(2):
                        n = 2 * t + k
                        b = n % 4
                        cnt = layer * (3 if b < 2 else 2) + n // 4 + 1
                        dve.wait_ge(S(f"yg_full{b}"), 16 * cnt)
                        ins = ve.scalar_tensor_tensor(out=X[0:r, t, :], in0=YG[0:r, b, :], scalar=CW[0:r, t, k:k + 1],
                                                      in1=X[0:r, t, :], op0=ALU.mult, op1=ALU.add)
                        ins.then_inc(S("yg_used"), 1)
                        dve.wait_ge(S("yg_used"), layer * 10 + n + 1)
                    dve.sem_inc(S("x_updated"), 1)
                end_phase(dve, ph)

            moe(0, 4)
            norm_dve(dve, ch, 2)
            N = [NAT[:, k, :] for k in range(24)]
            TWO_PI = 2 * math.pi
            C1 = 6.28125
            C2 = TWO_PI - C1
            MAGIC = 12582912.0
            dve.wait_ge(S("delta"), 1)
            dt_b = bc(DT2.unsqueeze(2), [32, 2, 64])
            n3 = lambda v: v.rearrange("p (w q) -> p w q", w=2)
            ch(ve.tensor_tensor(n3(N[4]), n3(N[0]), dt_b, ALU.mult))
            ch(ve.tensor_tensor(n3(N[5]), n3(N[1]), dt_b, ALU.mult))
            ch(ve.tensor_scalar(N[10], N[5], 1.0 / TWO_PI, None, ALU.mult))
            ch(ve.tensor_scalar(N[10], N[10], MAGIC, None, ALU.add))
            ch(ve.tensor_scalar(N[10], N[10], MAGIC, None, ALU.subtract))
            ch(ve.scalar_tensor_tensor(out=N[6], in0=N[10], scalar=-C1, in1=N[5], op0=ALU.mult, op1=ALU.add))
            ch(ve.scalar_tensor_tensor(out=N[6], in0=N[10], scalar=-C2, in1=N[6], op0=ALU.mult, op1=ALU.add))
            ch(ve.tensor_scalar(N[6], N[6], 3.1415925, -3.1415925, ALU.min, ALU.max))
            ch(ve.tensor_scalar(N[8], N[6], -1.0, None, ALU.mult))
            ch(ve.tensor_tensor(N[8], N[8], N[6], ALU.max))
            ch(ve.tensor_scalar(N[8], N[8], -1.0, math.pi / 2, ALU.mult, ALU.add))
            dve.sem_inc(S("angles"), 1)
            dve.wait_ge(S("trig"), 1)
            ve.tensor_tensor(N[12], N[4], N[9], ALU.mult)
            ch(ve.tensor_tensor(N[13], N[4], N[7], ALU.mult))
            ch(ve.tensor_scalar(N[11], N[12], -1.0, None, ALU.add))
            ve.tensor_tensor(N[16], N[0], N[0], ALU.mult)
            ch(ve.tensor_tensor(N[17], N[1], N[1], ALU.mult))
            ch(ve.tensor_tensor(N[16], N[16], N[17], ALU.add))
            ch(ve.reciprocal(N[18], N[16]))
            ve.tensor_tensor(N[19], N[11], N[0], ALU.mult)
            ch(ve.tensor_tensor(N[20], N[13], N[1], ALU.mult))
            ch(ve.tensor_tensor(N[19], N[19], N[20], ALU.add))
            ch(ve.tensor_tensor(N[14], N[19], N[18], ALU.mult))
            ve.tensor_tensor(N[21], N[13], N[0], ALU.mult)
            ch(ve.tensor_tensor(N[22], N[11], N[1], ALU.mult))
            ch(ve.tensor_tensor(N[21], N[21], N[22], ALU.subtract))
            ch(ve.tensor_tensor(N[15], N[21], N[18], ALU.mult))
            dve.sem_inc(S("par_done"), 1)
            dve.wait_ge(S("par_ready"), 1)
            ve.memset(PW[:, 0, 0, :], 1.0)
            ch(ve.memset(PW[:, 1, 0, :], 0.0))

            def cmul(o, x, y, t1, t2, sub_im=False):
                ve.tensor_tensor(t1, x[0], y[0], ALU.mult)
                ch(ve.tensor_tensor(t2, x[1], y[1], ALU.mult))
                ch(ve.tensor_tensor(o[0], t1, t2, ALU.subtract))
                ve.tensor_tensor(t1, x[0], y[1], ALU.mult)
                ch(ve.tensor_tensor(t2, x[1], y[0], ALU.mult))
                ch(ve.tensor_tensor(o[1], t1, t2, ALU.add))

            for lo, hi, by in ((1, 2, 1), (1, 3, 2), (1, 5, 4)):
                n = hi - lo
                x = [PW[:, r, lo:hi, :] for r in range(2)]
                y = [bc(PW[:, r, by:by + 1, :], [P, n, GP]) for r in range(2)]
                o = [PW[:, r, lo + by:hi + by, :] for r in range(2)]
                t1 = CC.rearrange("p a x g -> p (a x) g")[:, 0:n, :]
                t2 = PR.rearrange("p a x g -> p (a x) g")[:, 0:n, :]
                cmul(o, x, y, t1, t2)
            for k in range(8):
                ve.tensor_copy(PWR[:, :, k, :], PW[:, :, 7 - k, :])
            ve.tensor_copy(CC[:, 0, 0, :], PW[:, 0, 8, :])
            ve.tensor_copy(CC[:, 1, 1, :], PW[:, 0, 8, :])
            ve.tensor_copy(CC[:, 1, 0, :], PW[:, 1, 8, :])
            ch(ve.tensor_scalar(CC[:, 0, 1, :], PW[:, 1, 8, :], -1.0, None, ALU.mult))
            cf = [bc(CF[:, r, :].unsqueeze(2), [P, GP, CH]) for r in range(2)]
            SCR4 = PH[:, 32 * P:48 * P].rearrange("p (k g c) -> p k g c", k=4, g=GP)
            bb = [BB[:, r, :, :] for r in range(2)]
            for k, (i, j) in enumerate(((0, 0), (1, 1), (0, 1), (1, 0))):
                ins = ve.tensor_tensor(SCR4[:, k], cf[i], bb[j], ALU.mult)
            ch(ins)
            ve.tensor_tensor(bb[0], SCR4[:, 0], SCR4[:, 1], ALU.subtract)
            ch(ve.tensor_tensor(bb[1], SCR4[:, 2], SCR4[:, 3], ALU.add))
            dve.wait_ge(S("c_ready"), 4)
            ch(ve.tensor_scalar(CT[:, 1, :, :], CT[:, 1, :, :], -1.0, None, ALU.mult))
            ch(ve.tensor_tensor(EYE, PMOD[0:CH, 1:2].to_broadcast([CH, CH]), IOTA[0:CH, 0:CH], ALU.is_equal))
            ch(ve.tensor_tensor(DD[0], bc(EYE.unsqueeze(1).unsqueeze(1), [CH, 2, GP, CH]),
                                bc(DCOL.unsqueeze(3), [CH, 2, GP, CH]), ALU.mult))
            ch(ve.tensor_copy(DD[1], DD[0]))
            end_phase(dve, 5)
            ch(ve.memset(H[:, :, :, 0], 0.0))
            for k in range(NB):
                g0 = BP * k
                pw = [PWR[:, r, :, g0:g0 + BP].rearrange("p k g -> p g k").unsqueeze(3) for r in range(2)]
                pw = [bc(v, [P, BP, L, CH]) for v in pw]
                bv = [bc(BB[:, r, g0:g0 + BP, :].unsqueeze(2), [P, BP, L, CH]) for r in range(2)]
                t1 = TMPW[:, 0:BP * P].rearrange("p (g s c) -> p g s c", g=BP, s=L)
                t2 = TMPX[:, 0:BP * P].rearrange("p (g s c) -> p g s c", g=BP, s=L)
                o = [WSB[:, r].rearrange("p g (s c) -> p g s c", s=L) for r in range(2)]
                if k:
                    dve.wait_ge(S("w_transposed"), k)
                cmul(o, pw, bv, t1, t2)
                dve.sem_inc(S("w_ready"), 1)
            dve.wait_ge(S("g_ready"), NB)
            dve.wait_ge(S("state_ready"), 2)
            ch0 = ch.n

            def step(c, out):
                h = H[:, :, :, c:c + 1] if isinstance(c, int) else H[:, :, :, bass.ds(c, 1)]
                g = G[:, :, :, c:c + 1] if isinstance(c, int) else G[:, :, :, bass.ds(c, 1)]
                h = h.rearrange("p r g o -> p r (g o)")
                g = g.rearrange("p r g o -> p r (g o)")
                ins = ve.tensor_tensor(PR, CC, bc(h.unsqueeze(1), [P, 2, 2, GP]), ALU.mult)
                yield ins
                yield ve.tensor_tensor(QQ, PR[:, :, 0, :], PR[:, :, 1, :], ALU.add)
                yield ve.tensor_tensor(out, QQ, g, ALU.add)

            for c in range(PCH):
                out = HF if c == PCH - 1 else H[:, :, :, c + 1]
                for ins in step(c, out):
                    ch(ins)
            for a_ in range(2):
                hs = [H[:, r, :, PCH:NCH] for r in range(2)]
                t1 = TMPW[:, 0:GP * NSEQ].rearrange("p (g s) -> p g s", g=GP)
                t2 = TMPX[:, 0:GP * NSEQ].rearrange("p (g s) -> p g s", g=GP)
                ve.tensor_tensor(t1, bc(CC[:, a_, 0, :].unsqueeze(2), [P, GP, NSEQ]), hs[0], ALU.mult)
                ch(ve.tensor_tensor(t2, bc(CC[:, a_, 1, :].unsqueeze(2), [P, GP, NSEQ]), hs[1], ALU.mult))
                ch(ve.tensor_tensor(t1, t1, t2, ALU.add))
                ch(ve.tensor_tensor(HO[:, a_], t1, G[:, a_, :, PCH:NCH], ALU.add))
            dve.sem_inc(S("scanned"), 1)
            end_phase(dve, 6)
            for b in range(2):
                ins = ve.memset(KP[b][:, :, :, 0:112], 0.0)
            ch(ins)

            def decayed_c(k):
                g0 = BP * k
                tmp = TMPV.rearrange("p (w g s c) -> p w g s c", w=2, g=BP, s=9)
                if k >= 3:
                    dve.wait_ge(S("y_ssm"), k - 2)
                for w in range(2):
                    for out, pw, cv in ((VV[:, k % 3], A1S, B1S), (None, A2S, B2S)):
                        o = tmp[:, w] if out is None else out[:, w].rearrange("p g (s c) -> p g s c", s=9)
                        ins = ve.tensor_tensor(
                            o, bc(pw[:, w, :, g0:g0 + BP].rearrange("p k g -> p g k").unsqueeze(3), [P, BP, 9, CH]),
                            bc(cv[:, w, g0:g0 + BP, :].unsqueeze(2), [P, BP, 9, CH]), ALU.mult)
                ch(ins)
                vv = VV[:, k % 3].rearrange("p w g n -> p (w g n)")
                ch(ve.tensor_tensor(vv, vv, TMPV, ALU.add))
                dve.sem_inc(S("v_ready"), 1)

            def taps_out(k):
                g0 = BP * k
                dve.wait_ge(S("taps"), k + 1)
                if k >= 2:
                    dve.wait_ge(S(f"toeplitz{k % 2}"), 16 * L * (k // 2))
                for g in range(BP):
                    ins = ve.tensor_copy(KP[k % 2][:, :, g, 112:240], PSUM[32 * g:32 * g + CH, 2 + 4 * (k % 2), 0:2 * P
                                                                           ].rearrange("p (w n) -> p w n", w=2))
                ch(ins)
                v = KP[k % 2][:, :, :, 112:128]
                ch(ve.tensor_tensor(v, v, DD[k % 2][:, :, g0:g0 + BP, :], ALU.add))
                dve.sem_inc(S("taps_ready"), 1)

            dve.wait_ge(S("stacked"), 1)
            decayed_c(0)
            decayed_c(1)
            taps_out(0)
            for k in range(1, NB):
                if k + 1 < NB:
                    decayed_c(k + 1)
                taps_out(k)
            end_phase(dve, 7)
            for n in range(2):
                for t in range(NT):
                    i = n * NT + t
                    r = ROWS[t]
                    dve.wait_ge(S("glu_gate"), i + 1)
                    dve.wait_ge(S("glu_added"), i)
                    ch(ve.tensor_tensor(GL_T[0:r, :], PSUM[0:r, 2 * (i % 2), :], GL_SG[0:r, i % 2, :], ALU.mult))
                    xv = X[0:r, t, n * 512:(n + 1) * 512]
                    ve.tensor_tensor(xv, xv, GL_T[0:r, :], ALU.add).then_inc(S("glu_added"), 1)
                    if n:
                        dve.wait_ge(S("glu_added"), i + 1)
                        dve.sem_inc(S("x_updated"), 1)
            end_phase(dve, 8)
            moe(1, 9)
            norm_dve(dve, ch, 4)

        @block.tensor
        def _(pe):
            te = nc.tensor

            def ring_wait(q):
                pe.wait_ge(S(f"ring_full{q % RS}"), full(q))

            for b in range(2):
                pe.sem_inc(S(f"xg_transposed{b}"), 1)
                pe.sem_inc(S(f"gate_up{b}"), 1)
            xt_pe(pe, 0)
            pe.wait_ge(S("consts_ready"), 1)
            for t in range(NT):
                r = ROWS[t]
                b0 = 3 * (t % 2)
                pe.wait_ge(S("xt_ready"), NT)
                if t >= 2:
                    pe.wait_ge(S("qkv_read"), t - 1)
                for n in range(3):
                    for c in range(KC):
                        if t == 0 and n == 0 and c % 2 == 0:
                            ring_wait(c // 2)
                        last = te.matmul(PSUM[0:r, b0 + n, :], XT[:, c, t * P:t * P + r],
                                         RING[:, c // 2, (c % 2) * QKV + n * 512:(c % 2) * QKV + (n + 1) * 512],
                                         start=(c == 0), stop=(c == KC - 1))
                last.then_inc(S("qkv_done"), 1)
                if t == NT - 1:
                    pe.wait_ge(S("qkv_done"), NT)
                    pe.sem_inc(S("ring_free"), 4)
                for tt in ([t - 1] if t else []) + ([t] if t == NT - 1 else []):
                    rr = ROWS[tt]
                    pe.wait_ge(S("rotated"), tt + 1)
                    if tt:
                        pe.wait_ge(S("kt_ready"), tt)
                    if tt < 4:
                        for c in range(KC):
                            last = te.transpose(PSUM[:, 6 + c // 4, (c % 4) * P:(c % 4 + 1) * P],
                                                QO[:, tt % 2, c * P:(c + 1) * P], IDENT[:, :])
                        last.then_inc(S("qk_transposed"), 1)
                        pe.wait_ge(S("qt_ready"), tt + 1)
                        for h in range(KVH):
                            last = te.transpose(PSUM[:, 6, h * P:(h + 1) * P], KD[:, tt % 2, h * P:(h + 1) * P], IDENT[:, :])
                        last.then_inc(S("k_transposed"), 1)
                    else:
                        for h in range(NH):
                            last = te.transpose(PSUM[0:64, 6 + h // 8, (h % 8) * 64:(h % 8 + 1) * 64],
                                                QO[0:64, tt % 2, h * 64:(h + 1) * 64], IDENT[0:64, 0:64])
                        last.then_inc(S("qk_transposed"), 1)
                        pe.wait_ge(S("qt_ready"), tt + 1)
                        for h in range(KVH):
                            last = te.transpose(PSUM[0:64, 6, h * 64:(h + 1) * 64],
                                                KD[0:64, tt % 2, h * P:h * P + 64], IDENT[0:64, 0:64])
                        last.then_inc(S("k_transposed"), 1)
            end_phase(pe, 1)
            pe.wait_ge(S("ck_in"), 16)
            for i in range(NSEQ):
                if i >= 2:
                    pe.wait_ge(S("kct_ready"), i - 1)
                for h in range(KVH):
                    last = te.transpose(PSUM[0:64, 4 + i % 2, h * P:(h + 1) * P], CK[:, i, h * 64:(h + 1) * 64], IDENT[:, :])
                last.then_inc(S("ck_transposed"), 1)
            pe.wait_ge(S("kct_ready"), NSEQ)
            pe.wait_ge(S("vc_in"), 16)

            def scores(i):
                kind, b, h = UNITS[i]
                if i >= 2:
                    pe.wait_ge(S("scores_shifted"), i - 1)
                b0 = 2 * (i % 2)
                if kind == "p":
                    w = width(UNITS[i])
                    k0 = (b - 1) * P if b else 0
                    for par in range(2):
                        for g in range(2):
                            c = (4 * h + 2 * g + par) // 2
                            last = te.matmul(PSUM[:, b0 + par, g * 256:g * 256 + w],
                                             QT[par * 64:par * 64 + 64, c, b * P:(b + 1) * P],
                                             KT[par * 64:par * 64 + 64, h, k0:k0 + w], start=True, stop=True)
                else:
                    for j in range(4):
                        sq = 4 * b + j
                        for hh in range(KVH):
                            lhs = QTS[:, sq, 32 * hh:32 * hh + 32]
                            out = PSUM[32 * hh:32 * hh + 32, b0 + j // 2, :]
                            o0 = (j % 2) * 256
                            te.matmul(out[:, o0:o0 + P], lhs, KCT[:, sq, hh, :], start=True, stop=True)
                            last = te.matmul(out[:, o0 + P:o0 + 192], lhs, KTS[:, hh, :], start=True, stop=True)
                last.then_inc(S("scores"), 1)

            def p_transpose(i):
                kind, b, h = UNITS[i]
                pe.wait_ge(S("probs"), i + 1)
                if i:
                    pe.wait_ge(S("pt_ready_dve"), i)
                    pe.wait_ge(S("pt_ready_act"), i)
                w = width(UNITS[i])
                sc = scores_sb(i, w)
                for g in range(4):
                    for hf in range((w + P - 1) // P):
                        n = min(P, w - hf * P)
                        last = te.transpose(PSUM[0:n, 4 + g // 2, ((g % 2) * 2 + hf) * P:((g % 2) * 2 + hf + 1) * P],
                                            sc[:, g, hf * P:hf * P + n], IDENT[:, :])
                last.then_inc(S("p_transposed"), 1)

            def pv(i):
                kind, b, h = UNITS[i]
                pe.wait_ge(S("pt_ready_dve"), i + 1)
                pe.wait_ge(S("pt_ready_act"), i + 1)
                if i:
                    pe.wait_ge(S("o_scaled"), i)
                pt = PT[:, i % 2, :].rearrange("p (g h q) -> p g h q", g=4, h=2)
                for g in range(4):
                    out = PSUM[:, 6, g * 64:(g + 1) * 64]
                    if kind == "p":
                        if b:
                            te.matmul(out, pt[:, g, 0, :], V[:, b - 1, h * 64:(h + 1) * 64], start=True, stop=False)
                            last = te.matmul(out, pt[:, g, 1, :], V[:, b, h * 64:(h + 1) * 64], start=False, stop=True)
                        else:
                            last = te.matmul(out, pt[:, g, 0, :], V[:, b, h * 64:(h + 1) * 64], start=True, stop=True)
                    else:
                        sq = 4 * b + g
                        for hh in range(KVH):
                            o = PSUM[32 * hh:32 * hh + 32, 6, g * 64:(g + 1) * 64]
                            te.matmul(o, pt[:, g, 0, 32 * hh:32 * hh + 32], VC[:, sq, hh * 64:(hh + 1) * 64],
                                      start=True, stop=False)
                            last = te.matmul(o, pt[0:64, g, 1, 32 * hh:32 * hh + 32], V[0:64, 4, hh * 64:(hh + 1) * 64],
                                             start=False, stop=True)
                last.then_inc(S("pv_done"), 1)
                if kind == "s":
                    pe.wait_ge(S("o_scaled"), i + 1)
                    for j in range(4):
                        last = te.transpose(PSUM[:, 7 if b == 0 else 0, j * P:(j + 1) * P],
                                            OD[:, j, :], IDENT[:, :])
                    last.then_inc(S("od_transposed"), 1)

            scores(0)
            for i in range(NU):
                if i + 1 < NU:
                    scores(i + 1)
                p_transpose(i)
                pv(i)
            end_phase(pe, 2)
            pe.wait_ge(S("ots_ready"), 2)
            for t in range(4):
                if t >= 2:
                    pe.wait_ge(S("ot_ready"), t - 1)
                for c in range(KC):
                    last = te.transpose(PSUM[:, 2 * (t % 2) + c // 4, (c % 4) * P:(c % 4 + 1) * P],
                                        O[:, t, c * P:(c + 1) * P], IDENT[:, :])
                last.then_inc(S("o_transposed"), 1)
            for t in range(NT):
                r = ROWS[t]
                if t < 4:
                    pe.wait_ge(S("ot_ready"), t + 1)
                else:
                    pe.wait_ge(S("ots_ready"), 2)
                if t >= 2:
                    pe.wait_ge(S("x_updated"), t - 1)
                for n in range(2):
                    for c in range(KC):
                        q = Q_WO + c // 3
                        if t == 0 and n == 0 and c % 3 == 0:
                            ring_wait(q)
                        last = te.matmul(PSUM[0:r, 4 + 2 * (t % 2) + n, :], OT[:, c, t * P:t * P + r],
                                         RING[:, q % RS, (c % 3) * D + n * 512:(c % 3) * D + (n + 1) * 512],
                                         start=(c == 0), stop=(c == KC - 1))
                last.then_inc(S("wo_done"), 1)
            pe.wait_ge(S("wo_done"), NT)
            pe.sem_inc(S("ring_free"), 3)
            end_phase(pe, 3)

            def moe(layer, ph):
                xt_pe(pe, 1 + 2 * layer)
                pe.wait_ge(S("router_in"), 64 * (layer + 1))
                pe.wait_ge(S("xt_ready"), TBASE[1 + 2 * layer] + NT)
                for t in range(NT):
                    for c in range(KC):
                        last = te.matmul(PSUM[0:ROWS[t], 4, t * 36:(t + 1) * 36], XT[:, c, t * P:t * P + ROWS[t]],
                                         WR[:, c, :], start=(c == 0), stop=(c == KC - 1))
                last.then_inc(S("logits"), 1)
                pe.wait_ge(S("chosen"), layer + 1)
                for t in range(NT + 1):
                    out = PSUM[:, 5, t * 32:(t + 1) * 32]
                    for j in range(min(t, NT)):
                        last = te.matmul(out, ONES[:, :], MM[:, j, :], start=(j == 0), stop=(t == NT and j == NT - 1))
                    if t < NT:
                        last = te.matmul(out, UPPER[:, :], MM[:, t, :], start=(t == 0), stop=True)
                last.then_inc(S("ranks"), 1)
                pe.wait_ge(S("onehots"), layer + 1)
                for i in range(2 * NT):
                    last = te.matmul(PSUM[:, 6, 0:NPAIR], R1[:, i // 2, i % 2, :], P1[:, i // 2, i % 2, :],
                                     start=(i == 0), stop=(i == 2 * NT - 1))
                last.then_inc(S("token_lists"), 1)
                pe.wait_ge(S("routed"), layer + 1)
                q0 = Q_M[layer]

                def gather_transposed(it, b):
                    done = it + ROUNDS * layer
                    pe.wait_ge(S(f"xg_full{b}"), it * 16 + 16 * (ROUNDS * layer + 1))
                    pe.wait_ge(S(f"xgt_ready{1 - b}"), done + (b + 1))
                    for c in range(KC):
                        last = te.transpose(PSUM[:, c // 4, (c % 4) * P:(c % 4 + 1) * P], XG[:, b, c * P:(c + 1) * P],
                                            IDENT[:, :])
                    last.then_inc(S(f"xg_transposed{b}"), 1)

                with pe.Fori(0, ROUNDS) as it:
                    for b in range(2):
                        done = it + ROUNDS * layer
                        gather_transposed(it, b)
                        pe.wait_ge(S(f"xgt_ready{b}"), done + 2)
                        for m in range(2):
                            pe.wait_ge(S(f"ring_full{(q0 + 2 * b + m) % RS}"), it * 48 + full(q0 + 2 * b + m))
                        for c in range(KC):
                            for m in range(2):
                                gu = RING[:, (q0 + 2 * b + m) % RS, 0:2 * D].rearrange("p (w c f) -> p w c f", w=2, c=KC)
                                last = te.matmul(PSUM[m * 64:(m + 1) * 64, 2 + b, 0:2 * FF],
                                                 XGT[:, b, c, m * 64:(m + 1) * 64], gu[:, :, c, :],
                                                 start=(c == 0), stop=(c == KC - 1))
                        last.then_inc(S(f"gate_up{b}"), 1)
                        pe.wait_ge(S(f"hidden_ready{b}"), done + 1)
                        te.transpose(PSUM[:, 2 + b, 256:256 + P], HTM[:, b, :], IDENT[:, :]
                                     ).then_inc(S(f"hidden_transposed{b}"), 1)
                        pe.wait_ge(S(f"hid_ready{b}"), done + 1)
                        pe.wait_ge(S(f"yb_dve{b}"), done + 1)
                        pe.wait_ge(S(f"yb_act{b}"), done + 1)
                        for n in range(2):
                            for m in range(2):
                                slot = (q0 + 2 * b + m) % RS
                                last = te.matmul(PSUM[m * 64:(m + 1) * 64, 4 + 2 * b + n, :], HID[:, b, m, :],
                                                 RING[:, slot, 2 * D + n * 512:2 * D + (n + 1) * 512], start=True, stop=True)
                        last.then_inc(S(f"expert_out{b}"), 1)
                        pe.wait_ge(S(f"expert_out{b}"), done + 1)
                        pe.sem_inc(S("ring_free"), 2)
                n = pe.value_load(OVR[0:1, layer, 0:1], min_val=0, max_val=OVP)
                before = pe.value_load(OVR[0:1, 0, 0:1], min_val=0, max_val=OVP) if layer else 0
                pe.sem_inc(S("ov_wfree"), 1)
                with pe.Fori(0, OVP) as j:
                    with pe.If(j < n):
                        pe.wait_ge(S("ov_x"), (before + j) * 16 + 16)
                        for c in range(KC):
                            last = te.transpose(PSUM[:, c // 4, (c % 4) * P:(c % 4 + 1) * P], XG[:, 0, c * P:(c + 1) * P],
                                                IDENT[:, :])
                        last.then_inc(S("ov_xt"), 1)
                        pe.wait_ge(S("ov_xgt"), before + (j + 1))
                        pe.wait_ge(S("ov_w"), (before + j) * 96 + 96)
                        areas = (XN.rearrange("p t d -> p (t d)"), XT.rearrange("p c t -> p (c t)"))
                        for c in range(KC):
                            for m in range(2):
                                gu = areas[m][:, 0:2 * D].rearrange("p (w c f) -> p w c f", w=2, c=KC)
                                last = te.matmul(PSUM[m * 64:(m + 1) * 64, 2, 0:2 * FF], XGT[:, 0, c, m * 64:(m + 1) * 64],
                                                 gu[:, :, c, :], start=(c == 0), stop=(c == KC - 1))
                        last.then_inc(S("ov_gu"), 1)
                        pe.wait_ge(S("ov_htm"), before + (j + 1))
                        te.transpose(PSUM[:, 2, 256:256 + P], HTM[:, 0, :], IDENT[:, :]).then_inc(S("ov_ht"), 1)
                        pe.wait_ge(S("ov_hid"), before + (j + 1))
                        for n_ in range(2):
                            for m in range(2):
                                last = te.matmul(PSUM[m * 64:(m + 1) * 64, 4 + n_, :], HID[:, 0, m, :],
                                                 areas[m][:, 2 * D + n_ * 512:2 * D + (n_ + 1) * 512], start=True, stop=True)
                        last.then_inc(S("ov_dn"), 1)
                end_phase(pe, ph)

            moe(0, 4)
            pe.wait_ge(S("par_done"), 1)
            for k in range(4):
                last = te.transpose(PSUM[:, 0, 32 * k:32 * k + 32], NAT[:, 12 + k, :], IDENT[0:32, 0:32])
            for w in range(2):
                last = te.transpose(PSUM[0:CH, 7, 32 * w:32 * w + 32], NAT[:, 23, CH * w:CH * w + CH], IDENT[0:32, 0:32])
            last.then_inc(S("par_transposed"), 1)
            pe.wait_ge(S("ssm_in"), 16 * 14)
            for r in range(2):
                for i in range(NSEQ):
                    last = te.transpose(PSUM[:, 1 + r, 32 * i:32 * i + 32], SIN_[:, r, i, :], IDENT[0:32, 0:32])
                last.then_inc(S("st_transposed"), 1)
            for r in range(2):
                for k in range(8):
                    last = te.transpose(PSUM[:, 3 + 2 * r + k // 4, (k % 4) * P:(k % 4 + 1) * P], CL[:, 8 * r + k, :], IDENT[:, :])
                last.then_inc(S("c_transposed"), 1)
            end_phase(pe, 5)
            pe.wait_ge(S("al_in"), 16 * NT)
            for k in range(NB):
                if k:
                    pe.wait_ge(S("u_ready"), k)
                pe.wait_ge(S("u_gathered"), k + 1)
                for g in range(8):
                    last = te.transpose(PSUM[:, g // 4, (g % 4) * NCH:(g % 4 + 1) * NCH],
                                        UA[:, k % 2, g].rearrange("p s c -> p (s c)"), IDENT[0:NCH, 0:NCH])
                last.then_inc(S("u_transposed"), 1)
                pe.wait_ge(S("w_ready"), k + 1)
                if k:
                    pe.wait_ge(S("wt_ready"), k)
                for r in range(2):
                    for g in range(BP):
                        last = te.transpose(PSUM[:, 2 + r, g * P:(g + 1) * P], WSB[:, r, g, :], IDENT[:, :])
                last.then_inc(S("w_transposed"), 1)
                pe.wait_ge(S("wt_ready"), k + 1)
                pe.wait_ge(S("u_ready"), k + 1)
                if k:
                    pe.wait_ge(S("g_ready"), k)
                for r in range(2):
                    for g in range(BP):
                        for w in range(2):
                            last = te.matmul(PSUM[64 * w:64 * w + 64, 4 + r, g * NCH:(g + 1) * NCH],
                                             WT[:, r, g, 64 * w:64 * w + 64], U[:, 2 * (BP * k + g) + w, :],
                                             start=True, stop=True)
                last.then_inc(S("g_done"), 1)
            pe.wait_ge(S("scanned"), 1)
            for r in range(2):
                last = te.transpose(PSUM[0:32, 0, r * P:(r + 1) * P], HF[:, r, :], IDENT[:, :])
            last.then_inc(S("hf_transposed"), 1)
            for r in range(2):
                for i in range(NSEQ):
                    last = te.transpose(PSUM[0:32, 2 + 2 * r + i // 4, (i % 4) * P:(i % 4 + 1) * P], HO[:, r, :, i], IDENT[:, :])
                last.then_inc(S("ho_transposed"), 1)
            end_phase(pe, 6)

            def taps(k):
                pe.wait_ge(S("v_ready"), k + 1)
                if k >= 2:
                    pe.wait_ge(S("taps_ready"), k - 1)
                for w in range(2):
                    for g in range(BP):
                        last = te.matmul(PSUM[32 * g:32 * g + CH, 2 + 4 * (k % 2), w * P:(w + 1) * P],
                                         BB[:, w, BP * k + g, :], VV[:, k % 3, w, g, 0:P], start=True, stop=True)
                last.then_inc(S("taps"), 1)

            pe.wait_ge(S("stacked"), 1)
            taps(0)
            taps(1)
            for k in range(NB):
                pe.wait_ge(S(f"toeplitz{k % 2}"), 16 * L * (k // 2 + 1))
                if k >= 2:
                    pe.wait_ge(S("z_ready"), k - 1)
                if k == 0:
                    pe.wait_ge(S("stacked"), 2)
                for g in range(BP):
                    for w in range(2):
                        pr = BP * k + g
                        out = PSUM[0:NCH, 4 * (k % 2) + w, g * P:(g + 1) * P]
                        te.matmul(out, H[:, w, pr, 0:NCH], VV[:, k % 3, w, g, CH:CH + P], start=True, stop=False)
                        last = te.matmul(out, U[:, 2 * pr + w, :], TT[:, k % 2, w, g, :], start=False, stop=True)
                last.then_inc(S("y_ssm"), 1)
                if k + 2 < NB:
                    taps(k + 2)
            pe.wait_ge(S("z_ready"), NB)
            for t in range(L):
                if t >= 2:
                    pe.wait_ge(S("zt_ready"), t - 1)
                for c in range(KC):
                    last = te.transpose(PSUM[:, 2 + 2 * (t % 2) + c // 4, (c % 4) * P:(c % 4) * P + NCH],
                                        Z[:, t, c * P:(c + 1) * P], IDENT[0:NCH, 0:NCH])
                last.then_inc(S("z_transposed"), 1)
            end_phase(pe, 7)
            for n in range(2):
                for t in range(NT):
                    i = n * NT + t
                    r = ROWS[t]
                    if i >= 2:
                        pe.wait_ge(S("glu_added"), i - 1)
                    for w in range(2):
                        for c in range(KC):
                            q = Q_GLU + 3 * n + c // 3
                            if t == 0 and w == 0 and c % 3 == 0:
                                ring_wait(q)
                            last = te.matmul(PSUM[0:r, 2 * (i % 2) + w, :], XT[:, c, t * P:t * P + r],
                                             RING[:, q % RS, (2 * (c % 3) + w) * 512:(2 * (c % 3) + w + 1) * 512],
                                             start=(c == 0), stop=(c == KC - 1))
                    last.then_inc(S("glu_done"), 1)
                pe.wait_ge(S("glu_done"), NT * (n + 1))
                pe.sem_inc(S("ring_free"), 3)
            end_phase(pe, 8)
            moe(1, 9)


_INS = ["x_prompt", "x_sample", "cache_k", "cache_v", "state_ssm_re", "state_ssm_im", "norm_mix", "norm_ffn",
        "norm_final", "attn_w_qkv", "attn_b_qkv", "attn_w_o", "attn_b_o", "attn_sinks", "ssm_a_re", "ssm_a_im",
        "ssm_log_dt", "ssm_b_re", "ssm_b_im", "ssm_c_re", "ssm_c_im", "ssm_d", "ssm_w_glu_a", "ssm_w_glu_b",
        "moe_w_router_group", "moe_b_router_group", "moe_w_router_expert", "moe_b_router_expert", "moe_w_gate",
        "moe_w_up", "moe_w_down"]
_OUTS = [(1, SEQ, D), (NSEQ, DSEQ, D), (1, 1, P, KVH, HD), (1, NSEQ, P, KVH, HD), (1, 1, P, KVH, HD),
         (1, NSEQ, P, KVH, HD), (1, 1, NGR, ST), (1, NSEQ, NGR, ST), (1, 1, NGR, ST), (1, NSEQ, NGR, ST)]


def rotary_table():
    pos = np.concatenate([np.arange(SEQ), np.tile(PAST + np.arange(DSEQ), NSEQ)]).astype(np.float32)
    half = HD // 2
    inv = (1.0 / (np.float32(10000.0) ** (np.arange(half, dtype=np.float32) * np.float32(2.0 / HD)))).astype(np.float32)
    ang = (pos[:, None] * inv[None, :]).astype(np.float32)
    return np.concatenate([np.cos(ang), np.sin(ang)], axis=1).astype(np.float32)


def kernel(**inputs):
    import concourse.bacc as bacc
    from concourse.bass_utils import run_bass_kernel_spmd

    nc = bacc.Bacc("TRN2", target_bir_lowering=False, num_devices=1)
    arrays, args = {}, []
    for name in _INS:
        arr = np.ascontiguousarray(inputs[name])
        arrays[f"in_{name}"] = arr
        args.append(nc.dram_tensor(f"in_{name}", arr.shape, mybir.dt.from_np(arr.dtype), kind="ExternalInput").ap())
    tab = rotary_table()
    arrays["in_rotary"] = tab
    args.append(nc.dram_tensor("in_rotary", tab.shape, FP, kind="ExternalInput").ap())
    for i, shape in enumerate(_OUTS):
        args.append(nc.dram_tensor(f"out_{i}", shape, FP, kind="ExternalOutput").ap())
    build(nc, *args)
    r = run_bass_kernel_spmd(nc, [arrays], core_ids=[0])
    return tuple(r.results[0][f"out_{i}"] for i in range(len(_OUTS)))
```

```python
import math
from contextlib import ExitStack

import numpy as np

import concourse.bass as bass
from concourse import mybir

FP = mybir.dt.float32
I32 = mybir.dt.int32
U32 = mybir.dt.uint32
ALU = mybir.AluOpType
ACT = mybir.ActivationFunctionType
AX = mybir.AxisListType

P = 128
D = 1024
SEQ = 512
NSEQ, DSEQ = 8, 8
NTOK = SEQ + NSEQ * DSEQ
NT = 5
ROWS = [P, P, P, P, NSEQ * DSEQ]
PAST = 2048
NH, KVH, HD = 16, 4, 64
GRP = NH // KVH
QD, KVD = NH * HD, KVH * HD
QKV = QD + 2 * KVD
NBLK = SEQ // P
SCALE = HD ** -0.5
BIG = 1.0e30
EPS = 1e-5
KC = D // P
NG, EPG = 4, 8
NE = NG * EPG
FF = 128
CAP = 64
PAIRS = NE // 2
ROUNDS = PAIRS // 2
OVT = (2 * NTOK - 1) // CAP
OVP = (OVT + 1) // 2
NPAIR = PAIRS + OVP
SLOTS = NPAIR * P
NGR, CH, ST = 64, 16, 64
GP = NGR // 2
L = 8
NCH = NTOK // L
PCH = SEQ // L
BP = 4
NB = GP // BP
RS = 4
RW = 3072


def bc(ap, shape):
    return ap.to_broadcast(shape)


def build(nc, x_prompt, x_sample, cache_k, cache_v, st_re, st_im, norm_mix, norm_ffn, norm_final,
          w_qkv, b_qkv, w_o, b_o, sinks, a_re, a_im, log_dt, b_re, b_im, c_re, c_im, ssm_d,
          w_ga, w_gb, w_rg, b_rg, w_re, b_re_r, w_gate, w_up, w_down, cs_tab,
          y_p, y_s, nk_p, nk_s, nv_p, nv_s, hr_p, hr_s, hi_p, hi_s):
    ctx = ExitStack()
    with ctx:
        def sem(name):
            return ctx.enter_context(nc.semaphore(name))

        def sb(name, shape, dt=FP):
            return ctx.enter_context(nc.sbuf_tensor(name, shape, dt))

        X = sb("X", [P, NT, D])
        XN = sb("XN", [P, NT, D])
        XT = sb("XT", [P, KC, NTOK])
        RING = sb("RING", [P, RS, RW])
        IDENT = sb("IDENT", [P, P])
        UPPER = sb("UPPER", [P, P])
        ONES = sb("ONES", [P, P])
        GAM = sb("GAM", [P, D])
        SS = sb("SS", [P, 5, NT])
        RSTD = sb("RSTD", [P, 5, NT])
        IOTA = sb("IOTA", [P, P])
        TOKID = sb("TOKID", [P, NT])
        PIDX = sb("PIDX", [P, 1], I32)
        PMOD = sb("PMOD", [P, 2])
        PMI = sb("PMI", [P, 2], I32)
        EPSC = sb("EPSC", [P, 1])
        OVR = sb("OVR", [P, 2, 1 + 2 * OVP], I32)
        PH_F = 24336
        PH = sb("PH", [P, PH_F])

        class Area:

            def __init__(self, base=0):
                self.at = base

            def take(self, n, parts=P):
                v = PH[0:parts, self.at:self.at + n]
                self.at += n
                assert self.at <= PH_F, self.at
                return v

        PSUM = ctx.enter_context(nc.psum_tensor("PSUM", [P, 8, 512], FP))

        def bank(i, n=1):
            return PSUM[:, i:i + n, :]

        xn_d = [nc.dram_tensor("xn_scratch", (NTOK, D), FP).ap()] * 2
        y_d = [nc.dram_tensor("y_scratch", (SLOTS, D), FP).ap()] * 2
        ZER = PH[:, PH_F - D:PH_F]
        IOI = ZER[:, 0:P].bitcast(I32)

        a = Area()
        QT = a.take(KC * SEQ).rearrange("p (c t) -> p c t", c=KC)
        QTS = a.take(NH * 64, 64).rearrange("p (s n) -> p s n", s=NSEQ)
        OT = PH[:, 0:KC * NTOK].rearrange("p (c t) -> p c t", c=KC)
        KT = a.take(KVH * SEQ).rearrange("p (h t) -> p h t", h=KVH)
        KTS = a.take(KVH * 64, 64).rearrange("p (h t) -> p h t", h=KVH)
        V = a.take(NT * KVD).rearrange("p (t n) -> p t n", t=NT)
        VC = a.take(NSEQ * KVD).rearrange("p (s n) -> p s n", s=NSEQ)
        BQKV = a.take(QKV)
        MPCUR = a.take(2 * P)
        MPREV, MCUR = MPCUR[:, 0:P], MPCUR[:, P:2 * P]
        MSC = a.take(P)
        MSN = a.take(120)
        SINK = a.take(NH)
        SINKS = a.take(1)
        SM = a.take(64)
        CS = a.take(NT * 64).rearrange("p (t n) -> p t n", t=NT)
        BO = a.take(D)
        at0 = a.at
        QR = a.take(QD + KVD)
        TA = a.take(QD + KVD)
        TB = a.take(QD + KVD)
        QO = a.take(2 * QD).rearrange("p (b n) -> p b n", b=2)
        KD = a.take(2 * 512).rearrange("p (b n) -> p b n", b=2)
        CK = a.take(NSEQ * KVD).rearrange("p (s n) -> p s n", s=NSEQ)
        assert a.at <= PH_F - D
        a.at = at0
        SB_ = a.take(2 * 1024).rearrange("p (b n) -> p b n", b=2)
        PT = a.take(2 * 1024).rearrange("p (b n) -> p b n", b=2)
        OD = CK[:, 0:4, 0:P]
        KCT = XT[0:64, :, :].rearrange("p c t -> p (c t)")[:, 0:NSEQ * KVH * P].rearrange(
            "p (s h k) -> p s h k", s=NSEQ, h=KVH)
        O = XN

        AT_BLOCKS = L * D + 2 * GP * (NCH + 1)
        AT_PARAMS = AT_BLOCKS + 6 * 2 * BP * P
        NAT_AT = AT_PARAMS - 24 * P - 2

        a = Area(PH_F - (KC + 1) * 36)
        WR = a.take(KC * 36).rearrange("p (c n) -> p c n", c=KC)
        BR = a.take(36)
        a = Area()
        LG = a.take(NT * 36).rearrange("p (t n) -> p t n", t=NT)
        GL8 = a.take(NT * 8).rearrange("p (t n) -> p t n", t=NT)
        GM8 = a.take(NT * 8).rearrange("p (t n) -> p t n", t=NT)
        GI8 = a.take(NT * 8).bitcast(U32).rearrange("p (t n) -> p t n", t=NT)
        GIF = a.take(NT)
        GOH = a.take(NT * 4).rearrange("p (t n) -> p t n", t=NT)
        GE = a.take(NT * 4).rearrange("p (t n) -> p t n", t=NT)
        GV = a.take(NT)
        EM = a.take(NT * 32).rearrange("p (t n) -> p t n", t=NT)
        EV8 = a.take(NT * 8).rearrange("p (t n) -> p t n", t=NT)
        EI8 = a.take(NT * 8).bitcast(U32).rearrange("p (t n) -> p t n", t=NT)
        EIF = a.take(NT * 2).rearrange("p (t n) -> p t n", t=NT)
        EX = a.take(NT)
        CW = a.take(NT * 2).rearrange("p (t n) -> p t n", t=NT)
        EOH = a.take(NT * 2 * 32).rearrange("p (t k n) -> p t k n", t=NT, k=2)
        ET = a.take(NT * 2 * 32).rearrange("p (t k n) -> p t k n", t=NT, k=2)
        MM = a.take(NT * 32).rearrange("p (t n) -> p t n", t=NT)
        RK = a.take(NT * 32).rearrange("p (t n) -> p t n", t=NT)
        CNT = a.take((NT + 1) * 32).rearrange("p (t n) -> p t n", t=NT + 1)
        OVN = a.take(32)
        OVI = a.take(32)
        OVE = a.take(32)
        OVM = a.take(32)
        RR = a.take(NT * 2).rearrange("p (t n) -> p t n", t=NT)
        OB = a.take(NT * 2).rearrange("p (t n) -> p t n", t=NT)
        SL = a.take(NT * 2).rearrange("p (t n) -> p t n", t=NT)
        SLI = a.take(NT * 2).bitcast(I32).rearrange("p (t n) -> p t n", t=NT)
        SMOD = a.take(NT * 2).rearrange("p (t n) -> p t n", t=NT)
        SDIV = a.take(NT * 2).rearrange("p (t n) -> p t n", t=NT)
        SMI = a.take(NT * 2).bitcast(I32).rearrange("p (t n) -> p t n", t=NT)
        SDI = a.take(NT * 2).bitcast(I32).rearrange("p (t n) -> p t n", t=NT)
        OVNI = a.take(32).bitcast(I32)
        R1 = a.take(NT * 2 * P).rearrange("p (t k n) -> p t k n", t=NT, k=2)
        P1 = a.take(NT * 2 * NPAIR).rearrange("p (t k n) -> p t k n", t=NT, k=2)
        IDX = a.take(NPAIR).bitcast(I32)
        IDXB = a.take(2).bitcast(I32)
        EIDT = a.take(2 * OVP * 32).rearrange("p (j n) -> p j n", n=32)
        EIDF = a.take(2 * OVP)
        NPF = a.take(2)
        XG = a.take(2 * D).rearrange("p (b n) -> p b n", b=2)
        XGT = a.take(2 * D).rearrange("p (b c t) -> p b c t", b=2, c=KC)
        SG = a.take(2 * FF).rearrange("p (b f) -> p b f", b=2)
        HTM = a.take(2 * FF).rearrange("p (b f) -> p b f", b=2)
        HID = a.take(2 * P).rearrange("p (b m t) -> p b m t", b=2, m=2)
        YB = a.take(2 * D).rearrange("p (b n) -> p b n", b=2)
        YG0 = a.take(4 * D).rearrange("p (b n) -> p b n", b=4)
        assert a.at <= NAT_AT
        XTF = XT.rearrange("p c t -> p (c t)")
        YG1 = XTF[:, 0:4 * D].rearrange("p (b n) -> p b n", b=4)
        YG = [(YG0 if t < 2 else YG1)[:, 2 * (t % 2):2 * (t % 2) + 2, :] for t in range(4)]

        a = Area()
        AL = a.take(L * D, NCH).rearrange("p (s d) -> p s d", s=L)
        Z = AL
        H = a.take(2 * GP * (NCH + 1)).rearrange("p (r g c) -> p r g c", r=2, g=GP)
        U = XN.rearrange("p t d -> p (t d)")[:, 0:NGR * NCH].rearrange("p (g c) -> p g c", g=NGR)
        G = XT.rearrange("p c t -> p (c t)")[:, 0:2 * GP * NCH].rearrange("p (r g c) -> p r g c", r=2, g=GP)
        at1 = a.at
        assert at1 == AT_BLOCKS
        a.at = AT_PARAMS
        BB = a.take(2 * GP * CH).rearrange("p (r g c) -> p r g c", r=2, g=GP)
        CT = a.take(2 * GP * CH).rearrange("p (r g c) -> p r g c", r=2, g=GP)
        PW = a.take(2 * 9 * GP).rearrange("p (r k g) -> p r k g", r=2, k=9)
        PWR = a.take(2 * 8 * GP).rearrange("p (r k g) -> p r k g", r=2, k=8)
        CC = a.take(4 * GP).rearrange("p (a x g) -> p a x g", a=2, x=2)
        CC2 = a.take(4 * GP).rearrange("p (a x g) -> p a x g", a=2, x=2)
        CF = a.take(2 * GP).rearrange("p (r g) -> p r g", r=2)
        HO = a.take(2 * GP * NSEQ).rearrange("p (r g s) -> p r g s", r=2, g=GP)
        HF = a.take(2 * GP).rearrange("p (r g) -> p r g", r=2)
        PR = a.take(4 * GP).rearrange("p (a x g) -> p a x g", a=2, x=2)
        QQ = a.take(2 * GP).rearrange("p (r g) -> p r g", r=2)
        DCOL = a.take(2 * GP, CH).rearrange("p (w g) -> p w g", w=2)
        EYE = a.take(CH, CH)
        DD2 = a.take(2 * GP * CH, 32 + CH).rearrange("p (w g c) -> p w g c", w=2, g=GP)
        DD = [DD2[32 * b:32 * b + CH] for b in range(2)]
        a.at = NAT_AT
        NAT = a.take(24 * P, 32).rearrange("p (k n) -> p k n", k=24)
        DT2 = a.take(2, 32)
        SCR4 = XG.rearrange("p b n -> p (b n)").rearrange("p (k g c) -> p k g c", k=4, g=GP)
        CL = XTF[:, 0:16 * P].rearrange("p (k n) -> p k n", k=16)
        SIN_ = XTF[0:32, 16 * P:(16 + 2 * NSEQ) * P].rearrange("p (r s n) -> p r s n", r=2, s=NSEQ)
        a.at = at1
        WSB = a.take(2 * 2 * BP * P).rearrange("p (b r g n) -> p b r g n", b=2, r=2, g=BP)
        WT = a.take(2 * BP * P).rearrange("p (r g n) -> p r g n", r=2, g=BP)
        TMPW = a.take(BP * P)
        TMPX = a.take(BP * P)
        a.at = at1
        VV = a.take(3 * 2 * BP * 144).rearrange("p (b w g n) -> p b w g n", b=3, w=2, g=BP)
        TT = a.take(2 * 2 * BP * P).rearrange("p (b w g n) -> p b w g n", b=2, w=2, g=BP)
        A1S = a.take(2 * 9 * GP).rearrange("p (w k g) -> p w k g", w=2, k=9)
        A2S = PW
        B1S = GAM[:, 0:2 * GP * CH].rearrange("p (w g c) -> p w g c", w=2, g=GP)
        B2S = CT
        BSWAP = XN.rearrange("p t d -> p (t d)")[64:P, NGR * NCH:NGR * NCH + GP * CH].rearrange(
            "p (g c) -> p g c", g=GP)
        KP = [XTF[32 * b:32 * b + CH, 0:2 * BP * 240].rearrange("p (w g n) -> p w g n", w=2, g=BP) for b in range(2)]
        HSWAP = XTF[64:P, 0:GP * NCH].rearrange("p (g c) -> p g c", g=GP)
        TMPV = XTF[:, GP * NCH:GP * NCH + 2 * BP * 144]
        a.at = at1 + 4 * 2 * BP * P
        UA = a.take(2 * 8 * L * CH, NCH).rearrange("p (b g s c) -> p b g s c", b=2, g=8, s=L)
        SOUT = PH[96:P, 0:2 * P]
        SOUTS = PH[96:P, 2 * P:2 * P + 2 * NSEQ * P].rearrange("p (r n) -> p r n", r=2)
        GL_SG = PH[:, 0:2 * 512].rearrange("p (b n) -> p b n", b=2)
        GL_T = PH[:, 1024:1024 + 512]

        s = {}

        def S(name):
            if name not in s:
                s[name] = sem(name)
            return s[name]

        phase = S("phase_done")
        NENG = 4

        def end_phase(eng, n):
            eng.drain().then_inc(phase, 1)
            eng.wait_ge(phase, NENG * n)

        class Chain:

            def __init__(self, eng, name):
                self.eng, self.sem, self.n = eng, S(name), 0

            def __call__(self, ins):
                self.n += 1
                ins.then_inc(self.sem, 1)
                self.eng.wait_ge(self.sem, self.n)

        LOADS = [1] * 4 + [1] * 3 + [3] * NE + [2] * 6 + [3] * NE
        Q_QKV, Q_WO, Q_M0, Q_GLU, Q_M1 = 0, 4, 7, 7 + NE, 13 + NE

        def full(q):
            return 16 * sum(LOADS[j] for j in range(q % RS, q + 1, RS))

        Q_M = [Q_M0, Q_M1]

        SHIFTS = {"act": range(0, 2), "sp": range(2, 5), "pool": range(5, L)}

        def toeplitz(eng, k, queue):
            eng.wait_ge(S("taps_ready"), k + 1)
            if k >= 2:
                eng.wait_ge(S("y_ssm"), k - 1)
            for sh in SHIFTS[queue]:
                eng.dma_start(TT[CH * sh:CH * sh + CH, k % 2].rearrange("p w g n -> p (w g) n"),
                              KP[k % 2][:, :, :, 112 - CH * sh:240 - CH * sh].rearrange("p w g n -> p (w g) n")
                              ).then_inc(S(f"toeplitz{'_sw' if queue == 'pool' else ''}{k % 2}"), 16)

        def toeplitz_wait(eng, k):
            sw = len(SHIFTS["pool"])
            eng.wait_ge(S(f"toeplitz{k % 2}"), 16 * (L - sw) * (k // 2 + 1))
            eng.wait_ge(S(f"toeplitz_sw{k % 2}"), 16 * sw * (k // 2 + 1))

        block = ctx.enter_context(nc.Block())

        @block.sync
        def _(sp):
            for t in range(4):
                sp.dma_start(X[:, t, :], x_prompt[0, t * P:(t + 1) * P, :]).then_inc(S(f"x_in{t}"), 16)
            sp.dma_start(X[0:64, 4, :], x_sample.rearrange("b t d -> (b t) d")).then_inc(S("x_in4"), 16)

            def ring_load(q, pieces):
                if q >= RS:
                    sp.wait_ge(S("ring_free"), q - RS + 1)
                assert len(pieces) == LOADS[q]
                for dst, src in pieces:
                    sp.dma_start(dst, src).then_inc(S(f"ring_full{q % RS}"), 16)

            for j in range(4):
                ring_load(Q_QKV + j, [(RING[:, j, :].rearrange("p (k n) -> p k n", k=2),
                                       w_qkv[0, 2 * j * P:(2 * j + 2) * P, :].rearrange("(k p) n -> p k n", p=P))])
            for j, k in enumerate([3, 3, 2]):
                q = Q_WO + j
                ring_load(q, [(RING[:, q % RS, 0:k * D].rearrange("p (k n) -> p k n", k=k),
                               w_o[0, 3 * j * P:(3 * j + k) * P, :].rearrange("(k p) n -> p k n", p=P))])

            sp.wait_ge(S("rotated"), 5)
            for i in range(NSEQ):
                sp.dma_start(nk_s[0, i, P - DSEQ:P, :, :],
                              KD[8 * i:8 * i + 8, 0, :].rearrange("p (h w d) -> p h w d", h=KVH, w=2)[:, :, 0, :]
                              ).then_inc(S("win_out"), 16)
                sp.dma_start(nv_s[0, i, P - DSEQ:P, :, :].rearrange("r h d -> r (h d)"),
                              V[8 * i:8 * i + 8, 4, :]).then_inc(S("win_out"), 16)

            def experts(layer):
                q0 = Q_M[layer]
                with sp.Fori(0, NE // RS) as it:
                    for j in range(RS):
                        slot = (q0 + j) % RS
                        sp.wait_ge(S("ring_free"), it * RS + (q0 + j - RS + 1))
                        for i, src in enumerate((w_gate, w_up)):
                            sp.dma_start(RING[:, slot, i * D:(i + 1) * D].rearrange("p (c f) -> p c f", c=KC),
                                         src[layer, bass.ds(it * RS + j, 1), :, :].rearrange("o (p c) f -> p (o c) f", p=P)
                                         ).then_inc(S(f"ring_full{slot}"), 16)
                        sp.dma_start(RING[:, slot, 2 * D:3 * D],
                                     w_down[layer, bass.ds(it * RS + j, 1), :, :].rearrange("o f d -> f (o d)")
                                     ).then_inc(S(f"ring_full{slot}"), 16)

            def overflow(layer):
                sp.wait_ge(S("routed"), layer + 1)
                sp.wait_ge(S(f"xn_stored{layer}"), 16 * NT)
                n = sp.value_load(OVR[0:1, layer, 0:1], min_val=0, max_val=OVP)
                before = sp.value_load(OVR[0:1, 0, 0:1], min_val=0, max_val=OVP) if layer else 0
                with sp.If(n > 0):
                    with sp.Fori(0, OVP) as j:
                        with sp.If(j < n):
                            sp.wait_ge(S("ov_wfree"), before + j + (layer + 1))
                            for m, area in enumerate((XN.rearrange("p t d -> p (t d)"), XT.rearrange("p c t -> p (c t)"))):
                                e = sp.value_load(OVR[0:1, layer, bass.ds(2 * j + m + 1, 1)], min_val=0, max_val=NE - 1)
                                for i, src in enumerate((w_gate, w_up)):
                                    sp.dma_start(area[:, i * D:(i + 1) * D].rearrange("p (c f) -> p c f", c=KC),
                                                 src[layer, bass.ds(e, 1), :, :].rearrange("o (p c) f -> p (o c) f", p=P)
                                                 ).then_inc(S("ov_w"), 16)
                                sp.dma_start(area[:, 2 * D:3 * D],
                                             w_down[layer, bass.ds(e, 1), :, :].rearrange("o f d -> f (o d)")
                                             ).then_inc(S("ov_w"), 16)

            experts(0)
            overflow(0)
            sp.wait_ge(S("al_in"), 16 * NT)
            sp.wait_ge(S("ssm_in"), 16 * 6)
            for n in range(2):
                for j, k in enumerate([3, 3, 2]):
                    q = Q_GLU + 3 * n + j
                    if q == Q_GLU + RS:
                        for k_ in range(NB):
                            toeplitz(sp, k_, "sp")
                    view = RING[:, q % RS, 0:k * D].rearrange("p (k w n) -> p k w n", k=k, w=2)
                    ring_load(q, [(view[:, :, w, :],
                                   src[0, 3 * j * P:(3 * j + k) * P, n * 512:(n + 1) * 512].rearrange(
                                       "(k p) n -> p k n", p=P)) for w, src in enumerate((w_ga, w_gb))])
            experts(1)
            overflow(1)
            for t in range(NT):
                sp.wait_ge(S("xn_done"), 4 * NT + t + 1)
                dst = y_p[0, t * P:(t + 1) * P, :] if t < 4 else y_s.rearrange("b t d -> (b t) d")
                sp.dma_start(dst, XN[0:ROWS[t], t, :]).then_inc(S("y_out"), 16)
            sp.wait_ge(S("y_out"), 16 * NT)

        @block.gpsimd
        def _(pool):
            ch = Chain(pool, "pool_chain")
            pool.memset(EPSC[:, :], EPS).then_inc(S("eps_ready"), 1)
            pool.memset(IDENT[:, :], 0.0)
            pool.memset(UPPER[:, :], 1.0)
            pool.memset(MPREV, 0.0)
            pool.memset(MCUR, 0.0)
            ch(pool.memset(ONES[:, :], 1.0))
            pool.affine_select(out=IDENT[:, :], in_=IDENT[:, :], compare_op=ALU.not_equal, fill=1.0, base=0,
                               pattern=[[-1, P]], channel_multiplier=1).then_inc(S("ident_ready"), 1)
            pool.affine_select(out=UPPER[:, :], in_=UPPER[:, :], compare_op=ALU.is_ge, fill=0.0, base=-1,
                               pattern=[[1, P]], channel_multiplier=-1)
            pool.affine_select(out=MPREV, in_=MPREV, compare_op=ALU.is_ge, fill=-BIG, base=0,
                               pattern=[[1, P]], channel_multiplier=-1)
            pool.affine_select(out=MCUR, in_=MCUR, compare_op=ALU.is_ge, fill=-BIG, base=0,
                               pattern=[[-1, P]], channel_multiplier=1)
            ch(pool.iota(IOI[:, :], pattern=[[1, P]], base=0, channel_multiplier=0))
            ch(pool.tensor_copy(IOTA[:, :], IOI[:, :]))
            ch(pool.iota(PIDX[:, :], pattern=[[0, 1]], base=0, channel_multiplier=1))
            ch(pool.iota(IOI[:, 0:NT], pattern=[[P, NT]], base=0, channel_multiplier=1))
            ch(pool.tensor_copy(TOKID[:, :], IOI[:, 0:NT]))
            ch(pool.memset(TOKID[64:P, 4:5], 0.0))
            pool.sem_inc(S("consts_ready"), 1)
            end_phase(pool, 1)
            ch(pool.memset(ZER, 0.0))
            for i in range(OVP):
                pool.dma_start(y_d[0][(PAIRS + i) * P:(PAIRS + i + 1) * P, :], ZER).then_inc(S("zeros_out"), 16)
            pool.wait_ge(S("zeros_out"), 16 * OVP)
            end_phase(pool, 2)
            end_phase(pool, 3)

            def moe(layer, ph):
                pool.wait_ge(S("routed"), layer + 1)
                pool.wait_ge(S(f"xn_stored{layer}"), 16 * NT)
                with pool.Fori(0, ROUNDS) as it:
                    for b in range(2):
                        pool.wait_ge(S(f"xg_transposed{b}"), it + (ROUNDS * layer + 1))
                        pool.tensor_copy(IDXB[:, b:b + 1], IDX[:, bass.ds(2 * it + b, 1)]).then_inc(S(f"idx_ready{b}"), 1)
                        pool.wait_ge(S(f"idx_ready{b}"), it + (ROUNDS * layer + 1))
                        pool.sem_inc(S("gathers"), 1)
                        pool.indirect_dma_start(
                            out=XG[:, b, :], out_offset=None, in_=xn_d[layer],
                            in_offset=bass.IndirectOffsetOnAxis(ap=IDXB[:, b:b + 1], axis=0),
                        ).then_inc(S(f"xg_full{b}"), 16)
                n = pool.value_load(OVR[0:1, layer, 0:1], min_val=0, max_val=OVP)
                before = pool.value_load(OVR[0:1, 0, 0:1], min_val=0, max_val=OVP) if layer else 0
                with pool.If(n > 0):
                    with pool.Fori(0, OVP) as j:
                        with pool.If(j < n):
                            pool.wait_ge(S("ov_wfree"), before + j + (layer + 1))
                            pool.tensor_copy(IDXB[:, 0:1], IDX[:, bass.ds(j + PAIRS, 1)]).then_inc(S("ov_idx"), 1)
                            pool.wait_ge(S("ov_idx"), before + (j + 1))
                            pool.sem_inc(S("gathers"), 1)
                            pool.indirect_dma_start(
                                out=XG[:, 0, :], out_offset=None, in_=xn_d[layer],
                                in_offset=bass.IndirectOffsetOnAxis(ap=IDXB[:, 0:1], axis=0),
                            ).then_inc(S("ov_x"), 16)
                pool.wait_ge(S("all_stored"), layer + 1)
                for t in range(NT):
                    if t >= 4:
                        pool.wait_ge(S("yg_used"), layer * 2 * NT + 2 * (t - 3))
                    for k in range(2):
                        pool.indirect_dma_start(
                            out=YG[t % 4][0:ROWS[t], k, :], out_offset=None, in_=y_d[layer],
                            in_offset=bass.IndirectOffsetOnAxis(ap=SLI[0:ROWS[t], t, k:k + 1], axis=0),
                        ).then_inc(S(f"yg_full{t % 4}"), 16)
                end_phase(pool, ph)

            moe(0, 4)
            pool.wait_ge(S("al_in"), 16 * NT)
            for k in range(NB):
                if k >= 2:
                    pool.wait_ge(S("u_transposed"), k - 1)
                pool.tensor_copy(UA[:, k % 2], AL[:, :, 8 * CH * k:8 * CH * (k + 1)].rearrange(
                    "p s (g c) -> p g s c", g=8)).then_inc(S("u_gathered"), 1)
                if k == 1:
                    end_phase(pool, 5)
            end_phase(pool, 6)
            for k in range(NB):
                toeplitz(pool, k, "pool")
            end_phase(pool, 7)
            end_phase(pool, 8)
            moe(1, 9)

        def norm_act(act, n, t):
            if n == 0:
                act.wait_ge(S(f"x_in{t}"), 16)
            else:
                act.wait_ge(S("x_updated"), NT * (n - 1) + t + 1)
            r = ROWS[t]
            nc.scalar.activation(XN[0:r, t, :], X[0:r, t, :], ACT.Square,
                                 accum_out=SS[0:r, n, t:t + 1]).then_inc(S("squares"), 1)
            act.wait_ge(S("squares"), NT * n + t + 1)
            nc.scalar.activation(RSTD[0:r, n, t:t + 1], SS[0:r, n, t:t + 1], ACT.Sqrt, bias=EPSC[0:r, :],
                                 scale=1.0 / D).then_inc(S("roots"), 1)

        TBASE = {0: 0, 1: NT, 3: 2 * NT}
        XT_BANKS = {0: (0, 2), 1: (0,), 3: (4,)}
        LOGIT_BANK = [2, 6]

        def xt_bank(n, t):
            return XT_BANKS[n][t % len(XT_BANKS[n])]

        def xt_act(act, n, t):
            act.wait_ge(S("x_transposed"), TBASE[n] + t + 1)
            r = ROWS[t]
            nc.scalar.activation(XT[:, :, t * P:t * P + r], bank(xt_bank(n, t), 2).rearrange(
                "p b (c t) -> p (b c) t", c=4)[:, :, 0:r], ACT.Copy).then_inc(S("xt_ready"), 1)

        def norm_dve(dve, ch, n, t):
            dve.wait_ge(S("roots"), NT * n + t + 1)
            r = ROWS[t]
            ch(nc.vector.reciprocal(RSTD[0:r, n, t:t + 1], RSTD[0:r, n, t:t + 1]))
            if t == 0:
                dve.wait_ge(S("gamma_in"), 16 * (n + 1))
            nc.vector.scalar_tensor_tensor(out=XN[0:r, t, :], in0=X[0:r, t, :], scalar=RSTD[0:r, n, t:t + 1],
                                           in1=GAM[0:r, :], op0=ALU.mult, op1=ALU.mult).then_inc(S("xn_done"), 1)

        def xt_pe(pe, n, t):
            pe.wait_ge(S("xn_done"), NT * n + t + 1)
            if n == 0 and t == 0:
                pe.wait_ge(S("ident_ready"), 1)
            k = len(XT_BANKS[n])
            if t >= k:
                pe.wait_ge(S("xt_ready"), TBASE[n] + t - k + 1)
            r = ROWS[t]
            for c in range(KC):
                last = nc.tensor.transpose(PSUM[:, xt_bank(n, t) + c // 4, (c % 4) * P:(c % 4) * P + r],
                                           XN[0:r, t, c * P:(c + 1) * P], IDENT[0:r, 0:r])
            last.then_inc(S("x_transposed"), 1)

        def logits_pe(pe, layer, t):
            if t == 0:
                pe.wait_ge(S("router_in"), 64 * (layer + 1))
            pe.wait_ge(S("xt_ready"), TBASE[1 + 2 * layer] + t + 1)
            for c in range(KC):
                last = nc.tensor.matmul(PSUM[0:ROWS[t], LOGIT_BANK[layer], t * 36:(t + 1) * 36],
                                        XT[:, c, t * P:t * P + ROWS[t]], WR[:, c, :], start=(c == 0), stop=(c == KC - 1))
            if t == NT - 1:
                last.then_inc(S("logits"), 1)

        def router_load(act, layer):
            act.dma_start(WR[:, :, 0:4], w_rg[layer].rearrange("(c p) n -> p c n", p=P)).then_inc(S("router_in"), 16)
            act.dma_start(WR[:, :, 4:36], w_re[layer].rearrange("(c p) n -> p c n", p=P)).then_inc(S("router_in"), 16)
            act.dma_start(BR[:, 0:4], b_rg[layer:layer + 1, :].to_broadcast([P, 4])).then_inc(S("router_in"), 16)
            act.dma_start(BR[:, 4:36], b_re_r[layer:layer + 1, :].to_broadcast([P, 32])).then_inc(S("router_in"), 16)

        def xt_and_store(act, layer, t):
            xt_act(act, 1 + 2 * layer, t)
            act.dma_start(xn_d[layer][t * P:t * P + ROWS[t], :], XN[0:ROWS[t], t, :]
                          ).then_inc(S(f"xn_stored{layer}"), 16)

        def gamma_load(act, n):
            src = [norm_mix[0:1, :], norm_ffn[0:1, :], norm_mix[1:2, :], norm_ffn[1:2, :],
                   norm_final.rearrange("(o d) -> o d", o=1)][n]
            if n:
                act.wait_ge(S("xn_done"), NT * n)
            act.dma_start(GAM[:, :], src.to_broadcast([P, D])).then_inc(S("gamma_in"), 16)

        UNITS = [("p", b, h) for b in range(NBLK) for h in range(KVH)] + [("s", 0, 0), ("s", 1, 0)]
        NU = len(UNITS)

        def width(u):
            kind, b, _ = u
            return 192 if kind == "s" else (P if b == 0 else 2 * P)

        def scores_ps(i, w):
            return bank(2 * (i % 2), 2).rearrange("p b (g k) -> p (b g) k", g=2)[:, :, 0:w]

        def scores_sb(i, w):
            return SB_[:, i % 2, :].rearrange("p (g k) -> p g k", g=4)[:, :, 0:w]

        @block.scalar
        def _(act):
            ch = Chain(act, "act_chain")
            for b in range(2):
                act.sem_inc(S(f"xgt_ready{b}"), 1)
                act.sem_inc(S(f"yb_act{b}"), 1)
                act.sem_inc(S(f"y_stored{b}"), 16)
            gamma_load(act, 0)
            act.wait_ge(S("eps_ready"), 1)
            for t in range(NT):
                norm_act(act, 0, t)
            for t in range(NT):
                xt_act(act, 0, t)
                if t == 1:
                    act.dma_start(BQKV, b_qkv[0:1, :].to_broadcast([P, QKV])).then_inc(S("att_in"), 16)
                    act.dma_start(CS[:, 0:4, :], cs_tab[0:SEQ, :].rearrange("(t p) n -> p t n", p=P)).then_inc(S("att_in"), 16)
                    act.dma_start(CS[0:64, 4, :], cs_tab[SEQ:NTOK, :]).then_inc(S("att_in"), 16)
                    act.dma_start(SINK, sinks[0:1, :].to_broadcast([P, NH])).then_inc(S("att_in"), 16)
                    act.dma_start(SINKS, sinks.rearrange("o (h u) -> (o h) u", u=1).unsqueeze(1).to_broadcast([NH, 8, 1])
                                  ).then_inc(S("att_in"), 16)
                    act.dma_start(BO, b_o[0:1, :].to_broadcast([P, D])).then_inc(S("att_in"), 16)
            gamma_load(act, 1)
            act.wait_ge(S("qkv_done"), 1)
            act.dma_start(VC, cache_v[0].rearrange("s r h d -> r s (h d)")).then_inc(S("vc_in"), 16)
            act.dma_start(CK, cache_k[0].rearrange("s r h d -> r s (h d)")).then_inc(S("ck_in"), 16)
            act.dma_start(nk_s[0, :, 0:P - DSEQ, :, :].rearrange("s r h d -> s r (h d)"),
                          cache_k[0, :, DSEQ:P, :, :].rearrange("s r h d -> s r (h d)")).then_inc(S("win_out"), 16)
            act.dma_start(nv_s[0, :, 0:P - DSEQ, :, :].rearrange("s r h d -> s r (h d)"),
                          cache_v[0, :, DSEQ:P, :, :].rearrange("s r h d -> s r (h d)")).then_inc(S("win_out"), 16)
            for t in range(NT):
                act.wait_ge(S("qk_transposed"), t + 1)
                if t < 4:
                    nc.scalar.activation(QT[:, 0:4, t * P:(t + 1) * P], PSUM[:, 6, :].rearrange("p (c t) -> p c t", c=4),
                                         ACT.Copy)
                    nc.scalar.activation(QT[:, 4:8, t * P:(t + 1) * P], PSUM[:, 7, :].rearrange("p (c t) -> p c t", c=4),
                                         ACT.Copy).then_inc(S("qt_ready"), 1)
                    act.wait_ge(S("k_transposed"), t + 1)
                    nc.scalar.activation(KT[:, :, t * P:(t + 1) * P], PSUM[:, 6, :].rearrange("p (c t) -> p c t", c=4),
                                         ACT.Copy).then_inc(S("kt_ready"), 1)
                else:
                    nc.scalar.activation(QTS.rearrange("p s (h t) -> p h s t", h=NH),
                                         PSUM[0:64, 6:8, :].rearrange("p b (c s t) -> p (b c) s t", s=NSEQ, t=DSEQ),
                                         ACT.Copy).then_inc(S("qt_ready"), 1)
                    act.wait_ge(S("k_transposed"), t + 1)
                    nc.scalar.activation(KTS, PSUM[0:64, 6, 0:256].rearrange("p (c t) -> p c t", t=64),
                                         ACT.Copy).then_inc(S("kt_ready"), 1)
                if t == 3:
                    act.wait_ge(S("rotated"), 4)
                    act.dma_start(nk_p[0, 0].rearrange("r h d -> r h d"),
                                  KD[:, 1, :].rearrange("p (h w d) -> p h w d", h=KVH, w=2)[:, :, 0, :]
                                  ).then_inc(S("win_out"), 16)
                    act.dma_start(nv_p[0, 0].rearrange("r h d -> r (h d)"), V[:, 3, :]).then_inc(S("win_out"), 16)
            end_phase(act, 1)
            for i in range(NSEQ):
                act.wait_ge(S("ck_transposed"), i + 1)
                nc.scalar.activation(KCT[:, i, :, :], PSUM[0:64, 4 + i % 2, :].rearrange("p (h k) -> p h k", h=KVH),
                                     ACT.Copy).then_inc(S("kct_ready"), 1)

            def exps(i):
                act.wait_ge(S("scores_masked"), i + 1)
                sc = scores_sb(i, width(UNITS[i]))
                par = 4 * (i % 2)
                nc.scalar.activation(SM[:, 48 + par:52 + par], SM[:, 8 + par:12 + par], ACT.Exp)
                for g in range(4):
                    ins = nc.scalar.activation(sc[:, g, :], sc[:, g, :], ACT.Exp, bias=SM[:, 36 + par + g:37 + par + g],
                                               accum_out=SM[:, 16 + par + g:17 + par + g])
                ins.then_inc(S("probs"), 1)

            def pt_evac(i):
                act.wait_ge(S("p_transposed"), i + 1)
                if i >= 2:
                    act.wait_ge(S("pv_done"), i - 1)
                if UNITS[i][0] == "p" and UNITS[i][1] == 0:
                    nc.scalar.activation(PT[:, i % 2, 512:1024].rearrange("p (g h q) -> p g h q", g=2, h=2)[:, :, 0, :],
                                         PSUM[:, 5, :].rearrange("p (g h q) -> p g h q", g=2, h=2)[:, :, 0, :],
                                         ACT.Copy).then_inc(S("pt_ready_act"), 1)
                elif UNITS[i][0] == "p":
                    nc.scalar.activation(PT[:, i % 2, 512:1024], PSUM[:, 5, :], ACT.Copy).then_inc(S("pt_ready_act"), 1)
                else:
                    v = PT[:, i % 2, 512:1024].rearrange("p (g h q) -> p g h q", g=2, h=2)
                    ps = PSUM[:, 5, :].rearrange("p (g h q) -> p g h q", g=2, h=2)
                    nc.scalar.activation(v[:, :, 0, :], ps[:, :, 0, :], ACT.Copy)
                    nc.scalar.activation(v[0:64, :, 1, :], ps[0:64, :, 1, :], ACT.Copy).then_inc(S("pt_ready_act"), 1)

            exps(0)
            for i in range(NU):
                pt_evac(i)
                if i + 1 < NU:
                    exps(i + 1)
            act.wait_ge(S("win_out"), 16 * (4 + 2 * NSEQ))
            end_phase(act, 2)
            router_load(act, 0)
            for t in range(4):
                act.wait_ge(S("o_transposed"), t + 1)
                nc.scalar.activation(OT[:, :, t * P:(t + 1) * P], bank(2 * (t % 2), 2).rearrange(
                    "p b (c t) -> p (b c) t", c=4), ACT.Copy).then_inc(S("ot_ready"), 1)
            for t in range(NT):
                norm_act(act, 1, t)
                if t:
                    xt_and_store(act, 0, t - 1)
            xt_and_store(act, 0, NT - 1)
            end_phase(act, 3)

            def parameter_loads():
                for k, src in enumerate((a_re, a_im)):
                    act.dma_start(NAT[:, k, :], src[0].rearrange("(g w) p -> g (w p)", w=2)).then_inc(S("par_in"), 16)
                act.dma_start(DT2, log_dt[0].rearrange("(g w) -> g w", w=2)).then_inc(S("par_in"), 16)
                for r, src in enumerate((b_re, b_im)):
                    for w in range(2):
                        act.dma_start(BB[64 * w:64 * w + 64, r, :, :],
                                      src[0].rearrange("(g w) p c -> w p g c", w=2)[w]).then_inc(S("par_in"), 16)
                act.dma_start(NAT[:, 23, 0:32], ssm_d[0].rearrange("(g q) -> g q", q=32)).then_inc(S("par_in"), 16)

            def delta():
                act.wait_ge(S("par_in"), 16 * 8)
                nc.scalar.activation(DT2, DT2, ACT.Exp).then_inc(S("delta"), 1)

            def parameters():
                act.wait_ge(S("angles"), 1)
                nc.scalar.activation(NAT[:, 4, :], NAT[:, 4, :], ACT.Exp)
                nc.scalar.activation(NAT[:, 7, :], NAT[:, 6, :], ACT.Sin)
                nc.scalar.activation(NAT[:, 9, :], NAT[:, 8, :], ACT.Sin).then_inc(S("trig"), 1)
                act.wait_ge(S("par_transposed"), 1)
                nc.scalar.activation(DCOL, PSUM[0:CH, 1, 0:64].rearrange("p (w g) -> p w g", w=2), ACT.Copy)
                nc.scalar.activation(PW[:, :, 1, :], PSUM[:, 0, 0:64].rearrange("p (r g) -> p r g", r=2), ACT.Copy)
                nc.scalar.activation(CF, PSUM[:, 0, 64:128].rearrange("p (r g) -> p r g", r=2), ACT.Copy).then_inc(S("par_ready"), 1)

            def moe(layer, ph):
                gamma_load(act, 2 + 2 * layer)
                if layer == 0:
                    parameter_loads()
                act.wait_ge(S("group_shifted"), layer + 1)
                nc.scalar.activation(GE, GE, ACT.Exp).then_inc(S("group_exp"), 1)
                act.wait_ge(S("expert_shifted"), layer + 1)
                nc.scalar.activation(EX, EX, ACT.Exp).then_inc(S("expert_exp"), 1)
                act.wait_ge(S("routed"), layer + 1)

                def tokens_out(it, b):
                    done = it + ROUNDS * layer
                    act.wait_ge(S(f"xg_transposed{b}"), done + 2)
                    act.wait_ge(S(f"gate_up{b}"), done + 1)
                    nc.scalar.activation(XGT[:, b, :, :], bank(0, 2).rearrange("p b (c t) -> p (b c) t", c=4),
                                         ACT.Copy).then_inc(S(f"xgt_ready{b}"), 1)

                def pair(it, b, last_pair=False):
                    done = it + ROUNDS * layer
                    act.wait_ge(S(f"gate_up{b}"), done + 2)
                    nc.scalar.activation(SG[:, b, :], PSUM[:, 2 + b, 0:FF], ACT.Silu).then_inc(S(f"silu_ready{b}"), 1)
                    if not last_pair:
                        tokens_out(it + b, 1 - b)
                    act.wait_ge(S(f"expert_out{b}"), done + 1)
                    act.wait_ge(S(f"y_stored{b}"), it * 16 + 16 * (ROUNDS * layer + 1))
                    nc.scalar.activation(YB[:, b, 512:1024], PSUM[:, 4 + 2 * b + 1, :], ACT.Copy
                                         ).then_inc(S(f"yb_act{b}"), 1)
                    act.wait_ge(S(f"yb_act{b}"), done + 2)
                    act.wait_ge(S(f"yb_dve{b}"), done + 2)
                    act.dma_start(y_d[layer][bass.ds(it * (2 * P) + b * P, P), :] if not isinstance(it, int)
                                  else y_d[layer][(2 * it + b) * P:(2 * it + b + 1) * P, :], YB[:, b, :]
                                  ).then_inc(S(f"y_stored{b}"), 16)

                tokens_out(0, 0)
                with act.Fori(0, ROUNDS - 1) as it:
                    for b in range(2):
                        pair(it, b)
                pair(ROUNDS - 1, 0)
                pair(ROUNDS - 1, 1, last_pair=True)
                if layer == 0:
                    delta()
                n = act.value_load(OVR[0:1, layer, 0:1], min_val=0, max_val=OVP)
                before = act.value_load(OVR[0:1, 0, 0:1], min_val=0, max_val=OVP) if layer else 0
                for b in range(2):
                    act.wait_ge(S(f"y_stored{b}"), 16 * (ROUNDS * (layer + 1) + 1))
                with act.If(n > 0):
                    with act.Fori(0, OVP) as j:
                        with act.If(j < n):
                            act.wait_ge(S("ov_xt"), before + (j + 1))
                            nc.scalar.activation(XGT[:, 0, :, :], bank(0, 2).rearrange("p b (c t) -> p (b c) t", c=4),
                                                 ACT.Copy).then_inc(S("ov_xgt"), 1)
                            act.wait_ge(S("ov_gu"), before + (j + 1))
                            nc.scalar.activation(SG[:, 0, :], PSUM[:, 2, 0:FF], ACT.Silu).then_inc(S("ov_silu"), 1)
                            act.wait_ge(S("ov_dn"), before + (j + 1))
                            nc.scalar.activation(YB[:, 0, :], bank(4, 2).rearrange("p b n -> p (b n)"), ACT.Copy
                                                 ).then_inc(S("ov_yb"), 1)
                            act.wait_ge(S("ov_yb"), before + (j + 1))
                            act.dma_start(y_d[layer][bass.ds((j + PAIRS) * P, P), :], YB[:, 0, :]
                                          ).then_inc(S("ov_y"), 16)
                            act.wait_ge(S("ov_y"), (before + j) * 16 + 16)
                            act.sem_inc(S("ov_wfree"), 1)
                act.sem_inc(S("all_stored"), 1)
                if layer == 0:
                    parameters()
                for t in range(NT):
                    norm_act(act, 2 + 2 * layer, t)
                end_phase(act, ph)

            moe(0, 4)
            for t in range(NT):
                act.wait_ge(S("xn_done"), 2 * NT + t + 1)
                n = ROWS[t] // L
                act.dma_start(AL[t * 16:t * 16 + n, :, :].rearrange("c s d -> c s d"),
                              XN[0:ROWS[t], t, :]).then_inc(S("al_in"), 16)
            for r, src in enumerate((c_re, c_im)):
                for w in range(2):
                    act.dma_start(CL[:, 8 * r:8 * r + 8, 64 * w:64 * w + 64],
                                  src[0].rearrange("(k g) c p -> (g c) k p", g=8)).then_inc(S("ssm_in"), 16)
            for r, src in enumerate((st_re, st_im)):
                act.dma_start(SIN_[:, r, :, :], src[0].rearrange("s (g w) p -> g s (w p)", w=2)).then_inc(S("ssm_in"), 16)
            for r in range(2):
                act.wait_ge(S("st_transposed"), r + 1)
                nc.scalar.activation(H[:, r, :, PCH:NCH].rearrange("p g s -> p s g"),
                                     PSUM[:, 1 + r, 0:256].rearrange("p (s g) -> p s g", s=NSEQ), ACT.Copy
                                     ).then_inc(S("state_ready"), 1)
            for r in range(2):
                act.wait_ge(S("c_transposed"), r + 1)
                for w in range(2):
                    nc.scalar.activation(CT[64 * w:64 * w + 64, r, :, :],
                                         bank(3 + 2 * r, 2).rearrange("p b (g w c) -> p (b g) w c", w=2, c=CH)[
                                             64 * w:64 * w + 64, :, w, :], ACT.Copy).then_inc(S("c_ready"), 1)
            end_phase(act, 5)
            lo, hi = slice(0, 64), slice(64, P)
            for w, src in enumerate((lo, hi)):
                nc.scalar.activation(B1S[lo, w], CT[src, 0], ACT.Copy)
                ins = nc.scalar.activation(B1S[hi, w], CT[src, 1], ACT.Copy)
            ch(ins)
            for w in range(2):
                nc.scalar.activation(B2S[lo, w], B1S[hi, w], ACT.Copy)
                ins = nc.scalar.activation(B2S[hi, w], B1S[lo, w], ACT.Copy, scale=-1.0)
            ch(ins)
            for k in range(NB):
                act.wait_ge(S("w_transposed"), k + 1)
                if k:
                    act.wait_ge(S("g_done"), k)
                nc.scalar.activation(WT.rearrange("p r g n -> p r (g n)"), bank(2, 2), ACT.Copy).then_inc(S("wt_ready"), 1)
                act.wait_ge(S("u_transposed"), k + 1)
                nc.scalar.activation(U[:, 8 * k:8 * k + 8, :].rearrange("p (b g) c -> p b g c", b=2),
                                     PSUM[:, 0:2, 0:4 * NCH].rearrange("p b (g c) -> p b g c", g=4), ACT.Copy
                                     ).then_inc(S("u_ready"), 1)
                act.wait_ge(S("g_done"), k + 1)
                nc.scalar.activation(G[:, :, BP * k:BP * k + BP, :],
                                     PSUM[:, 4:6, 0:BP * NCH].rearrange("p r (g c) -> p r g c", g=BP), ACT.Copy
                                     ).then_inc(S("g_ready"), 1)
            for w, src in enumerate((lo, hi)):
                for half in (lo, hi):
                    ins = nc.scalar.activation(A1S[half, w], PW[src, 0], ACT.Copy)
            ch(ins)
            nc.scalar.activation(A2S[lo, 0], PW[lo, 1], ACT.Copy)
            ch(nc.scalar.activation(A2S[hi, 0], PW[lo, 1], ACT.Copy))
            ch(nc.scalar.activation(A2S[lo, 1], PW[hi, 1], ACT.Copy))
            act.wait_ge(S("w_ready"), NB)
            ch(nc.scalar.activation(BSWAP, BB[lo, 1], ACT.Copy))
            ch(nc.scalar.activation(BB[lo, 1], BB[hi, 0], ACT.Copy))
            nc.scalar.activation(BB[hi, 0], BSWAP, ACT.Copy).then_inc(S("stacked"), 1)
            act.wait_ge(S("hf_transposed"), 1)
            nc.scalar.activation(SOUT[:, 0:2 * P], PSUM[0:32, 0, 0:2 * P], ACT.Copy).then_inc(S("hf_copied"), 1)
            for r in range(2):
                act.wait_ge(S("ho_transposed"), r + 1)
                nc.scalar.activation(SOUTS[:, r].rearrange("p (b n) -> p b n", b=2),
                                     PSUM[0:32, 2 + 2 * r:4 + 2 * r, :], ACT.Copy).then_inc(S("ho_copied"), 1)
            end_phase(act, 6)
            ch(nc.scalar.activation(HSWAP, H[lo, 1, :, 0:NCH], ACT.Copy))
            ch(nc.scalar.activation(H[lo, 1, :, 0:NCH], H[hi, 0, :, 0:NCH], ACT.Copy))
            nc.scalar.activation(H[hi, 0, :, 0:NCH], HSWAP, ACT.Copy).then_inc(S("stacked"), 1)
            toeplitz(act, 0, "act")
            for k in range(NB):
                if k + 1 < NB:
                    toeplitz(act, k + 1, "act")
                act.wait_ge(S("y_ssm"), k + 1)
                for w in range(2):
                    zv = Z.rearrange("p t (g w c) -> p g w t c", w=2, c=CH)[:, BP * k:BP * k + BP, w, :, :]
                    ins = nc.scalar.activation(zv, PSUM[0:NCH, 4 * (k % 2) + w, :].rearrange(
                        "p (g t c) -> p g t c", g=BP, c=CH), ACT.Gelu_apprx_tanh)
                ins.then_inc(S("z_ready"), 1)
            act.wait_ge(S("hf_copied"), 1)
            act.wait_ge(S("ho_copied"), 2)
            act.dma_start(hr_p[0, 0].rearrange("(g w) p -> g (w p)", w=2), SOUT[:, 0:P]).then_inc(S("h_out"), 16)
            act.dma_start(hi_p[0, 0].rearrange("(g w) p -> g (w p)", w=2), SOUT[:, P:2 * P]).then_inc(S("h_out"), 16)
            for r, dst in enumerate((hr_s, hi_s)):
                act.dma_start(dst[0].rearrange("s (g w) p -> g s (w p)", w=2),
                              SOUTS[:, r].rearrange("p (s n) -> p s n", s=NSEQ)).then_inc(S("h_out"), 16)
            for t in range(L):
                act.wait_ge(S("z_transposed"), t + 1)
                nc.scalar.activation(
                    XT.rearrange("p c (n t) -> p c n t", t=L)[:, :, :, t],
                    PSUM[:, 2 + 2 * (t % 2):4 + 2 * (t % 2), :].rearrange("p b (c n) -> p (b c) n", c=4)[:, :, 0:NCH],
                    ACT.Copy).then_inc(S("zt_ready"), 1)
            act.wait_ge(S("h_out"), 16 * 4)
            end_phase(act, 7)
            gamma_load(act, 3)
            router_load(act, 1)
            for n in range(2):
                for t in range(NT):
                    i = n * NT + t
                    act.wait_ge(S("glu_done"), i + 1)
                    if i >= 2:
                        act.wait_ge(S("glu_added"), i - 1)
                    p0 = 64 if t == 4 else 0
                    nc.scalar.activation(GL_SG[0:ROWS[t], i % 2, :], PSUM[p0:p0 + ROWS[t], 2 * (i % 2) + 1, :], ACT.Sigmoid
                                         ).then_inc(S("glu_gate"), 1)
                    if n:
                        norm_act(act, 3, t)
                        if t:
                            xt_and_store(act, 1, t - 1)
            xt_and_store(act, 1, NT - 1)
            end_phase(act, 8)
            moe(1, 9)

        @block.vector
        def _(dve):
            ch = Chain(dve, "dve_chain")
            ve = nc.vector
            for b in range(2):
                dve.sem_inc(S(f"yb_dve{b}"), 1)
            for t in range(NT):
                norm_dve(dve, ch, 0, t)
            dve.wait_ge(S("consts_ready"), 1)
            ve.tensor_scalar(PMI[:, 0:1], PIDX[:, :], DSEQ - 1, None, ALU.bitwise_and)
            ch(ve.tensor_scalar(PMI[:, 1:2], PIDX[:, :], CH - 1, None, ALU.bitwise_and))
            ch(ve.tensor_copy(PMOD[:, :], PMI[:, :]))
            ch(ve.tensor_scalar(MSC, IOTA[:, :], PMOD[:, 0:1], -BIG, ALU.is_lt, ALU.mult))
            ch(ve.tensor_scalar(SM[:, 61:62], PMOD[:, 0:1], 56.0, None, ALU.add))
            ch(ve.tensor_scalar(MSN, IOTA[:, 0:120], SM[:, 61:62], -BIG, ALU.is_gt, ALU.mult))
            ch(ve.tensor_scalar(QR[:, 0:120], IOTA[:, 0:120], 56.0, -BIG, ALU.is_lt, ALU.mult))
            ch(ve.tensor_tensor(MSN, MSN, QR[:, 0:120], ALU.add))
            dve.wait_ge(S("att_in"), 16 * 6)
            for t in range(NT):
                r = ROWS[t]
                b0 = 3 * (t % 2)
                dve.wait_ge(S("qkv_done"), t + 1)
                if t < 4:
                    ve.tensor_tensor(QR[:, 0:1024], bank(b0, 2).rearrange("p b n -> p (b n)"), BQKV[:, 0:1024], ALU.add)
                    ve.tensor_tensor(QR[:, 1024:1280], PSUM[:, b0 + 2, 0:256], BQKV[:, 1024:1280], ALU.add)
                    ch(ve.tensor_tensor(V[:, t, :], PSUM[:, b0 + 2, 256:512], BQKV[:, 1280:1536], ALU.add))
                else:
                    lo, hi = slice(0, 64), slice(64, P)
                    ve.tensor_tensor(QR[lo, 0:512], PSUM[lo, b0, :], BQKV[lo, 0:512], ALU.add)
                    ve.tensor_tensor(QR[lo, 512:1024], PSUM[hi, b0 + 1, :], BQKV[hi, 512:1024], ALU.add)
                    ve.tensor_tensor(QR[lo, 1024:1280], PSUM[lo, b0 + 2, 0:256], BQKV[lo, 1024:1280], ALU.add)
                    ch(ve.tensor_tensor(V[lo, t, :], PSUM[hi, b0 + 2, 256:512], BQKV[hi, 1280:1536], ALU.add))
                q4 = QR[0:r, :].rearrange("p (h w d) -> p h w d", w=2, d=32)
                cos = CS[0:r, t, 0:32].unsqueeze(1).unsqueeze(1)
                sin = CS[0:r, t, 32:64].unsqueeze(1)
                ta = TA[0:r, :].rearrange("p (h w d) -> p h w d", w=2, d=32)
                tb = TB[0:r, :].rearrange("p (h w d) -> p h w d", w=2, d=32)
                ve.tensor_tensor(ta, q4, bc(cos, [r, 20, 2, 32]), ALU.mult).then_inc(S("qkv_read"), 1)
                ve.tensor_tensor(tb[:, :, 0, :], q4[:, :, 1, :], bc(sin, [r, 20, 32]), ALU.mult)
                ch(ve.tensor_tensor(tb[:, :, 1, :], q4[:, :, 0, :], bc(sin, [r, 20, 32]), ALU.mult))
                if t >= 2:
                    dve.wait_ge(S("k_transposed"), t - 1)
                qo = QO[0:r, t % 2, :].rearrange("p (h w d) -> p h w d", w=2, d=32)
                kd = KD[0:r, t % 2, :].rearrange("p (h e w d) -> p h e w d", e=2, w=2, d=32)
                ve.tensor_tensor(qo[:, :, 0, :], ta[:, 0:16, 0, :], tb[:, 0:16, 0, :], ALU.subtract)
                ve.tensor_tensor(qo[:, :, 1, :], ta[:, 0:16, 1, :], tb[:, 0:16, 1, :], ALU.add)
                for e in range(2):
                    ve.tensor_tensor(kd[:, :, e, 0, :], ta[:, 16:20, 0, :], tb[:, 16:20, 0, :], ALU.subtract)
                    last = ve.tensor_tensor(kd[:, :, e, 1, :], ta[:, 16:20, 1, :], tb[:, 16:20, 1, :], ALU.add)
                last.then_inc(S("rotated"), 1)
            end_phase(dve, 1)

            def sink_of(i):
                kind, b, h = UNITS[i]
                if kind == "s":
                    return bc(SINKS, [P, 4])
                return SINK[:, 4 * h:4 * h + 4].rearrange("p (g w) -> p w g", w=2)

            def scale_mask(i):
                par = 4 * (i % 2)
                kind, b, h = UNITS[i]
                w = width(UNITS[i])
                dve.wait_ge(S("scores"), i + 1)
                ps, sc = scores_ps(i, w), scores_sb(i, w)
                if kind == "p" and b == 0:
                    ch(ve.scalar_tensor_tensor(out=sc, in0=ps, scalar=SCALE, in1=bc(MCUR.unsqueeze(1), [P, 4, P]),
                                               op0=ALU.mult, op1=ALU.add))
                elif kind == "p":
                    m = MPCUR.unsqueeze(1)
                    ch(ve.scalar_tensor_tensor(out=sc, in0=ps, scalar=SCALE, in1=bc(m, [P, 4, 2 * P]),
                                               op0=ALU.mult, op1=ALU.add))
                else:
                    ve.scalar_tensor_tensor(out=sc[:, :, 0:P], in0=ps[:, :, 0:P], scalar=SCALE,
                                            in1=bc(MSC.unsqueeze(1), [P, 4, P]), op0=ALU.mult, op1=ALU.add)
                    for j in range(4):
                        off = 56 - 8 * (4 * b + j)
                        ins = ve.scalar_tensor_tensor(out=sc[:, j, P:192], in0=ps[:, j, P:192], scalar=SCALE,
                                                      in1=MSN[:, off:off + 64], op0=ALU.mult, op1=ALU.add)
                    ch(ins)
                ch(ve.tensor_reduce(SM[:, 0:4], sc, AX.X, ALU.max))
                ch(ve.tensor_tensor(SM[:, 4:8], SM[:, 0:4], sink_of(i), ALU.max))
                ve.tensor_tensor(SM[:, 8 + par:12 + par], sink_of(i), SM[:, 4:8], ALU.subtract)
                ve.tensor_scalar(SM[:, 36 + par:40 + par], SM[:, 4:8], -1.0, None, ALU.mult).then_inc(S("scores_masked"), 1)

            def denominators(i):
                par = 4 * (i % 2)
                dve.wait_ge(S("probs"), i + 1)
                if i:
                    dve.wait_ge(S("denominator"), i)
                ch(ve.tensor_tensor(SM[:, 32:36], SM[:, 16 + par:20 + par], SM[:, 48 + par:52 + par], ALU.add))
                ve.reciprocal(SM[:, 24 + par:28 + par], SM[:, 32:36]).then_inc(S("denominator"), 1)

            def pt_evac(i):
                dve.wait_ge(S("p_transposed"), i + 1)
                v = PT[:, i % 2, 0:512].rearrange("p (g h q) -> p g h q", g=2, h=2)
                ps = PSUM[:, 4, :].rearrange("p (g h q) -> p g h q", g=2, h=2)
                if UNITS[i][0] == "p" and UNITS[i][1] == 0:
                    ve.tensor_copy(v[:, :, 0, :], ps[:, :, 0, :]).then_inc(S("pt_ready_dve"), 1)
                elif UNITS[i][0] == "p":
                    ve.tensor_copy(PT[:, i % 2, 0:512], PSUM[:, 4, :]).then_inc(S("pt_ready_dve"), 1)
                else:
                    ve.tensor_copy(v[:, :, 0, :], ps[:, :, 0, :])
                    ve.tensor_copy(v[0:64, :, 1, :], ps[0:64, :, 1, :]).then_inc(S("pt_ready_dve"), 1)

            def out_scale(i):
                kind, b, h = UNITS[i]
                dve.wait_ge(S("pv_done"), i + 1)
                dve.wait_ge(S("denominator"), i + 1)
                rd = SM[:, 24 + 4 * (i % 2):28 + 4 * (i % 2)].unsqueeze(2)
                ps = PSUM[:, 6 + i % 2, 0:256].rearrange("p (g d) -> p g d", g=4)
                if kind == "p":
                    o = O[:, b, h * 256:(h + 1) * 256].rearrange("p (g w d) -> p w g d", g=2, w=2)
                    ve.tensor_tensor(o, ps.rearrange("p (w g) d -> p w g d", w=2),
                                     bc(rd, [P, 4, HD]).rearrange("p (w g) d -> p w g d", w=2), ALU.mult).then_inc(S("o_scaled"), 1)
                else:
                    if b:
                        dve.wait_ge(S("od_transposed"), 1)
                    for e in range(2):
                        ins = ve.tensor_tensor(OD[:, :, e * 64:(e + 1) * 64], ps, bc(rd, [P, 4, HD]), ALU.mult)
                    ins.then_inc(S("o_scaled"), 1)

            def od_evac(b):
                dve.wait_ge(S("od_transposed"), b + 1)
                ps = PSUM[:, b, :].rearrange("p (s h t) -> p s h t", s=4, h=NH)
                for w in range(2):
                    for j in range(4):
                        col = SEQ + (4 * b + j) * 8
                        ins = ve.tensor_copy(OT[64 * w:64 * w + 64, :, col:col + 8],
                                             ps[64 * w:64 * w + 64, j, :, :].rearrange("p (c w) t -> p c w t", w=2)[:, :, w, :])
                ins.then_inc(S("ots_ready"), 1)

            scale_mask(0)
            for i in range(NU):
                if i + 1 < NU:
                    scale_mask(i + 1)
                pt_evac(i)
                denominators(i)
                if i:
                    out_scale(i - 1)
            out_scale(NU - 1)
            end_phase(dve, 2)
            od_evac(0)
            od_evac(1)
            for t in range(NT):
                r = ROWS[t]
                dve.wait_ge(S("wo_done"), t + 1)
                b0 = 4 + 2 * (t % 2)
                ch(ve.tensor_tensor(X[0:r, t, :], X[0:r, t, :], BO[0:r, :], ALU.add))
                if t < 4:
                    ins = ve.tensor_tensor(X[:, t, :], X[:, t, :], bank(b0, 2).rearrange("p b n -> p (b n)"), ALU.add)
                else:
                    for n in range(2):
                        xv = X[0:64, t, n * 512:(n + 1) * 512]
                        ins = ve.tensor_tensor(xv, xv, PSUM[64 * n:64 * n + 64, b0 + n, :], ALU.add)
                ins.then_inc(S("x_updated"), 1)
                norm_dve(dve, ch, 1, t)
            end_phase(dve, 3)

            def cmul(o, x, y, t1, t2, sub_im=False):
                ve.tensor_tensor(t1, x[0], y[0], ALU.mult)
                ch(ve.tensor_tensor(t2, x[1], y[1], ALU.mult))
                ch(ve.tensor_tensor(o[0], t1, t2, ALU.subtract))
                ve.tensor_tensor(t1, x[0], y[1], ALU.mult)
                ch(ve.tensor_tensor(t2, x[1], y[0], ALU.mult))
                ch(ve.tensor_tensor(o[1], t1, t2, ALU.add))

            def parameters():
                N = [NAT[:, k, :] for k in range(24)]
                TWO_PI = 2 * math.pi
                C1 = 6.28125
                C2 = TWO_PI - C1
                MAGIC = 12582912.0
                dve.wait_ge(S("delta"), 1)
                dt_b = bc(DT2.unsqueeze(2), [32, 2, 64])
                n3 = lambda v: v.rearrange("p (w q) -> p w q", w=2)
                ch(ve.tensor_tensor(n3(N[4]), n3(N[0]), dt_b, ALU.mult))
                ch(ve.tensor_tensor(n3(N[5]), n3(N[1]), dt_b, ALU.mult))
                ch(ve.tensor_scalar(N[10], N[5], 1.0 / TWO_PI, None, ALU.mult))
                ch(ve.tensor_scalar(N[10], N[10], MAGIC, None, ALU.add))
                ch(ve.tensor_scalar(N[10], N[10], MAGIC, None, ALU.subtract))
                ch(ve.scalar_tensor_tensor(out=N[6], in0=N[10], scalar=-C1, in1=N[5], op0=ALU.mult, op1=ALU.add))
                ch(ve.scalar_tensor_tensor(out=N[6], in0=N[10], scalar=-C2, in1=N[6], op0=ALU.mult, op1=ALU.add))
                ch(ve.tensor_scalar(N[6], N[6], 3.1415925, -3.1415925, ALU.min, ALU.max))
                ch(ve.tensor_scalar(N[8], N[6], -1.0, None, ALU.mult))
                ch(ve.tensor_tensor(N[8], N[8], N[6], ALU.max))
                ch(ve.tensor_scalar(N[8], N[8], -1.0, math.pi / 2, ALU.mult, ALU.add))
                dve.sem_inc(S("angles"), 1)
                dve.wait_ge(S("trig"), 1)
                ve.tensor_tensor(N[12], N[4], N[9], ALU.mult)
                ch(ve.tensor_tensor(N[13], N[4], N[7], ALU.mult))
                ch(ve.tensor_scalar(N[11], N[12], -1.0, None, ALU.add))
                ve.tensor_tensor(N[16], N[0], N[0], ALU.mult)
                ch(ve.tensor_tensor(N[17], N[1], N[1], ALU.mult))
                ch(ve.tensor_tensor(N[16], N[16], N[17], ALU.add))
                ch(ve.reciprocal(N[18], N[16]))
                ve.tensor_tensor(N[19], N[11], N[0], ALU.mult)
                ch(ve.tensor_tensor(N[20], N[13], N[1], ALU.mult))
                ch(ve.tensor_tensor(N[19], N[19], N[20], ALU.add))
                ch(ve.tensor_tensor(N[14], N[19], N[18], ALU.mult))
                ve.tensor_tensor(N[21], N[13], N[0], ALU.mult)
                ch(ve.tensor_tensor(N[22], N[11], N[1], ALU.mult))
                ch(ve.tensor_tensor(N[21], N[21], N[22], ALU.subtract))
                ch(ve.tensor_tensor(N[15], N[21], N[18], ALU.mult))
                dve.sem_inc(S("par_done"), 1)
                dve.wait_ge(S("par_ready"), 1)
                ve.memset(PW[:, 0, 0, :], 1.0)
                ch(ve.memset(PW[:, 1, 0, :], 0.0))

                for lo, hi, by in ((1, 2, 1), (1, 3, 2), (1, 5, 4)):
                    n = hi - lo
                    x = [PW[:, r, lo:hi, :] for r in range(2)]
                    y = [bc(PW[:, r, by:by + 1, :], [P, n, GP]) for r in range(2)]
                    o = [PW[:, r, lo + by:hi + by, :] for r in range(2)]
                    t1 = CC.rearrange("p a x g -> p (a x) g")[:, 0:n, :]
                    t2 = PR.rearrange("p a x g -> p (a x) g")[:, 0:n, :]
                    cmul(o, x, y, t1, t2)
                for k in range(8):
                    ve.tensor_copy(PWR[:, :, k, :], PW[:, :, 7 - k, :])
                p16 = [PR[:, 1, r, :] for r in range(2)]
                cmul(p16, [PW[:, r, 8, :] for r in range(2)], [PW[:, r, 8, :] for r in range(2)],
                     PR[:, 0, 0, :], PR[:, 0, 1, :])
                for m, (re, im) in ((CC, (PW[:, 0, 8, :], PW[:, 1, 8, :])), (CC2, p16)):
                    ve.tensor_copy(m[:, 0, 0, :], re)
                    ve.tensor_copy(m[:, 1, 1, :], re)
                    ve.tensor_copy(m[:, 1, 0, :], im)
                    ins = ve.tensor_scalar(m[:, 0, 1, :], im, -1.0, None, ALU.mult)
                ch(ins)
                cf = [bc(CF[:, r, :].unsqueeze(2), [P, GP, CH]) for r in range(2)]
                bb = [BB[:, r, :, :] for r in range(2)]
                for k, (i, j) in enumerate(((0, 0), (1, 1), (0, 1), (1, 0))):
                    ins = ve.tensor_tensor(SCR4[:, k], cf[i], bb[j], ALU.mult)
                ch(ins)
                ve.tensor_tensor(bb[0], SCR4[:, 0], SCR4[:, 1], ALU.subtract)
                ch(ve.tensor_tensor(bb[1], SCR4[:, 2], SCR4[:, 3], ALU.add))

            def moe(layer, ph):
                ve.memset(CNT[:, 0, :], 0.0)
                ve.memset(LG, 0.0)
                ch(ve.memset(GL8, -BIG))
                dve.wait_ge(S("logits"), layer + 1)
                ps = PSUM[:, LOGIT_BANK[layer], 0:NT * 36].rearrange("p (t n) -> p t n", t=NT)
                ve.tensor_tensor(LG[:, 0:4, :], ps[:, 0:4, :], bc(BR.unsqueeze(1), [P, 4, 36]), ALU.add)
                ch(ve.tensor_tensor(LG[0:64, 4, :], ps[0:64, 4, :], BR[0:64, :], ALU.add))
                ch(ve.tensor_copy(GL8[:, :, 0:4], LG[:, :, 0:4]))
                for t in range(NT):
                    ins = ve.max(GM8[:, t, :], GL8[:, t, :])
                ch(ins)
                for t in range(NT):
                    ins = ve.max_index(GI8[:, t, :], GM8[:, t, :], GL8[:, t, :])
                ch(ins)
                ve.tensor_tensor(GE, LG[:, :, 0:4], bc(GM8[:, :, 0:1], [P, NT, 4]), ALU.subtract).then_inc(S("group_shifted"), 1)
                ch(ve.tensor_copy(GIF, GI8[:, :, 0]))
                ch(ve.tensor_tensor(GOH, bc(IOTA[:, 0:4].unsqueeze(1), [P, NT, 4]), bc(GIF.unsqueeze(2), [P, NT, 4]), ALU.is_equal))
                em4 = EM.rearrange("p t (g e) -> p t g e", g=NG)
                lge = LG[:, :, 4:36].rearrange("p t (g e) -> p t g e", g=NG)
                ch(ve.tensor_tensor(em4, lge, bc(GOH.unsqueeze(3), [P, NT, NG, EPG]), ALU.mult))
                ch(ve.tensor_scalar(GOH, GOH, BIG, -BIG, ALU.mult, ALU.add))
                ch(ve.tensor_tensor(em4, em4, bc(GOH.unsqueeze(3), [P, NT, NG, EPG]), ALU.add))
                for t in range(NT):
                    ins = ve.max(EV8[:, t, :], EM[:, t, :])
                ch(ins)
                for t in range(NT):
                    ins = ve.max_index(EI8[:, t, :], EV8[:, t, :], EM[:, t, :])
                ch(ins)
                ve.tensor_tensor(EX, EV8[:, :, 1], EV8[:, :, 0], ALU.subtract).then_inc(S("expert_shifted"), 1)
                ch(ve.tensor_copy(EIF, EI8[:, :, 0:2]))
                ch(ve.tensor_tensor(EOH, bc(IOTA[:, 0:32].unsqueeze(1).unsqueeze(1), [P, NT, 2, 32]),
                                    bc(EIF.unsqueeze(3), [P, NT, 2, 32]), ALU.is_equal))
                ch(ve.memset(EOH[64:P, 4, :, :], 0.0))
                ve.tensor_tensor(MM, EOH[:, :, 0, :], EOH[:, :, 1, :], ALU.add).then_inc(S("chosen"), 1)
                dve.wait_ge(S("group_exp"), layer + 1)
                ch(ve.tensor_reduce(GV, GE, AX.X, ALU.add))
                dve.wait_ge(S("expert_exp"), layer + 1)
                ch(ve.tensor_scalar(CW[:, :, 1], EX, 1.0, None, ALU.add))
                ch(ve.tensor_tensor(CW[:, :, 1], CW[:, :, 1], GV, ALU.mult))
                ch(ve.reciprocal(CW[:, :, 0], CW[:, :, 1]))
                ch(ve.tensor_tensor(CW[:, :, 1], CW[:, :, 0], EX, ALU.mult))
                dve.wait_ge(S("ranks"), layer + 1)
                ps = PSUM[:, 5, 0:2 * NT * 32].rearrange("p (a t n) -> p a t n", a=2, t=NT)
                for t in range(NT):
                    ch(ve.tensor_tensor(CNT[:, t + 1, :], CNT[:, t, :], ps[:, 1, t, :], ALU.add))
                ve.tensor_tensor(RK, CNT[:, 0:NT, :], ps[:, 0], ALU.add)
                ch(ve.tensor_scalar(OVN, CNT[:, NT, :], float(CAP - 1), None, ALU.add))
                ch(ve.tensor_copy(OVNI, OVN))
                ch(ve.tensor_scalar(OVNI, OVNI, CAP.bit_length() - 1, None, ALU.logical_shift_right))
                ch(ve.tensor_copy(OVN, OVNI))
                ch(ve.tensor_scalar(OVN, OVN, -1.0, None, ALU.add))
                ch(ve.tensor_scalar(OVN, OVN, 0.0, None, ALU.max))
                ch(ve.memset(OVM, 1.0))
                ch(ve.tensor_tensor_scan(OVI, OVM, OVN, 0.0, ALU.mult, ALU.add))
                ch(ve.tensor_tensor(OVE, OVI, OVN, ALU.subtract))
                rk4 = bc(RK[:, 0:NT, :].unsqueeze(2), [P, NT, 2, 32])
                ch(ve.tensor_tensor(ET, EOH, rk4, ALU.mult))
                ch(ve.tensor_reduce(RR, ET, AX.X, ALU.add))
                ch(ve.tensor_tensor(ET, EOH, bc(OVE.unsqueeze(1).unsqueeze(1), [P, NT, 2, 32]), ALU.mult))
                ch(ve.tensor_reduce(OB, ET, AX.X, ALU.add))
                ch(ve.tensor_scalar(SL, EIF, float(CAP), None, ALU.mult))
                ch(ve.tensor_scalar(OB, OB, float(CAP), float(NE * CAP - CAP), ALU.mult, ALU.add))
                ch(ve.tensor_tensor(OB, OB, SL, ALU.subtract))
                ch(ve.tensor_scalar(SMOD, RR, float(CAP), None, ALU.is_ge))
                ch(ve.tensor_tensor(OB, OB, SMOD, ALU.mult))
                ch(ve.tensor_tensor(SL, SL, RR, ALU.add))
                ch(ve.tensor_tensor(SL, SL, OB, ALU.add))
                ch(ve.tensor_copy(SLI, SL))
                ve.tensor_scalar(SMI, SLI, P - 1, None, ALU.bitwise_and)
                ch(ve.tensor_scalar(SDI, SLI, P.bit_length() - 1, None, ALU.logical_shift_right))
                ve.tensor_copy(SMOD, SMI)
                ch(ve.tensor_copy(SDIV, SDI))
                ve.tensor_tensor(R1, bc(IOTA[:, 0:P].unsqueeze(1).unsqueeze(1), [P, NT, 2, P]),
                                 bc(SMOD.unsqueeze(3), [P, NT, 2, P]), ALU.is_equal)
                ch(ve.tensor_tensor(P1, bc(IOTA[:, 0:NPAIR].unsqueeze(1).unsqueeze(1), [P, NT, 2, NPAIR]),
                                    bc(SDIV.unsqueeze(3), [P, NT, 2, NPAIR]), ALU.is_equal))
                ve.tensor_tensor(P1, P1, bc(TOKID[:, :].unsqueeze(2).unsqueeze(2), [P, NT, 2, NPAIR]), ALU.mult
                                 ).then_inc(S("onehots"), 1)
                ch(ve.tensor_tensor(EIDT[0:1], bc(OVI[0:1, :].unsqueeze(1), [1, 2 * OVP, 32]),
                                    bc(IOTA[0:1, 0:2 * OVP].unsqueeze(2), [1, 2 * OVP, 32]), ALU.is_le))
                ch(ve.tensor_reduce(EIDF[0:1, :], EIDT[0:1], AX.X, ALU.add))
                ch(ve.tensor_scalar(EIDF[0:1, :], EIDF[0:1, :], float(NE - 1), None, ALU.min))
                ch(ve.tensor_copy(OVR[0:1, layer, 1:1 + 2 * OVP], EIDF[0:1, :]))
                ch(ve.tensor_scalar(NPF[0:1, 0:1], OVI[0:1, 31:32], 1.0, None, ALU.add))
                ch(ve.tensor_copy(OVR[0:1, layer, 0:1], NPF[0:1, 0:1]))
                ch(ve.tensor_scalar(OVR[0:1, layer, 0:1], OVR[0:1, layer, 0:1], 1, None, ALU.logical_shift_right))
                dve.wait_ge(S("token_lists"), layer + 1)
                ch(ve.tensor_copy(IDX, PSUM[:, 6, 0:NPAIR]))
                dve.sem_inc(S("routed"), 1)
                with dve.Fori(0, ROUNDS) as it:
                    for b in range(2):
                        done = it + ROUNDS * layer
                        dve.wait_ge(S(f"silu_ready{b}"), done + 1)
                        ve.tensor_tensor(HTM[:, b, :], SG[:, b, :], PSUM[:, 2 + b, FF:2 * FF], ALU.mult
                                         ).then_inc(S(f"hidden_ready{b}"), 1)
                        dve.wait_ge(S(f"hidden_transposed{b}"), done + 1)
                        ve.tensor_copy(HID[:, b, :, :].rearrange("p m t -> p (m t)"), PSUM[:, 2 + b, 256:256 + P]
                                       ).then_inc(S(f"hid_ready{b}"), 1)
                        dve.wait_ge(S(f"expert_out{b}"), done + 1)
                        dve.wait_ge(S(f"y_stored{b}"), it * 16 + 16 * (ROUNDS * layer + 1))
                        ve.tensor_copy(YB[:, b, 0:512], PSUM[:, 4 + 2 * b, :]).then_inc(S(f"yb_dve{b}"), 1)
                n = dve.value_load(OVR[0:1, layer, 0:1], min_val=0, max_val=OVP)
                before = dve.value_load(OVR[0:1, 0, 0:1], min_val=0, max_val=OVP) if layer else 0
                with dve.If(n > 0):
                    with dve.Fori(0, OVP) as j:
                        with dve.If(j < n):
                            dve.wait_ge(S("ov_silu"), before + (j + 1))
                            ve.tensor_tensor(HTM[:, 0, :], SG[:, 0, :], PSUM[:, 2, FF:2 * FF], ALU.mult
                                             ).then_inc(S("ov_htm"), 1)
                            dve.wait_ge(S("ov_ht"), before + (j + 1))
                            ve.tensor_copy(HID[:, 0, :, :].rearrange("p m t -> p (m t)"), PSUM[:, 2, 256:256 + P]
                                           ).then_inc(S("ov_hid"), 1)
                if layer == 0:
                    parameters()
                for t in range(NT):
                    r = ROWS[t]
                    dve.wait_ge(S(f"yg_full{t % 4}"), 32 * (layer * (2 if t % 4 == 0 else 1) + t // 4 + 1))
                    for k in range(2):
                        ve.scalar_tensor_tensor(out=X[0:r, t, :], in0=YG[t % 4][0:r, k, :], scalar=CW[0:r, t, k:k + 1],
                                                in1=X[0:r, t, :], op0=ALU.mult, op1=ALU.add).then_inc(S("yg_used"), 1)
                        dve.wait_ge(S("yg_used"), (layer * NT + t) * 2 + k + 1)
                    dve.sem_inc(S("x_updated"), 1)
                    if t:
                        norm_dve(dve, ch, 2 + 2 * layer, t - 1)
                norm_dve(dve, ch, 2 + 2 * layer, NT - 1)
                end_phase(dve, ph)

            moe(0, 4)
            def w_block(k):
                g0 = BP * k
                pw = [PWR[:, r, :, g0:g0 + BP].rearrange("p k g -> p g k").unsqueeze(3) for r in range(2)]
                pw = [bc(v, [P, BP, L, CH]) for v in pw]
                bv = [bc(BB[:, r, g0:g0 + BP, :].unsqueeze(2), [P, BP, L, CH]) for r in range(2)]
                t1 = TMPW[:, 0:BP * P].rearrange("p (g s c) -> p g s c", g=BP, s=L)
                t2 = TMPX[:, 0:BP * P].rearrange("p (g s c) -> p g s c", g=BP, s=L)
                o = [WSB[:, k % 2, r].rearrange("p g (s c) -> p g s c", s=L) for r in range(2)]
                if k >= 2:
                    dve.wait_ge(S("w_transposed"), k - 1)
                cmul(o, pw, bv, t1, t2)
                dve.sem_inc(S("w_ready"), 1)

            w_block(0)
            w_block(1)
            ch(ve.memset(H[:, :, :, 0], 0.0))
            ch(ve.tensor_tensor(EYE, PMOD[0:CH, 1:2].to_broadcast([CH, CH]), IOTA[0:CH, 0:CH], ALU.is_equal))
            ch(ve.tensor_tensor(DD[0], bc(EYE.unsqueeze(1).unsqueeze(1), [CH, 2, GP, CH]),
                                bc(DCOL.unsqueeze(3), [CH, 2, GP, CH]), ALU.mult))
            ch(ve.tensor_copy(DD[1], DD[0]))
            dve.wait_ge(S("c_ready"), 4)
            ch(ve.tensor_scalar(CT[:, 1, :, :], CT[:, 1, :, :], -1.0, None, ALU.mult))
            end_phase(dve, 5)

            def two_chunks(k):
                dve.wait_ge(S("g_ready"), k + 1)
                gs = slice(BP * k, BP * k + BP)
                t = TMPW.rearrange("p (x g j) -> p x g j", x=2, g=BP)[:, :, :, 0:PCH // 2]
                for a_ in range(2):
                    tt = TMPX.rearrange("p (a g j) -> p a g j", a=2, g=BP)[:, a_, :, 0:PCH // 2]
                    ch(ve.tensor_tensor(t, bc(CC[:, a_, :, gs].unsqueeze(3), [P, 2, BP, PCH // 2]),
                                        G[:, :, gs, 0:PCH:2], ALU.mult))
                    ch(ve.tensor_tensor(tt, t[:, 0], t[:, 1], ALU.add))
                odd = G[:, :, gs, 1:PCH:2]
                ch(ve.tensor_tensor(odd, odd, TMPX.rearrange("p (a g j) -> p a g j", a=2, g=BP)[:, :, :, 0:PCH // 2], ALU.add))

            for k in range(2, NB):
                w_block(k)
                two_chunks(k - 2)
            two_chunks(NB - 2)
            two_chunks(NB - 1)
            dve.wait_ge(S("state_ready"), 2)
            for c in range(0, PCH, 2):
                out = HF if c == PCH - 2 else H[:, :, :, c + 2]
                ch(ve.tensor_tensor(PR, CC2, bc(H[:, :, :, c].unsqueeze(1), [P, 2, 2, GP]), ALU.mult))
                ch(ve.tensor_tensor(QQ, PR[:, :, 0, :], PR[:, :, 1, :], ALU.add))
                ch(ve.tensor_tensor(out, QQ, G[:, :, :, c + 1], ALU.add))
            half = [P, 2, GP, PCH // 2]
            t = WSB.rearrange("p b r g n -> p (b r g n)").rearrange("p (x g j) -> p x g j", x=2, g=GP)
            sum_ = WT.rearrange("p r g n -> p (r g n)").rearrange("p (g j) -> p g j", g=GP)
            dve.wait_ge(S("w_transposed"), NB)
            for a_ in range(2):
                ch(ve.tensor_tensor(t, bc(CC[:, a_, :, :].unsqueeze(3), half), H[:, :, :, 0:PCH:2], ALU.mult))
                ch(ve.tensor_tensor(sum_, t[:, 0], t[:, 1], ALU.add))
                ch(ve.tensor_tensor(H[:, a_, :, 1:PCH:2], sum_, G[:, a_, :, 0:PCH:2], ALU.add))
            for a_ in range(2):
                hs = [H[:, r, :, PCH:NCH] for r in range(2)]
                t1 = TMPW[:, 0:GP * NSEQ].rearrange("p (g s) -> p g s", g=GP)
                t2 = TMPX[:, 0:GP * NSEQ].rearrange("p (g s) -> p g s", g=GP)
                ve.tensor_tensor(t1, bc(CC[:, a_, 0, :].unsqueeze(2), [P, GP, NSEQ]), hs[0], ALU.mult)
                ch(ve.tensor_tensor(t2, bc(CC[:, a_, 1, :].unsqueeze(2), [P, GP, NSEQ]), hs[1], ALU.mult))
                ch(ve.tensor_tensor(t1, t1, t2, ALU.add))
                ch(ve.tensor_tensor(HO[:, a_], t1, G[:, a_, :, PCH:NCH], ALU.add))
            dve.sem_inc(S("scanned"), 1)
            end_phase(dve, 6)

            def decayed_c(k):
                g0 = BP * k
                tmp = TMPV.rearrange("p (w g s c) -> p w g s c", w=2, g=BP, s=9)
                if k >= 3:
                    dve.wait_ge(S("y_ssm"), k - 2)
                for w in range(2):
                    for out, pw, cv in ((VV[:, k % 3], A1S, B1S), (None, A2S, B2S)):
                        o = tmp[:, w] if out is None else out[:, w].rearrange("p g (s c) -> p g s c", s=9)
                        ins = ve.tensor_tensor(
                            o, bc(pw[:, w, :, g0:g0 + BP].rearrange("p k g -> p g k").unsqueeze(3), [P, BP, 9, CH]),
                            bc(cv[:, w, g0:g0 + BP, :].unsqueeze(2), [P, BP, 9, CH]), ALU.mult)
                ch(ins)
                vv = VV[:, k % 3].rearrange("p w g n -> p (w g n)")
                ch(ve.tensor_tensor(vv, vv, TMPV, ALU.add))
                dve.sem_inc(S("v_ready"), 1)

            def taps_out(k):
                g0 = BP * k
                dve.wait_ge(S("taps"), k + 1)
                if k >= 2:
                    toeplitz_wait(dve, k - 2)
                for g in range(BP):
                    ins = ve.tensor_copy(KP[k % 2][:, :, g, 112:240], PSUM[32 * g:32 * g + CH, 2 + 4 * (k % 2), 0:2 * P
                                                                           ].rearrange("p (w n) -> p w n", w=2))
                ch(ins)
                v = KP[k % 2][:, :, :, 112:128]
                ch(ve.tensor_tensor(v, v, DD[k % 2][:, :, g0:g0 + BP, :], ALU.add))
                dve.sem_inc(S("taps_ready"), 1)

            dve.wait_ge(S("stacked"), 1)
            decayed_c(0)
            for b in range(2):
                ins = ve.memset(KP[b][:, :, :, 0:112], 0.0)
            ch(ins)
            taps_out(0)
            decayed_c(1)
            taps_out(1)
            decayed_c(2)
            for k in range(2, NB):
                taps_out(k)
                if k + 1 < NB:
                    decayed_c(k + 1)
            end_phase(dve, 7)
            for n in range(2):
                for t in range(NT):
                    i = n * NT + t
                    r = ROWS[t]
                    dve.wait_ge(S("glu_gate"), i + 1)
                    dve.wait_ge(S("glu_added"), i)
                    ch(ve.tensor_tensor(GL_T[0:r, :], PSUM[0:r, 2 * (i % 2), :], GL_SG[0:r, i % 2, :], ALU.mult))
                    xv = X[0:r, t, n * 512:(n + 1) * 512]
                    ve.tensor_tensor(xv, xv, GL_T[0:r, :], ALU.add).then_inc(S("glu_added"), 1)
                    if n:
                        dve.wait_ge(S("glu_added"), i + 1)
                        dve.sem_inc(S("x_updated"), 1)
                        norm_dve(dve, ch, 3, t)
            end_phase(dve, 8)
            moe(1, 9)

        @block.tensor
        def _(pe):
            te = nc.tensor

            def ring_wait(q):
                pe.wait_ge(S(f"ring_full{q % RS}"), full(q))

            for b in range(2):
                pe.sem_inc(S(f"xg_transposed{b}"), 1)
                pe.sem_inc(S(f"gate_up{b}"), 1)
            for t in range(NT):
                xt_pe(pe, 0, t)
            pe.wait_ge(S("consts_ready"), 1)
            for t in range(NT):
                r = ROWS[t]
                b0 = 3 * (t % 2)
                pe.wait_ge(S("xt_ready"), NT)
                if t >= 2:
                    pe.wait_ge(S("qkv_read"), t - 1)
                parts = [(0, r, 512 * n, 512) for n in range(3)] if t < 4 else [
                    (0, 64, 0, 512), (64, P, 512, 512), (0, 64, 1024, 256), (64, P, 1280, 256)]
                for pair in ([[p] for p in parts] if t < 4 else [parts[0:2], parts[2:4]]):
                    for c in range(KC):
                        if t == 0 and pair[0][2] == 0 and c % 2 == 0:
                            ring_wait(c // 2)
                        for lo, hi, col, n in pair:
                            last = te.matmul(PSUM[lo:hi, b0 + col // 512, col % 512:col % 512 + n],
                                             XT[:, c, t * P:t * P + r],
                                             RING[:, c // 2, (c % 2) * QKV + col:(c % 2) * QKV + col + n],
                                             start=(c == 0), stop=(c == KC - 1))
                last.then_inc(S("qkv_done"), 1)
                if t == NT - 1:
                    pe.wait_ge(S("qkv_done"), NT)
                    pe.sem_inc(S("ring_free"), 4)
                for tt in ([t - 1] if t else []) + ([t] if t == NT - 1 else []):
                    rr = ROWS[tt]
                    pe.wait_ge(S("rotated"), tt + 1)
                    if tt:
                        pe.wait_ge(S("kt_ready"), tt)
                    if tt < 4:
                        for c in range(KC):
                            last = te.transpose(PSUM[:, 6 + c // 4, (c % 4) * P:(c % 4 + 1) * P],
                                                QO[:, tt % 2, c * P:(c + 1) * P], IDENT[:, :])
                        last.then_inc(S("qk_transposed"), 1)
                        pe.wait_ge(S("qt_ready"), tt + 1)
                        for h in range(KVH):
                            last = te.transpose(PSUM[:, 6, h * P:(h + 1) * P], KD[:, tt % 2, h * P:(h + 1) * P], IDENT[:, :])
                        last.then_inc(S("k_transposed"), 1)
                    else:
                        for h in range(NH):
                            last = te.transpose(PSUM[0:64, 6 + h // 8, (h % 8) * 64:(h % 8 + 1) * 64],
                                                QO[0:64, tt % 2, h * 64:(h + 1) * 64], IDENT[0:64, 0:64])
                        last.then_inc(S("qk_transposed"), 1)
                        pe.wait_ge(S("qt_ready"), tt + 1)
                        for h in range(KVH):
                            last = te.transpose(PSUM[0:64, 6, h * 64:(h + 1) * 64],
                                                KD[0:64, tt % 2, h * P:h * P + 64], IDENT[0:64, 0:64])
                        last.then_inc(S("k_transposed"), 1)
            end_phase(pe, 1)
            def scores(i):
                kind, b, h = UNITS[i]
                if i >= 2:
                    pe.wait_ge(S("scores_masked"), i - 1)
                b0 = 2 * (i % 2)
                if kind == "p":
                    w = width(UNITS[i])
                    k0 = (b - 1) * P if b else 0
                    for par in range(2):
                        for g in range(2):
                            c = (4 * h + 2 * g + par) // 2
                            last = te.matmul(PSUM[:, b0 + par, g * 256:g * 256 + w],
                                             QT[par * 64:par * 64 + 64, c, b * P:(b + 1) * P],
                                             KT[par * 64:par * 64 + 64, h, k0:k0 + w], start=True, stop=True)
                else:
                    for j in range(4):
                        sq = 4 * b + j
                        for hh in range(KVH):
                            lhs = QTS[:, sq, 32 * hh:32 * hh + 32]
                            out = PSUM[32 * hh:32 * hh + 32, b0 + j // 2, :]
                            o0 = (j % 2) * 256
                            te.matmul(out[:, o0:o0 + P], lhs, KCT[:, sq, hh, :], start=True, stop=True)
                            last = te.matmul(out[:, o0 + P:o0 + 192], lhs, KTS[:, hh, :], start=True, stop=True)
                last.then_inc(S("scores"), 1)

            def p_transpose(i):
                kind, b, h = UNITS[i]
                pe.wait_ge(S("probs"), i + 1)
                if i:
                    pe.wait_ge(S("pt_ready_dve"), i)
                    pe.wait_ge(S("pt_ready_act"), i)
                w = width(UNITS[i])
                sc = scores_sb(i, w)
                for g in range(4):
                    for hf in range((w + P - 1) // P):
                        n = min(P, w - hf * P)
                        last = te.transpose(PSUM[0:n, 4 + g // 2, ((g % 2) * 2 + hf) * P:((g % 2) * 2 + hf + 1) * P],
                                            sc[:, g, hf * P:hf * P + n], IDENT[:, :])
                last.then_inc(S("p_transposed"), 1)

            def pv(i):
                kind, b, h = UNITS[i]
                pe.wait_ge(S("pt_ready_dve"), i + 1)
                pe.wait_ge(S("pt_ready_act"), i + 1)
                if i >= 2:
                    pe.wait_ge(S("o_scaled"), i - 1)
                pt = PT[:, i % 2, :].rearrange("p (g h q) -> p g h q", g=4, h=2)
                for g in range(4):
                    out = PSUM[:, 6 + i % 2, g * 64:(g + 1) * 64]
                    if kind == "p":
                        if b:
                            te.matmul(out, pt[:, g, 0, :], V[:, b - 1, h * 64:(h + 1) * 64], start=True, stop=False)
                            last = te.matmul(out, pt[:, g, 1, :], V[:, b, h * 64:(h + 1) * 64], start=False, stop=True)
                        else:
                            last = te.matmul(out, pt[:, g, 0, :], V[:, b, h * 64:(h + 1) * 64], start=True, stop=True)
                    else:
                        sq = 4 * b + g
                        for hh in range(KVH):
                            o = PSUM[32 * hh:32 * hh + 32, 6 + i % 2, g * 64:(g + 1) * 64]
                            te.matmul(o, pt[:, g, 0, 32 * hh:32 * hh + 32], VC[:, sq, hh * 64:(hh + 1) * 64],
                                      start=True, stop=False)
                            last = te.matmul(o, pt[0:64, g, 1, 32 * hh:32 * hh + 32], V[0:64, 4, hh * 64:(hh + 1) * 64],
                                             start=False, stop=True)
                last.then_inc(S("pv_done"), 1)
                if kind == "s":
                    pe.wait_ge(S("o_scaled"), i + 1)
                    pe.wait_ge(S("scores_masked"), NU - 1)
                    for j in range(4):
                        last = te.transpose(PSUM[:, b, j * P:(j + 1) * P],
                                            OD[:, j, :], IDENT[:, :])
                    last.then_inc(S("od_transposed"), 1)

            scores(0)
            pe.wait_ge(S("ck_in"), 16)
            for i in range(NSEQ):
                if i >= 2:
                    pe.wait_ge(S("kct_ready"), i - 1)
                for h in range(KVH):
                    last = te.transpose(PSUM[0:64, 4 + i % 2, h * P:(h + 1) * P], CK[:, i, h * 64:(h + 1) * 64], IDENT[:, :])
                last.then_inc(S("ck_transposed"), 1)
            pe.wait_ge(S("kct_ready"), NSEQ)
            pe.wait_ge(S("vc_in"), 16)
            for i in range(NU):
                if i + 1 < NU:
                    scores(i + 1)
                p_transpose(i)
                if i:
                    pv(i - 1)
            pv(NU - 1)
            end_phase(pe, 2)
            pe.wait_ge(S("ots_ready"), 2)
            for t in range(4):
                if t >= 2:
                    pe.wait_ge(S("ot_ready"), t - 1)
                for c in range(KC):
                    last = te.transpose(PSUM[:, 2 * (t % 2) + c // 4, (c % 4) * P:(c % 4 + 1) * P],
                                        O[:, t, c * P:(c + 1) * P], IDENT[:, :])
                last.then_inc(S("o_transposed"), 1)
            for t in range(NT):
                r = ROWS[t]
                if t < 4:
                    pe.wait_ge(S("ot_ready"), t + 1)
                else:
                    pe.wait_ge(S("ots_ready"), 2)
                if t >= 2:
                    pe.wait_ge(S("x_updated"), t - 1)
                for pair in ([[0], [1]] if t < 4 else [[0, 1]]):
                    for c in range(KC):
                        q = Q_WO + c // 3
                        if t == 0 and pair[0] == 0 and c % 3 == 0:
                            ring_wait(q)
                        for n in pair:
                            p0 = 64 * n if t == 4 else 0
                            last = te.matmul(PSUM[p0:p0 + r, 4 + 2 * (t % 2) + n, :], OT[:, c, t * P:t * P + r],
                                             RING[:, q % RS, (c % 3) * D + n * 512:(c % 3) * D + (n + 1) * 512],
                                             start=(c == 0), stop=(c == KC - 1))
                last.then_inc(S("wo_done"), 1)
                if t == 1:
                    pe.wait_ge(S("ot_ready"), 4)
                if t >= 1:
                    xt_pe(pe, 1, t - 1)
                if t >= 2:
                    logits_pe(pe, 0, t - 2)
            pe.wait_ge(S("wo_done"), NT)
            pe.sem_inc(S("ring_free"), 3)
            logits_pe(pe, 0, NT - 2)
            xt_pe(pe, 1, NT - 1)
            logits_pe(pe, 0, NT - 1)
            end_phase(pe, 3)

            def moe(layer, ph):
                pe.wait_ge(S("chosen"), layer + 1)
                mm = MM.rearrange("p t n -> p (t n)")
                te.matmul(PSUM[:, 5, 0:NT * 32], UPPER[:, :], mm, start=True, stop=True)
                last = te.matmul(PSUM[:, 5, NT * 32:2 * NT * 32], ONES[:, :], mm, start=True, stop=True)
                last.then_inc(S("ranks"), 1)
                pe.wait_ge(S("onehots"), layer + 1)
                for i in range(2 * NT):
                    last = te.matmul(PSUM[:, 6, 0:NPAIR], R1[:, i // 2, i % 2, :], P1[:, i // 2, i % 2, :],
                                     start=(i == 0), stop=(i == 2 * NT - 1))
                last.then_inc(S("token_lists"), 1)
                pe.wait_ge(S("routed"), layer + 1)
                q0 = Q_M[layer]

                def gather_transposed(it, b):
                    pe.wait_ge(S(f"xg_full{b}"), it * 16 + 16 * (ROUNDS * layer + 1))
                    xg = XG[:, b, :].rearrange("t (p c) -> t c p", c=KC)
                    for c in range(KC):
                        last = te.transpose(PSUM[:, c // 4, (c % 4) * P:(c % 4 + 1) * P], xg[:, c, :], IDENT[:, :])
                    last.then_inc(S(f"xg_transposed{b}"), 1)

                def pair(it, b, last_pair=False):
                    done = it + ROUNDS * layer
                    pe.wait_ge(S(f"xgt_ready{b}"), done + 2)
                    for m in range(2):
                        pe.wait_ge(S(f"ring_full{(q0 + 2 * b + m) % RS}"), it * 48 + full(q0 + 2 * b + m))
                    for c in range(KC):
                        for m in range(2):
                            gu = RING[:, (q0 + 2 * b + m) % RS, 0:2 * D].rearrange("p (w c f) -> p w c f", w=2, c=KC)
                            last = te.matmul(PSUM[m * 64:(m + 1) * 64, 2 + b, 0:2 * FF],
                                             XGT[:, b, c, m * 64:(m + 1) * 64], gu[:, :, c, :],
                                             start=(c == 0), stop=(c == KC - 1))
                    last.then_inc(S(f"gate_up{b}"), 1)
                    if not last_pair:
                        gather_transposed(it + b, 1 - b)
                    pe.wait_ge(S(f"hidden_ready{b}"), done + 1)
                    te.transpose(PSUM[:, 2 + b, 256:256 + P], HTM[:, b, :], IDENT[:, :]
                                 ).then_inc(S(f"hidden_transposed{b}"), 1)
                    pe.wait_ge(S(f"hid_ready{b}"), done + 1)
                    pe.wait_ge(S(f"yb_dve{b}"), done + 1)
                    pe.wait_ge(S(f"yb_act{b}"), done + 1)
                    for n in range(2):
                        for m in range(2):
                            slot = (q0 + 2 * b + m) % RS
                            last = te.matmul(PSUM[m * 64:(m + 1) * 64, 4 + 2 * b + n, :], HID[:, b, m, :],
                                             RING[:, slot, 2 * D + n * 512:2 * D + (n + 1) * 512], start=True, stop=True)
                    last.then_inc(S(f"expert_out{b}"), 1)
                    pe.wait_ge(S(f"expert_out{b}"), done + 1)
                    pe.sem_inc(S("ring_free"), 2)

                gather_transposed(0, 0)
                with pe.Fori(0, ROUNDS - 1) as it:
                    for b in range(2):
                        pair(it, b)
                pair(ROUNDS - 1, 0)
                pair(ROUNDS - 1, 1, last_pair=True)
                n = pe.value_load(OVR[0:1, layer, 0:1], min_val=0, max_val=OVP)
                before = pe.value_load(OVR[0:1, 0, 0:1], min_val=0, max_val=OVP) if layer else 0
                pe.sem_inc(S("ov_wfree"), 1)
                with pe.If(n > 0):
                    with pe.Fori(0, OVP) as j:
                        with pe.If(j < n):
                            pe.wait_ge(S("ov_x"), (before + j) * 16 + 16)
                            for c in range(KC):
                                last = te.transpose(PSUM[:, c // 4, (c % 4) * P:(c % 4 + 1) * P], XG[:, 0, :].rearrange("t (p c) -> t c p", c=KC)[:, c, :],
                                                    IDENT[:, :])
                            last.then_inc(S("ov_xt"), 1)
                            pe.wait_ge(S("ov_xgt"), before + (j + 1))
                            pe.wait_ge(S("ov_w"), (before + j) * 96 + 96)
                            areas = (XN.rearrange("p t d -> p (t d)"), XT.rearrange("p c t -> p (c t)"))
                            for c in range(KC):
                                for m in range(2):
                                    gu = areas[m][:, 0:2 * D].rearrange("p (w c f) -> p w c f", w=2, c=KC)
                                    last = te.matmul(PSUM[m * 64:(m + 1) * 64, 2, 0:2 * FF], XGT[:, 0, c, m * 64:(m + 1) * 64],
                                                     gu[:, :, c, :], start=(c == 0), stop=(c == KC - 1))
                            last.then_inc(S("ov_gu"), 1)
                            pe.wait_ge(S("ov_htm"), before + (j + 1))
                            te.transpose(PSUM[:, 2, 256:256 + P], HTM[:, 0, :], IDENT[:, :]).then_inc(S("ov_ht"), 1)
                            pe.wait_ge(S("ov_hid"), before + (j + 1))
                            for n_ in range(2):
                                for m in range(2):
                                    last = te.matmul(PSUM[m * 64:(m + 1) * 64, 4 + n_, :], HID[:, 0, m, :],
                                                     areas[m][:, 2 * D + n_ * 512:2 * D + (n_ + 1) * 512], start=True, stop=True)
                            last.then_inc(S("ov_dn"), 1)
                if layer == 0:
                    pe.wait_ge(S("par_done"), 1)
                    for k in range(4):
                        last = te.transpose(PSUM[:, 0, 32 * k:32 * k + 32], NAT[:, 12 + k, :], IDENT[0:32, 0:32])
                    for w in range(2):
                        last = te.transpose(PSUM[0:CH, 1, 32 * w:32 * w + 32], NAT[:, 23, CH * w:CH * w + CH], IDENT[0:32, 0:32])
                    last.then_inc(S("par_transposed"), 1)
                end_phase(pe, ph)

            moe(0, 4)
            pe.wait_ge(S("ssm_in"), 16 * 6)
            for r in range(2):
                for i in range(NSEQ):
                    last = te.transpose(PSUM[:, 1 + r, 32 * i:32 * i + 32], SIN_[:, r, i, :], IDENT[0:32, 0:32])
                last.then_inc(S("st_transposed"), 1)
            for r in range(2):
                for k in range(8):
                    last = te.transpose(PSUM[:, 3 + 2 * r + k // 4, (k % 4) * P:(k % 4 + 1) * P], CL[:, 8 * r + k, :], IDENT[:, :])
                last.then_inc(S("c_transposed"), 1)
            end_phase(pe, 5)
            for k in range(NB):
                pe.wait_ge(S("w_ready"), k + 1)
                if k:
                    pe.wait_ge(S("wt_ready"), k)
                for r in range(2):
                    for g in range(BP):
                        last = te.transpose(PSUM[:, 2 + r, g * P:(g + 1) * P], WSB[:, k % 2, r, g, :], IDENT[:, :])
                last.then_inc(S("w_transposed"), 1)
                if k:
                    pe.wait_ge(S("u_ready"), k)
                pe.wait_ge(S("u_gathered"), k + 1)
                for g in range(8):
                    last = te.transpose(PSUM[:, g // 4, (g % 4) * NCH:(g % 4 + 1) * NCH],
                                        UA[:, k % 2, g].rearrange("p s c -> p (s c)"), IDENT[0:NCH, 0:NCH])
                last.then_inc(S("u_transposed"), 1)
                pe.wait_ge(S("wt_ready"), k + 1)
                pe.wait_ge(S("u_ready"), k + 1)
                if k:
                    pe.wait_ge(S("g_ready"), k)
                for r in range(2):
                    for g in range(BP):
                        for w in range(2):
                            last = te.matmul(PSUM[64 * w:64 * w + 64, 4 + r, g * NCH:(g + 1) * NCH],
                                             WT[:, r, g, 64 * w:64 * w + 64], U[:, 2 * (BP * k + g) + w, :],
                                             start=True, stop=True)
                last.then_inc(S("g_done"), 1)
            pe.wait_ge(S("scanned"), 1)
            for r in range(2):
                last = te.transpose(PSUM[0:32, 0, r * P:(r + 1) * P], HF[:, r, :], IDENT[:, :])
            last.then_inc(S("hf_transposed"), 1)
            for r in range(2):
                for i in range(NSEQ):
                    last = te.transpose(PSUM[0:32, 2 + 2 * r + i // 4, (i % 4) * P:(i % 4 + 1) * P], HO[:, r, :, i], IDENT[:, :])
                last.then_inc(S("ho_transposed"), 1)
            end_phase(pe, 6)

            def taps(k):
                pe.wait_ge(S("v_ready"), k + 1)
                if k >= 2:
                    pe.wait_ge(S("taps_ready"), k - 1)
                for w in range(2):
                    for g in range(BP):
                        last = te.matmul(PSUM[32 * g:32 * g + CH, 2 + 4 * (k % 2), w * P:(w + 1) * P],
                                         BB[:, w, BP * k + g, :], VV[:, k % 3, w, g, 0:P], start=True, stop=True)
                last.then_inc(S("taps"), 1)

            pe.wait_ge(S("stacked"), 1)
            taps(0)
            taps(1)
            for k in range(NB):
                toeplitz_wait(pe, k)
                if k >= 2:
                    pe.wait_ge(S("z_ready"), k - 1)
                if k == 0:
                    pe.wait_ge(S("stacked"), 2)
                for g in range(BP):
                    for w in range(2):
                        pr = BP * k + g
                        out = PSUM[0:NCH, 4 * (k % 2) + w, g * P:(g + 1) * P]
                        te.matmul(out, H[:, w, pr, 0:NCH], VV[:, k % 3, w, g, CH:CH + P], start=True, stop=False)
                        last = te.matmul(out, U[:, 2 * pr + w, :], TT[:, k % 2, w, g, :], start=False, stop=True)
                last.then_inc(S("y_ssm"), 1)
                if k + 2 < NB:
                    taps(k + 2)
            pe.wait_ge(S("z_ready"), NB)
            for t in range(L):
                if t >= 2:
                    pe.wait_ge(S("zt_ready"), t - 1)
                for c in range(KC):
                    last = te.transpose(PSUM[:, 2 + 2 * (t % 2) + c // 4, (c % 4) * P:(c % 4) * P + NCH],
                                        Z[:, t, c * P:(c + 1) * P], IDENT[0:NCH, 0:NCH])
                last.then_inc(S("z_transposed"), 1)
            end_phase(pe, 7)
            for n in range(2):
                for t in range(NT):
                    i = n * NT + t
                    r = ROWS[t]
                    if i >= 2:
                        pe.wait_ge(S("glu_added"), i - 1)
                    for pair in ([[0], [1]] if t < 4 else [[0, 1]]):
                        for c in range(KC):
                            q = Q_GLU + 3 * n + c // 3
                            if t == 0 and pair[0] == 0 and c % 3 == 0:
                                ring_wait(q)
                            for w in pair:
                                p0 = 64 * w if t == 4 else 0
                                last = te.matmul(PSUM[p0:p0 + r, 2 * (i % 2) + w, :], XT[:, c, t * P:t * P + r],
                                                 RING[:, q % RS, (2 * (c % 3) + w) * 512:(2 * (c % 3) + w + 1) * 512],
                                                 start=(c == 0), stop=(c == KC - 1))
                    last.then_inc(S("glu_done"), 1)
                    if n and t >= 1:
                        xt_pe(pe, 3, t - 1)
                    if n and t >= 2:
                        logits_pe(pe, 1, t - 2)
                pe.wait_ge(S("glu_done"), NT * (n + 1))
                pe.sem_inc(S("ring_free"), 3)
            logits_pe(pe, 1, NT - 2)
            xt_pe(pe, 3, NT - 1)
            logits_pe(pe, 1, NT - 1)
            end_phase(pe, 8)
            moe(1, 9)


_INS = ["x_prompt", "x_sample", "cache_k", "cache_v", "state_ssm_re", "state_ssm_im", "norm_mix", "norm_ffn",
        "norm_final", "attn_w_qkv", "attn_b_qkv", "attn_w_o", "attn_b_o", "attn_sinks", "ssm_a_re", "ssm_a_im",
        "ssm_log_dt", "ssm_b_re", "ssm_b_im", "ssm_c_re", "ssm_c_im", "ssm_d", "ssm_w_glu_a", "ssm_w_glu_b",
        "moe_w_router_group", "moe_b_router_group", "moe_w_router_expert", "moe_b_router_expert", "moe_w_gate",
        "moe_w_up", "moe_w_down"]
_OUTS = [(1, SEQ, D), (NSEQ, DSEQ, D), (1, 1, P, KVH, HD), (1, NSEQ, P, KVH, HD), (1, 1, P, KVH, HD),
         (1, NSEQ, P, KVH, HD), (1, 1, NGR, ST), (1, NSEQ, NGR, ST), (1, 1, NGR, ST), (1, NSEQ, NGR, ST)]


def rotary_table():
    pos = np.concatenate([np.arange(SEQ), np.tile(PAST + np.arange(DSEQ), NSEQ)]).astype(np.float32)
    half = HD // 2
    inv = (1.0 / (np.float32(10000.0) ** (np.arange(half, dtype=np.float32) * np.float32(2.0 / HD)))).astype(np.float32)
    ang = (pos[:, None] * inv[None, :]).astype(np.float32)
    return np.concatenate([np.cos(ang), np.sin(ang)], axis=1).astype(np.float32)


def kernel(**inputs):
    import concourse.bacc as bacc
    from concourse.bass_utils import run_bass_kernel_spmd

    nc = bacc.Bacc("TRN2", target_bir_lowering=False, num_devices=1)
    arrays, args = {}, []
    for name in _INS:
        arr = np.ascontiguousarray(inputs[name])
        arrays[f"in_{name}"] = arr
        args.append(nc.dram_tensor(f"in_{name}", arr.shape, mybir.dt.from_np(arr.dtype), kind="ExternalInput").ap())
    tab = rotary_table()
    arrays["in_rotary"] = tab
    args.append(nc.dram_tensor("in_rotary", tab.shape, FP, kind="ExternalInput").ap())
    for i, shape in enumerate(_OUTS):
        args.append(nc.dram_tensor(f"out_{i}", shape, FP, kind="ExternalOutput").ap())
    build(nc, *args)
    r = run_bass_kernel_spmd(nc, [arrays], core_ids=[0])
    return tuple(r.results[0][f"out_{i}"] for i in range(len(_OUTS)))
```
